# Optimizing a Trainium2 kernel written in Bass

```python
import jax, jax.numpy as jnp
from jax import lax
import numpy as np
import math

D_MODEL = 1024
BATCH = 1
SEQ = 256
DEPTH = 1

CHUNK = 64
RET_HEADS = 4
RET_DK = 128
RET_DV = 256
RET_QK_WIDTH = RET_HEADS * RET_DK
RET_V_WIDTH = RET_HEADS * RET_DV
LRU_WIDTH = 1024
LRU_BLOCKS = 4
LRU_BLOCK = LRU_WIDTH // LRU_BLOCKS
LRU_CONV = 4
LRU_C = 8.0
LRU_MIN_RAD = 0.9
LRU_MAX_RAD = 0.999
D_FF = 3 * D_MODEL
FFN_CONV = 3
ROPE_BASE = 10000.0
RMS_EPS = 1e-6
GN_EPS = 1e-6

IN_SIZES = (RET_QK_WIDTH, RET_QK_WIDTH, RET_V_WIDTH, RET_V_WIDTH,
            LRU_WIDTH, LRU_WIDTH, D_MODEL, D_MODEL)
D_IN = sum(IN_SIZES)
SPLIT_POINTS = tuple(sum(IN_SIZES[:i + 1]) for i in range(len(IN_SIZES) - 1))


def rms_norm(x, w):
    x32 = x.astype(jnp.float32)
    y = x32 * lax.rsqrt(jnp.mean(x32 * x32, axis=-1, keepdims=True) + RMS_EPS)
    return (y * w.astype(jnp.float32)).astype(x.dtype)

def causal_depthwise_conv(x, w, b):
    k_width, channels = w.shape
    y = lax.conv_general_dilated(
        x, w[:, None, :].astype(x.dtype), window_strides=(1,),
        padding=[(k_width - 1, 0)], dimension_numbers=("NWC", "WIO", "NWC"),
        feature_group_count=channels)
    return y + b.astype(x.dtype)

def rotary(x, positions):
    half = x.shape[-1] // 2
    inv_freq = ROPE_BASE ** (-jnp.arange(half, dtype=jnp.float32) / half)
    ang = positions.astype(jnp.float32)[..., None] * inv_freq
    cos = jnp.cos(ang)[:, :, None, :]
    sin = jnp.sin(ang)[:, :, None, :]
    x32 = x.astype(jnp.float32)
    x1, x2 = x32[..., :half], x32[..., half:]
    return jnp.concatenate([x1 * cos - x2 * sin, x1 * sin + x2 * cos], axis=-1).astype(x.dtype)

def chunkwise_retention(q, k, v):
    bsz, seq, heads, dk = q.shape
    dv = v.shape[-1]
    n_chunks = seq // CHUNK
    log_gamma = jnp.log1p(-jnp.power(2.0, -5.0 - jnp.arange(heads, dtype=jnp.float32)))
    idx = jnp.arange(CHUNK, dtype=jnp.float32)
    dist = jnp.abs(idx[:, None] - idx[None, :])
    intra_decay = jnp.exp(log_gamma[:, None, None] * dist)
    q_decay = jnp.exp(log_gamma[:, None] * (idx + 1.0))
    k_decay = jnp.exp(log_gamma[:, None] * (CHUNK - 1.0 - idx))
    chunk_decay = jnp.exp(log_gamma * CHUNK)

    def to_chunks(t):
        return t.astype(jnp.float32).reshape(bsz, n_chunks, CHUNK, heads, -1).transpose(1, 0, 3, 2, 4)

    qc, kc, vc = to_chunks(q), to_chunks(k), to_chunks(v)

    def step(state, inp):
        qi, ki, vi = inp
        scores = jnp.einsum("bhid,bhjd->bhij", qi, ki) * intra_decay
        out = (jnp.einsum("bhij,bhjv->bhiv", scores, vi)
               + jnp.einsum("bhid,bhdv->bhiv", qi * q_decay[:, :, None], state))
        state = (state * chunk_decay[:, None, None]
                 + jnp.einsum("bhjd,bhjv->bhdv", ki * k_decay[:, :, None], vi))
        return state, out

    state0 = jnp.zeros((bsz, heads, dk, dv), jnp.float32)
    _, out = lax.scan(step, state0, (qc, kc, vc))
    return out.transpose(1, 0, 3, 2, 4).reshape(bsz, seq, heads, dv)

def head_group_norm(o, w):
    bsz, seq, heads, dv = o.shape
    mu = jnp.mean(o, axis=-1, keepdims=True)
    var = jnp.mean(jnp.square(o - mu), axis=-1, keepdims=True)
    y = (o - mu) * lax.rsqrt(var + GN_EPS)
    return y.reshape(bsz, seq, heads * dv) * w.astype(jnp.float32)

def _linear_recurrence_combine(e1, e2):
    a1, b1 = e1
    a2, b2 = e2
    return a1 * a2, a2 * b1 + b2

def rg_lru(x, w_r, b_r, w_i, b_i, lam):
    bsz, seq, width = x.shape
    x32 = x.astype(jnp.float32)
    xb = x32.reshape(bsz, seq, LRU_BLOCKS, LRU_BLOCK)
    r = jax.nn.sigmoid(jnp.einsum("bsni,nij->bsnj", xb, w_r.astype(jnp.float32))
                       + b_r.astype(jnp.float32)).reshape(bsz, seq, width)
    i = jax.nn.sigmoid(jnp.einsum("bsni,nij->bsnj", xb, w_i.astype(jnp.float32))
                       + b_i.astype(jnp.float32)).reshape(bsz, seq, width)
    log_a = -LRU_C * r * jax.nn.softplus(-lam.astype(jnp.float32))
    a = jnp.exp(log_a)
    b = jnp.sqrt(-jnp.expm1(2.0 * log_a)) * (i * x32)
    _, h = lax.associative_scan(_linear_recurrence_combine, (a, b), axis=1)
    return h

def first_inputs(seed: int = 0) -> dict:
    key = jax.random.key(seed)
    ks = jax.random.split(key, 24)

    def nrm(k, shape, scale):
        return jax.random.normal(k, shape, jnp.float32) * scale

    def gain(k, shape):
        return 1.0 + 0.02 * jax.random.normal(k, shape, jnp.float32)

    x = jax.random.normal(ks[0], (BATCH, SEQ, D_MODEL), jnp.float32)
    start = jax.random.randint(ks[1], (BATCH, 1), 0, 64) * CHUNK
    positions = (start + jnp.arange(SEQ)[None, :]).astype(jnp.int32)

    u = jax.random.uniform(ks[12], (DEPTH, LRU_WIDTH), jnp.float32,
                           LRU_MIN_RAD ** 2, LRU_MAX_RAD ** 2)
    a0 = jnp.sqrt(u)
    lru_lambda = jnp.log(a0) - jnp.log1p(-a0)

    return {
        "x": x,
        "positions": positions,
        "norm1_w": gain(ks[2], (DEPTH, D_MODEL)),
        "w_in": nrm(ks[3], (DEPTH, D_MODEL, D_IN), D_MODEL ** -0.5),
        "merge_gate_b": nrm(ks[4], (DEPTH, 2, D_MODEL), 0.02),
        "ret_gn_w": gain(ks[5], (DEPTH, RET_V_WIDTH)),
        "w_ret_o": nrm(ks[6], (DEPTH, RET_V_WIDTH, D_MODEL), RET_V_WIDTH ** -0.5),
        "lru_conv_w": nrm(ks[7], (DEPTH, LRU_CONV, LRU_WIDTH), LRU_CONV ** -0.5),
        "lru_conv_b": nrm(ks[8], (DEPTH, LRU_WIDTH), 0.02),
        "lru_w_r": nrm(ks[9], (DEPTH, LRU_BLOCKS, LRU_BLOCK, LRU_BLOCK), LRU_BLOCK ** -0.5),
        "lru_b_r": nrm(ks[10], (DEPTH, LRU_BLOCKS, LRU_BLOCK), 0.02),
        "lru_w_i": nrm(ks[11], (DEPTH, LRU_BLOCKS, LRU_BLOCK, LRU_BLOCK), LRU_BLOCK ** -0.5),
        "lru_b_i": nrm(ks[13], (DEPTH, LRU_BLOCKS, LRU_BLOCK), 0.02),
        "lru_lambda": lru_lambda,
        "w_lru_o": nrm(ks[14], (DEPTH, LRU_WIDTH, D_MODEL), LRU_WIDTH ** -0.5),
        "w_out": nrm(ks[15], (DEPTH, D_MODEL, D_MODEL), D_MODEL ** -0.5),
        "norm2_w": gain(ks[16], (DEPTH, D_MODEL)),
        "ffn_w_up": nrm(ks[17], (DEPTH, D_MODEL, 2 * D_FF), D_MODEL ** -0.5),
        "ffn_conv_w": nrm(ks[18], (DEPTH, FFN_CONV, D_FF), FFN_CONV ** -0.5),
        "ffn_conv_b": nrm(ks[19], (DEPTH, D_FF), 0.02),
        "ffn_w_down": nrm(ks[20], (DEPTH, D_FF, D_MODEL), D_FF ** -0.5),
        "norm_f_w": gain(ks[21], (D_MODEL,)),
    }

def first_block(x, positions, norm1_w, w_in, merge_gate_b, ret_gn_w, w_ret_o,
              lru_conv_w, lru_conv_b, lru_w_r, lru_b_r, lru_w_i, lru_b_i, lru_lambda,
              w_lru_o, w_out, norm2_w, ffn_w_up, ffn_conv_w, ffn_conv_b, ffn_w_down,
              norm_f_w):
    bsz, seq, _ = x.shape
    for l in range(DEPTH):
        h = rms_norm(x, norm1_w[l])
        proj = h @ w_in[l]
        q, k, v, g_ret, x_lru, y_lru, gate_ret, gate_lru = jnp.split(proj, SPLIT_POINTS, axis=-1)

        q = rotary(q.reshape(bsz, seq, RET_HEADS, RET_DK), positions)
        k = rotary(k.reshape(bsz, seq, RET_HEADS, RET_DK), positions) * (RET_DK ** -0.5)
        o = chunkwise_retention(q, k, v.reshape(bsz, seq, RET_HEADS, RET_DV))
        o = head_group_norm(o, ret_gn_w[l])
        y_a = (o * jax.nn.silu(g_ret.astype(jnp.float32))).astype(x.dtype) @ w_ret_o[l]

        xc = causal_depthwise_conv(x_lru, lru_conv_w[l], lru_conv_b[l])
        hl = rg_lru(xc, lru_w_r[l], lru_b_r[l], lru_w_i[l], lru_b_i[l], lru_lambda[l])
        y_b = (hl * jax.nn.gelu(y_lru.astype(jnp.float32))).astype(x.dtype) @ w_lru_o[l]

        mix = (jax.nn.sigmoid(gate_ret + merge_gate_b[l, 0]) * y_a
               + jax.nn.sigmoid(gate_lru + merge_gate_b[l, 1]) * y_b)
        x = x + mix @ w_out[l]

        h = rms_norm(x, norm2_w[l])
        up = h @ ffn_w_up[l]
        gate, val = jnp.split(up, [D_FF], axis=-1)
        gate = causal_depthwise_conv(gate, ffn_conv_w[l], ffn_conv_b[l])
        x = x + (jax.nn.gelu(gate) * val) @ ffn_w_down[l]
    return rms_norm(x, norm_f_w)


DEPTH_2 = 2

D_MIX = D_MODEL
GLA_HEADS = 4
GLA_DV = 64
GLA_DK = GLA_DV // 2
GLA_GATE_RANK = 16
GLA_TAU = 16.0
GLA_CHUNK = 64
CONV_CH = D_MIX // 4
CONV_WIDTH = 31
SWA_Q_HEADS = 8
SWA_KV_HEADS = 2
SWA_HEAD_DIM = 64
SWA_WINDOW = 128
SWA_BLOCK = 128
D_FF_2 = 2816
LN_EPS = 1e-5


def _in_proj_widths():
    return [
        GLA_HEADS * GLA_DK,
        GLA_HEADS * GLA_DK,
        GLA_HEADS * GLA_DV,
        GLA_HEADS * GLA_DV,
        GLA_GATE_RANK,
        CONV_CH,
        CONV_CH,
        SWA_Q_HEADS * SWA_HEAD_DIM,
        SWA_KV_HEADS * SWA_HEAD_DIM,
        SWA_KV_HEADS * SWA_HEAD_DIM,
    ]

def rmsnorm(x, g):
    x32 = x.astype(jnp.float32)
    y = x32 * lax.rsqrt(jnp.mean(x32 * x32, axis=-1, keepdims=True) + RMS_EPS)
    return (y * g.astype(jnp.float32)).astype(x.dtype)

def swiglu_ffn(h, w_gate, w_up, w_down):
    return (jax.nn.silu(h @ w_gate) * (h @ w_up)) @ w_down

def gla_group(q, k, v, glog, r, norm_g):
    B, S, H, DK = q.shape
    DV = v.shape[-1]
    C = GLA_CHUNK
    N = S // C
    f32 = jnp.float32

    def chunks(t):
        return t.astype(f32).reshape(B, N, C, H, t.shape[-1]).transpose(1, 0, 3, 2, 4)

    qc = chunks(q) * (DK ** -0.5)
    kc = chunks(k)
    vc = chunks(v)
    bc = jnp.cumsum(chunks(glog), axis=3)
    causal = jnp.tril(jnp.ones((C, C), dtype=bool))[:, :, None]

    def step(state, inp):
        qn, kn, vn, bn = inp
        diff = bn[:, :, :, None, :] - bn[:, :, None, :, :]
        decay = jnp.where(causal, jnp.exp(jnp.where(causal, diff, 0.0)), 0.0)
        attn = jnp.einsum('bhid,bhjd,bhijd->bhij', qn, kn, decay)
        o = jnp.einsum('bhij,bhjv->bhiv', attn, vn) \
            + jnp.einsum('bhid,bhdv->bhiv', qn * jnp.exp(bn), state)
        b_last = bn[:, :, -1:, :]
        state = jnp.exp(b_last[:, :, 0, :])[..., None] * state \
            + jnp.einsum('bhjd,bhjv->bhdv', kn * jnp.exp(b_last - bn), vn)
        return state, o

    s0 = jnp.zeros((B, H, DK, DV), f32)
    _, o = lax.scan(step, s0, (qc, kc, vc, bc))
    o = o.transpose(1, 0, 3, 2, 4).reshape(B, S, H, DV)
    o = o * lax.rsqrt(jnp.mean(o * o, axis=-1, keepdims=True) + RMS_EPS) * norm_g.astype(f32)
    o = o.reshape(B, S, H * DV) * jax.nn.silu(r.astype(f32))
    return o.astype(q.dtype)

def conv_group(a, g, conv_w, conv_b, ln_g, ln_b):
    u = a * jax.nn.sigmoid(g)
    y = lax.conv_general_dilated(
        u, conv_w[:, None, :].astype(u.dtype), window_strides=(1,),
        padding=[(CONV_WIDTH - 1, 0)], dimension_numbers=('NWC', 'WIO', 'NWC'),
        feature_group_count=CONV_CH) + conv_b
    y32 = y.astype(jnp.float32)
    mu = jnp.mean(y32, axis=-1, keepdims=True)
    var = jnp.mean(jnp.square(y32 - mu), axis=-1, keepdims=True)
    y32 = (y32 - mu) * lax.rsqrt(var + LN_EPS) * ln_g.astype(jnp.float32) + ln_b.astype(jnp.float32)
    return jax.nn.silu(y32).astype(a.dtype)

def swa_group(q, k, v, sinks):
    B, S, _ = q.shape
    BLK, HKV, DH = SWA_BLOCK, SWA_KV_HEADS, SWA_HEAD_DIM
    G = SWA_Q_HEADS // HKV
    nb = S // BLK
    qb = q.reshape(B, nb, BLK, HKV, G, DH)
    kb = k.reshape(B, nb, BLK, HKV, DH)
    vb = v.reshape(B, nb, BLK, HKV, DH)

    def with_prev(t):
        prev = jnp.pad(t, ((0, 0), (1, 0), (0, 0), (0, 0), (0, 0)))[:, :-1]
        return jnp.concatenate([prev, t], axis=2)

    kk, vv = with_prev(kb), with_prev(vb)
    s = jnp.einsum('bnqhgd,bnkhd->bnhgqk', qb, kk).astype(jnp.float32) * (DH ** -0.5)
    qi = jnp.arange(BLK)[:, None]
    kj = jnp.arange(2 * BLK)[None, :]
    dist = qi - kj + BLK
    blk = jnp.arange(nb)[:, None, None]
    valid = (dist >= 0) & (dist < SWA_WINDOW) & ((blk > 0) | (kj >= BLK))
    slopes = jnp.exp2(-8.0 * (jnp.arange(SWA_Q_HEADS, dtype=jnp.float32) + 1.0) / SWA_Q_HEADS)
    slopes = slopes.reshape(HKV, G)
    s = s - slopes[:, :, None, None] * dist.astype(jnp.float32)
    s = jnp.where(valid[None, :, None, None], s, -jnp.inf)
    sink = jnp.broadcast_to(sinks.astype(jnp.float32).reshape(HKV, G)[None, None, :, :, None, None],
                            s.shape[:-1] + (1,))
    p = jax.nn.softmax(jnp.concatenate([s, sink], axis=-1), axis=-1)[..., :-1]
    o = jnp.einsum('bnhgqk,bnkhd->bnqhgd', p.astype(v.dtype), vv)
    return o.reshape(B, S, SWA_Q_HEADS * DH)

def hybrid_mixer(h, w_in, gla_w_gate2, gla_b_gate, gla_norm_g, conv_w, conv_b,
                 conv_ln_g, conv_ln_b, swa_sinks, w_out):
    B, S, _ = h.shape
    p = h @ w_in
    offsets = np.cumsum(_in_proj_widths())[:-1].tolist()
    gq, gk, gv, gr, glr, ca, cg, sq, sk, sv = jnp.split(p, offsets, axis=-1)
    glog = jax.nn.log_sigmoid((glr @ gla_w_gate2 + gla_b_gate).astype(jnp.float32)) / GLA_TAU
    o_gla = gla_group(gq.reshape(B, S, GLA_HEADS, GLA_DK), gk.reshape(B, S, GLA_HEADS, GLA_DK),
                      gv.reshape(B, S, GLA_HEADS, GLA_DV), glog.reshape(B, S, GLA_HEADS, GLA_DK),
                      gr, gla_norm_g)
    o_conv = conv_group(ca, cg, conv_w, conv_b, conv_ln_g, conv_ln_b)
    o_swa = swa_group(sq, sk, sv, swa_sinks)
    return jnp.concatenate([o_gla, o_conv, o_swa], axis=-1) @ w_out

def second_inputs(seed: int = 0) -> dict:
    key = jax.random.key(seed)
    ks = jax.random.split(key, 16)
    f32 = jnp.float32
    d_in = sum(_in_proj_widths())
    nrm = lambda k, shape, scale: jax.random.normal(k, shape, f32) * scale
    return {
        "x": jax.random.normal(ks[0], (BATCH, SEQ, D_MODEL), f32),
        "norm_g": 1.0 + nrm(ks[1], (DEPTH_2, 6, D_MODEL), 0.05),
        "ffn_w_gate": nrm(ks[2], (DEPTH_2, 2, D_MODEL, D_FF_2), D_MODEL ** -0.5),
        "ffn_w_up": nrm(ks[3], (DEPTH_2, 2, D_MODEL, D_FF_2), D_MODEL ** -0.5),
        "ffn_w_down": nrm(ks[4], (DEPTH_2, 2, D_FF_2, D_MODEL), D_FF_2 ** -0.5),
        "w_in": nrm(ks[5], (DEPTH_2, D_MODEL, d_in), D_MODEL ** -0.5),
        "gla_w_gate2": nrm(ks[6], (DEPTH_2, GLA_GATE_RANK, GLA_HEADS * GLA_DK), GLA_GATE_RANK ** -0.5),
        "gla_b_gate": nrm(ks[7], (DEPTH_2, GLA_HEADS * GLA_DK), 0.1),
        "gla_norm_g": 1.0 + nrm(ks[8], (DEPTH_2, GLA_HEADS, GLA_DV), 0.05),
        "conv_w": nrm(ks[9], (DEPTH_2, CONV_WIDTH, CONV_CH), CONV_WIDTH ** -0.5),
        "conv_b": nrm(ks[10], (DEPTH_2, CONV_CH), 0.02),
        "conv_ln_g": 1.0 + nrm(ks[11], (DEPTH_2, CONV_CH), 0.05),
        "conv_ln_b": nrm(ks[12], (DEPTH_2, CONV_CH), 0.02),
        "swa_sinks": nrm(ks[13], (DEPTH_2, SWA_Q_HEADS), 0.5),
        "w_out": nrm(ks[14], (DEPTH_2, D_MIX, D_MODEL), D_MIX ** -0.5),
    }

def second_block(x, norm_g, ffn_w_gate, ffn_w_up, ffn_w_down, w_in, gla_w_gate2, gla_b_gate,
              gla_norm_g, conv_w, conv_b, conv_ln_g, conv_ln_b, swa_sinks, w_out):
    for l in range(DEPTH_2):
        g = norm_g[l]
        h = swiglu_ffn(rmsnorm(x, g[0]), ffn_w_gate[l, 0], ffn_w_up[l, 0], ffn_w_down[l, 0])
        x = x + 0.5 * rmsnorm(h, g[1])
        h = hybrid_mixer(rmsnorm(x, g[2]), w_in[l], gla_w_gate2[l], gla_b_gate[l], gla_norm_g[l],
                         conv_w[l], conv_b[l], conv_ln_g[l], conv_ln_b[l], swa_sinks[l], w_out[l])
        x = x + rmsnorm(h, g[3])
        h = swiglu_ffn(rmsnorm(x, g[4]), ffn_w_gate[l, 1], ffn_w_up[l, 1], ffn_w_down[l, 1])
        x = x + 0.5 * rmsnorm(h, g[5])
    return x


def setup_inputs(seed=0):
    out = dict(first_inputs(seed))
    for name, value in second_inputs(seed + 1).items():
        if name != "x":
            out[name + "_2"] = value
    return out


def reference(
    x, positions, norm1_w, w_in, merge_gate_b, ret_gn_w, w_ret_o, lru_conv_w, lru_conv_b,
    lru_w_r, lru_b_r, lru_w_i, lru_b_i, lru_lambda, w_lru_o, w_out, norm2_w, ffn_w_up,
    ffn_conv_w, ffn_conv_b, ffn_w_down, norm_f_w, norm_g_2, ffn_w_gate_2, ffn_w_up_2,
    ffn_w_down_2, w_in_2, gla_w_gate2_2, gla_b_gate_2, gla_norm_g_2, conv_w_2, conv_b_2,
    conv_ln_g_2, conv_ln_b_2, swa_sinks_2, w_out_2,
):
    x = first_block(
        x, positions, norm1_w, w_in, merge_gate_b, ret_gn_w, w_ret_o, lru_conv_w, lru_conv_b,
        lru_w_r, lru_b_r, lru_w_i, lru_b_i, lru_lambda, w_lru_o, w_out, norm2_w, ffn_w_up,
        ffn_conv_w, ffn_conv_b, ffn_w_down, norm_f_w,
    )
    return second_block(
        x, norm_g_2, ffn_w_gate_2, ffn_w_up_2, ffn_w_down_2, w_in_2, gla_w_gate2_2,
        gla_b_gate_2, gla_norm_g_2, conv_w_2, conv_b_2, conv_ln_g_2, conv_ln_b_2, swa_sinks_2,
        w_out_2,
    )


_drawn_inputs = setup_inputs


def setup_inputs(seed=0):
    import zlib

    import numpy as np

    out = dict(_drawn_inputs(seed))
    spreads = {}
    factors = {'merge_gate_b': 8.0,
     'ret_gn_w': 4.042,
     'lru_b_r': 52.164,
     'lru_b_i': 29.375,
     'ffn_conv_b': 2.881,
     'conv_ln_b_2': 3.617,
     'lru_conv_b': 3.187,
     'norm2_w': 2.786}
    for name, (base, spread) in spreads.items():
        noise = np.random.default_rng([zlib.crc32(name.encode()), seed]).standard_normal(out[name].shape)
        drawn = base * np.exp(spread * noise) if base else spread * noise
        out[name] = __import__('jax').numpy.asarray(drawn.astype(out[name].dtype))
    for name, factor in factors.items():
        out[name] = (out[name] * factor).astype(out[name].dtype)
    return out
```

```python
from contextlib import ExitStack

import numpy as np
import concourse.bass as bass
from concourse import mybir

F32 = mybir.dt.float32
F32R = mybir.dt.float32r
I32 = mybir.dt.int32
U8 = mybir.dt.uint8
ACT = mybir.ActivationFunctionType
ALU = mybir.AluOpType
AX = mybir.AxisListType.X

P = 128
T = 256
TT = T // P
D = 1024
KT = D // P
UC = 256
FT = UC // P
NS = 3
HEADS, DK, DV, CH = 4, 128, 256, 64
DFF1, DFF2 = 3072, 2816
NF1, NF2 = DFF1 // P, DFF2 // P
DIN2 = 2064
LAYERS = 2
SWH, SWD = 8, 64
GH, GDK, GDV = 4, 32, 64
TAPS = 31
LEV = 8
RMS_EPS = 1e-6
LN_EPS = 1e-5
SQ2PI = 0.7978845608028654
GELU_C = 0.044715
MAGIC = 12582912.0

UNITS_IN1 = 28
U1_RG = 20
U1_GATES = 22
U1_RETO = 30
U1_LRUO = 34
U1_OUT = 38
U1_UP = 42
U1_DOWN = U1_UP + NF1
U1_END = U1_DOWN + 12
UL_DOWN_A = NF2
UL_MIX = NF2 + 12
UL_WOUT = UL_MIX + 9
UL_UP_B = UL_WOUT + 4
UL_DOWN_B = UL_UP_B + NF2
UL = UL_DOWN_B + 12
G1_RG = 20
G1_GATES = 28
G1_RETO = 36
G1_LRUO = 40
G1_OUT = 44
G1_UP = 48
G1_DOWN = G1_UP + NF1
G1_END = G1_DOWN + 4
GL_DOWN_A = NF2
GL_MIX = NF2 + 4
GL_WOUT = GL_MIX + 9
GL_UP_B = GL_WOUT + 4
GL_DOWN_B = GL_UP_B + NF2
GL = GL_DOWN_B + 4
TOTAL_UNITS = U1_END + LAYERS * UL
QUERY_UNITS = [U1_END + UL * l + UL_MIX + 4 + n for l in range(LAYERS) for n in range(2)]

PSM_X, PSM_SC, PSM_O, PSM_MEAN, PSM_VAR, PSM_1 = range(6)
(PSM_LEV, PSM_GLA, PSM_CROSS, PSM_SWA, PSM_PT, PSM_PV, PSM_L) = (0, 1, 5, 6, 8, 10, 11)
PS7_VEC, PS7_SINK, PS7_N0, PS7_N1, PS7_NF, PS7_1 = range(6)
(PS7_G0, PS7_G1, PS7_G2, PS7_Z, PS7_PV, PS7_GBC, PS7_CMEAN, PS7_CVAR, PS7_G3, PS7_G4, PS7_G5, PS7_L) = range(12)
ST_N0, ST_RMEAN, ST_RVAR, ST_N1, ST_NF, ST_1 = range(6)
(ST_G0, ST_G1, ST_G2, ST_GLA, ST_CMEAN, ST_CVAR, ST_G3, ST_G4, ST_G5, ST_L) = range(10)
BANK_MIX, BANK_WOUT, BANK_UP_B = NF2 % 3, (NF2 + 9) % 3, (NF2 + 13) % 3

VCOL = 128
V1 = {"norm1": 0, "gate_b": 8, "gn": 24, "lconv_w": 32, "lconv_b": 64, "b_r": 72, "b_i": 80, "lam": 88,
      "norm2": 96, "norm_f": 104}
V1B = {"fconv_w": 0, "fconv_b": 72}
VL = {"norm": 0, "conv_w": 48, "conv_b": 110, "ln_g": 112, "ln_b": 114, "gla_g": 116}


def tables():
    t = {}
    a = np.arange(P)
    t["ident"] = np.eye(P)
    t["means"] = np.stack([np.full(P, 1 / D), np.full(P, 1 / 256)], axis=1)
    t["headsel"] = np.stack([a < 64, a >= 64], axis=1) / 64.0
    t["invf"] = np.power(np.float32(10000.0), -(a % 64).astype(np.float32) / np.float32(64))[:, None]
    t["sgn"] = np.where(a < 64, -1.0, 1.0)[:, None]
    lev = np.zeros((9, P, P))
    mask = np.zeros((LEV, P, P))
    for n in range(LEV - 1):
        m = P >> n
        mid = (a // m) * m + m // 2 - 1
        after = (a[:, None] > mid[None, :]) & (a[:, None] <= a[None, :])
        before = (a[:, None] > a[None, :]) & (a[:, None] <= mid[None, :])
        lev[n] = after | before
        mask[n] = ((a[:, None] // m) == (a[None, :] // m)) & (a[:, None] <= mid[None, :]) & (a[None, :] > mid[None, :])
    lev[7] = a[:, None] > a[None, :]
    lev[8] = a[:, None] <= a[None, :]
    mask[LEV - 1] = np.eye(P)
    t["lev"] = (lev / 16.0).transpose(1, 0, 2).reshape(P, -1)
    d = a[:, None] - np.arange(T)[None, :] + P
    alibi = np.where((d >= 0) & (d < P), -d, -1e30)
    t["alibi"] = np.concatenate([alibi, alibi[:, P:]], axis=1)
    i = np.arange(T)
    log_gamma = np.log1p(-np.power(2.0, -5.0 - np.arange(HEADS)))
    seen = (i[:, None] // CH) <= (i[None, :] // CH)
    dec = np.exp(log_gamma[:, None, None] * np.abs(i[:, None] - i[None, :])) * seen * DK ** -0.5
    t["ret"] = np.concatenate([dec[:, :P, :], dec[:, P:, P:]], axis=2).transpose(1, 0, 2).reshape(P, -1)
    names, at, parts = {}, 0, []
    for k, v in t.items():
        names[k] = (at, at + v.shape[1])
        at += v.shape[1]
        parts.append(v.astype(np.float32))
    return names, np.concatenate(parts, axis=1), mask.transpose(1, 0, 2).reshape(P, -1).astype(np.float32)


COLS, TABLE, MASKS = tables()
NKEEP = COLS["alibi"][1]


def after(eng, s, n, e=0):
    if not isinstance(e, int):
        eng.wait_ge(s, e + n)
    elif n + e > 0:
        eng.wait_ge(s, n + e)


def build(nc, io, out):
    with ExitStack() as ctx:
        def sb(name, shape, dt=F32, scope=ctx):
            return scope.enter_context(nc.sbuf_tensor(name, shape, dt))

        def sem(name):
            return ctx.enter_context(nc.semaphore(name))

        x = sb("x", [P, KT, T])
        hn = sb("hn", [P, KT, T])
        sq = sb("sq", [P, KT, T])
        a_hi, a_lo = sb("a_hi", [P, KT, T], F32R), sb("a_lo", [P, KT, T], F32R)
        b_hi, b_lo = sb("b_hi", [P, KT, T], F32R), sb("b_lo", [P, KT, T], F32R)
        raw = [sb(f"raw{s}", [P, KT, UC]) for s in range(NS)]
        w_hi = [sb(f"w_hi{s}", [P, KT, UC], F32R) for s in range(NS)]
        w_lo = [sb(f"w_lo{s}", [P, KT, UC], F32R) for s in range(NS)]
        keep = sb("keep", [P, NKEEP])

        def const(name):
            return keep[:, COLS[name][0]:COLS[name][1]]

        ident, means, headsel = const("ident"), const("means"), const("headsel")
        masks = sb("masks", [P, LEV, P], U8)
        vecs = sb("vecs", [P, 4, VCOL])
        var2, rstd2 = sb("var2", [P, 2]), sb("rstd2", [P, 2])
        var8, rstd8 = sb("var8", [P, 8]), sb("rstd8", [P, 8])
        rb = sb("rb", [P, T])
        mhalf = sb("mhalf", [P, 1])
        ones_row = sb("ones_row", [1, P])
        sink_row = sb("sink_row", [1, LAYERS * 16])
        sinks = sb("sinks", [P, LAYERS, 16])
        glr_t = sb("glr_t", [32, T])
        w2aug = sb("w2aug", [17, LAYERS, P])

        m1 = ExitStack()
        ret_d = sb("ret_d", [P, HEADS, 384], scope=m1)
        cos2, sin2 = sb("cos2", [P, T], scope=m1), sb("sin2", [P, T], scope=m1)
        e_xl = sb("e_xl", [P, KT, T + 3], scope=m1)
        e2, e3, e4, e5, e6, e7 = (sb(f"e{n}", [P, KT, T], scope=m1) for n in range(2, 8))
        half_b = sb("half_b", [P, 40], scope=m1)
        sp4 = sb("sp4", [P, 8], scope=m1)
        sp_t = sb("sp_t", [P, 6, 8], scope=m1)
        m1.close()
        qk_raw, qk_sw, qk_rot = e_xl[:, :, 0:T], e2, e3
        xl, xc, la = e_xl, e2, e_xl[:, :, 3:T + 3]
        o_ret, g_ret, y_lru, i_gate = e5, e6, e7, e3
        tmp, ga, gb, gel, a_lru = e5, e4, hn, hn, sq
        v_ret = e4[:, :, :].rearrange("p (t a) n -> p t (a n)", t=TT)
        st_ret = sq[:, :, :].rearrange("p a b -> p (a b)")
        masks_f32 = e7[:, 0:4, :].rearrange("p k n -> p (k n)")
        pos_i, ang_t, ang = e4[:, 0, :].bitcast(I32), e5, e6

        ff = ExitStack()
        h_hi, h_lo = sb("h_hi", [P, NF1, T], F32R, scope=ff), sb("h_lo", [P, NF1, T], F32R, scope=ff)
        th, hb, cg, cub, ab = (sb(n, [P, NS, T], scope=ff) for n in ("th", "hb", "cg", "cub", "ab"))
        ff.close()

        m2 = ExitStack()
        ek = sb("ek", [P, 2, TT, LEV, P], scope=m2)
        qg, kg = sb("qg", [P, T], scope=m2), sb("kg", [P, T], scope=m2)
        vg = sb("vg", [P, TT, 256], scope=m2)
        s_gla = sb("s_gla", [P, TT, GH, P], scope=m2)
        s_cross = sb("s_cross", [P, GH, P], scope=m2)
        lg = sb("lg", [P, 5, TT * P], scope=m2)
        qs, ks = sb("qs", [P, 4, T], scope=m2), sb("ks", [P, T], scope=m2)
        vs = sb("vs", [P, TT, P], scope=m2)
        ss = sb("ss", [P, SWH, 384], scope=m2)
        mx = sb("mx", [P, 4, 16], scope=m2)
        ca = sb("ca", [P, 2, T], scope=m2)
        up = sb("up", [P, 2, T + TAPS - 1], scope=m2)
        yc = [sb(f"yc{n}", [P, 2, T], scope=m2) for n in range(2)]
        gr, og, th2, sq2 = (sb(n, [P, 2, T], scope=m2) for n in ("gr", "og", "th2", "sq2"))
        m2.close()
        qe = sq[:, :, :].rearrange("p (t a) (b i) -> p t (a b) i", t=TT, b=2)
        pt = ek[:, :, :, :, :].rearrange("p a t n i -> p (a t n) i")

        stream = [ctx.enter_context(nc.psum_tensor(f"stream{n}", [P, 512], F32)) for n in range(3)]
        psm = ctx.enter_context(nc.psum_tensor("psm", [P, 4, 512], F32))
        ps7 = ctx.enter_context(nc.psum_tensor("ps7", [P, 512], F32))

        raw_loaded = [sem(f"raw_loaded{s}") for s in range(NS)]
        w_hi_ready, w_split, unit_used = sem("w_hi_ready"), sem("w_split"), sem("unit_used")
        rg_done, group_evac = sem("rg_done"), sem("group_evac")
        psm_full, psm_free, ps7_full, ps7_free, stat_full = (sem(n) for n in (
            "psm_full", "psm_free", "ps7_full", "ps7_free", "stat_full"))
        x_loaded, small_loaded, out_ready, out_stored = (sem(n) for n in (
            "x_loaded", "small_loaded", "out_ready", "out_stored"))
        pool_init, dve_chain, act_chain = sem("pool_init"), sem("dve_chain"), sem("act_chain")
        x_ready, sq_ready, var_ready, rstd_ready, normed, a_hi_ready, a_split = (sem(n) for n in (
            "x_ready", "sq_ready", "var_ready", "rstd_ready", "normed", "a_hi_ready", "a_split"))
        mean_ready, var8_ready, rstd8_ready = sem("mean_ready"), sem("var8_ready"), sem("rstd8_ready")
        op_ready, op_hi_ready, op_split = sem("op_ready"), sem("op_hi_ready"), sem("op_split")
        th_ready, h_hi_ready, h_split, tap_ready, conv_done, csq_ready, cube_ready = (sem(n) for n in (
            "th_ready", "h_hi_ready", "h_split", "tap_ready", "conv_done", "csq_ready", "cube_ready"))
        ang_ready, trig_ready, swapped, rot_done, act_gate, lam_arg, lam_exp, lru_conv0, lru_act = (sem(n) for n in (
            "ang_ready", "trig_ready", "swapped", "rot_done", "act_gate", "lam_arg", "lam_exp", "lru_conv0", "lru_act"))
        o_sq, ge_sq, ge_cube, ge_th, ge_done, v_ready, sqrt_done = (sem(n) for n in (
            "o_sq", "ge_sq", "ge_cube", "ge_th", "ge_done", "v_ready", "sqrt_done"))
        ez_ready, glog_ready, e_ready, ke_ready, zeroed, act2 = (sem(n) for n in (
            "ez_ready", "glog_ready", "e_ready", "ke_ready", "zeroed", "act2"))
        og_sq, yc_ready, yc_sq, silu_in, silu_th, ss_ready, ss_exp, p_ready = (sem(n) for n in (
            "og_sq", "yc_ready", "yc_sq", "silu_in", "silu_th", "ss_ready", "ss_exp", "p_ready"))
        N_SMALL = 7

        def rows(ap, r0=0, n=KT):
            return ap[r0:r0 + n * P, :].rearrange("(k p) n -> p k n", p=P)

        def pair2(bank):
            return bank.rearrange("p (a b) -> p a b", a=2)

        block = ctx.enter_context(nc.Block())

        @block.sync
        def _(sp):
            def fill(c, e, halves):
                s = c % NS
                if not (isinstance(e, int) and c + NS * e < NS):
                    after(sp, w_split, c - NS + 1, e * NS)
                for dst, src in halves(raw[s]):
                    sp.dma_start(dst, src).then_inc(raw_loaded[s], 16)

            def plain(src, n=KT):
                return lambda r: [(r[:, 0:4, :], src[:, 0:4, :]), (r[:, 4:n, :], src[:, 4:n, :])]

            def pair(first, second):
                return lambda r: [(r[:, :, 0:P], first), (r[:, :, P:UC], second)]

            def interleaved(first, second):
                return lambda r: [(r[:, :, SWD * (2 * j + g):SWD * (2 * j + g) + SWD], src[:, :, SWD * j:SWD * j + SWD])
                                  for j in range(2) for g, src in enumerate((first, second))]

            sp.dma_start(hn[:, :, :].rearrange("p (t a) n -> p t (a n)", t=TT),
                         io["x"][0].rearrange("(t p) d -> p t d", p=P)).then_inc(x_loaded, 16)
            w_in = rows(io["w_in"][0])
            cols = [at + UC * i for at, m in ((0, 2), (512, 2), (1024, 4), (3072, 4), (4096, 4), (2048, 4))
                    for i in range(m)]
            c = 0
            for col in cols:
                fill(c, 0, plain(w_in[:, :, col:col + UC]))
                c += 1
            for name in ("lru_w_r", "lru_w_i"):
                fill(c, 0, plain(io[name][0].rearrange("b (k p) n -> p (b k) n", p=P)))
                c += 1
            for i in range(8):
                fill(c, 0, plain(w_in[:, :, 5120 + UC * i:5120 + UC * i + UC]))
                c += 1
            for name in ("w_ret_o", "w_lru_o", "w_out"):
                for i in range(4):
                    fill(c, 0, plain(rows(io[name][0])[:, :, UC * i:UC * i + UC]))
                    c += 1
            w_up = rows(io["ffn_w_up"][0])
            with sp.Fori(0, NF1 // 3) as i:
                for j in range(3):
                    fill(U1_UP + j, i, pair(w_up[:, :, bass.ds(i * (3 * P) + j * P, P)],
                                            w_up[:, :, bass.ds(i * (3 * P) + (j * P + DFF1), P)]))
            with sp.Fori(0, 2) as i:
                for j in range(6):
                    src = rows(io["ffn_w_down"][0], KT * P * (j % 3))
                    fill(U1_DOWN + j, i * 2, plain(src[:, :, bass.ds(i * 512 + UC * (j // 3), UC)]))

            def ffn(c, l, f):
                g_rows, u_rows = rows(io["ffn_w_gate_2"][l, f]), rows(io["ffn_w_up_2"][l, f])
                fill(c, 0, pair(g_rows[:, :, 0:P], u_rows[:, :, 0:P]))
                with sp.Fori(0, (NF2 - 1) // 3) as i:
                    for j in range(3):
                        at = bass.ds(i * (3 * P) + (j + 1) * P, P)
                        fill(c + 1 + j, i, pair(g_rows[:, :, at], u_rows[:, :, at]))
                with sp.Fori(0, 2) as i:
                    for j in range(6):
                        n = min(KT, NF2 - KT * (j % 3))
                        src = rows(io["ffn_w_down_2"][l, f], KT * P * (j % 3), n)
                        fill(c + NF2 + j, i * 2, plain(src[:, :, bass.ds(i * 512 + UC * (j // 3), UC)], n))

            for l in range(LAYERS):
                c0 = U1_END + UL * l
                ffn(c0, l, 0)
                c = c0 + UL_MIX
                wi = rows(io["w_in_2"][l])
                fill(c, 0, lambda r: [(r[:, 0:4, 0:P], wi[:, 0:4, 768:768 + P]), (r[:, 4:8, 0:P], wi[:, 4:8, 768:768 + P])])
                for n, col in enumerate((0, 256, 1808)):
                    fill(c + 1 + n, 0, plain(wi[:, :, col:col + UC]))
                for n in range(2):
                    col = 1296 + P * n
                    fill(c + 4 + n, 0, interleaved(wi[:, :, col:col + P], wi[:, :, col + 256:col + 256 + P]))
                for n, col in enumerate((784, 1040, 512)):
                    fill(c + 6 + n, 0, plain(wi[:, :, col:col + UC]))
                for n in range(4):
                    fill(c + 9 + n, 0, plain(rows(io["w_out_2"][l])[:, :, UC * n:UC * n + UC]))
                ffn(c0 + UL_UP_B, l, 1)
            sp.wait_ge(out_ready, 1)
            sp.dma_start(out[0].rearrange("(t p) d -> p t d", p=P),
                         hn[:, :, :].rearrange("p (t a) n -> p t (a n)", t=TT)).then_inc(out_stored, 16)
            sp.wait_ge(out_stored, 16)

        @block.gpsimd
        def _(pool):
            done = {"norm": 0, "head": 0}
            nc.gpsimd.memset(mhalf[:, :], -0.5).then_inc(pool_init, 1)
            nc.gpsimd.memset(ones_row[:, :], 1.0).then_inc(pool_init, 1)
            nc.gpsimd.memset(glr_t[:, :], 1.0).then_inc(pool_init, 1)
            pool.wait_ge(pool_init, 3)

            def power_norm():
                done["norm"] += 1
                pool.wait_ge(var_ready, done["norm"])
                nc.gpsimd.tensor_tensor(rstd2[:, :], var2[:, :], mhalf[:, 0:1].broadcast_to([P, 2]),
                                        ALU.pow).then_inc(rstd_ready, 1)

            def power_heads(n):
                done["head"] += 1
                pool.wait_ge(var8_ready, done["head"])
                nc.gpsimd.tensor_tensor(rstd8[:, 0:n], var8[:, 0:n], mhalf[:, 0:1].broadcast_to([P, n]),
                                        ALU.pow).then_inc(rstd8_ready, 1)

            power_norm()
            power_heads(8)
            power_norm()
            power_norm()
            for l in range(LAYERS):
                power_norm()
                power_norm()
                power_norm()
                g_mix = G1_END + GL * l + GL_MIX
                pool.wait_ge(group_evac, g_mix)
                nc.gpsimd.memset(s_gla[:, :, :, :], 0.0).then_inc(zeroed, 1)
                nc.gpsimd.memset(up[:, :, 0:TAPS - 1], 0.0).then_inc(zeroed, 1)
                for t in range(TT):
                    pool.wait_ge(group_evac, g_mix + 2)
                    pool.wait_ge(e_ready, TT * l + t + 1)
                    nc.gpsimd.tensor_tensor(
                        ek[:, 1, t], ek[:, 0, t],
                        kg[:, t * P:t * P + P].rearrange("p (o i) -> p o i", o=1).broadcast_to([P, LEV, P]),
                        ALU.mult).then_inc(ke_ready, 1)
                power_heads(8)
                power_heads(2)
                power_norm()
                power_norm()
                power_norm()

        @block.scalar
        def _(act):
            count = {"chain": 0, "a_hi": 0, "op_hi": 0}
            third = [0]

            def link(ins):
                count["chain"] += 1
                ins.then_inc(act_chain, 1)
                act.wait_ge(act_chain, count["chain"])

            def hi(c, e=0):
                if isinstance(e, int) and c + NS * e >= TOTAL_UNITS:
                    return
                s = c % NS
                queries = sum(q <= c and q % NS == s for q in QUERY_UNITS)
                after(act, raw_loaded[s], 32 * (c // NS + 1 + queries), e * 32)
                if not (isinstance(e, int) and c + NS * e < NS):
                    after(act, unit_used, c - NS + 1, e * NS)
                nc.scalar.activation(w_hi[s][:, :, :], raw[s][:, :, :], ACT.Copy).then_inc(w_hi_ready, 1)

            def squares(src, tiles=range(KT)):
                for k in tiles:
                    nc.scalar.activation(sq[:, k, :], src[:, k, :], ACT.Square).then_inc(sq_ready, 1)

            def x_squares(n):
                for k in range(KT):
                    act.wait_ge(x_ready, KT * n + k + 1)
                    squares(x, (k,))

            def norm_hi():
                for k in range(KT):
                    count["a_hi"] += 1
                    act.wait_ge(normed, count["a_hi"])
                    nc.scalar.activation(a_hi[:, k, :], hn[:, k, :], ACT.Copy).then_inc(a_hi_ready, 1)

            def operand_hi(dst, src, ready, used=0):
                act.wait_ge(*ready)
                after(act, unit_used, used)
                nc.scalar.activation(dst, src, ACT.Copy).then_inc(op_hi_ready, 1)

            def op(n):
                return op_ready, n

            act.dma_start(keep[:, :], io["table"][:, 0:NKEEP]).then_inc(small_loaded, 16)
            act.dma_start(sq[:, 0:2, :].rearrange("p a b -> p (a b)"), io["vec_rows"]).then_inc(small_loaded, 16)
            act.dma_start(pos_i, io["positions"].broadcast_to([P, T])).then_inc(small_loaded, 16)
            act.dma_start(masks_f32, io["masks"]).then_inc(small_loaded, 16)
            act.dma_start(ret_d[:, :, :].rearrange("p h n -> p (h n)"),
                          io["table"][:, COLS["ret"][0]:COLS["ret"][1]]).then_inc(small_loaded, 16)
            act.dma_start(sink_row[:, :], io["sink_row"]).then_inc(small_loaded, 16)
            act.dma_start(w2aug[:, :, :].rearrange("p l n -> p (l n)"), io["gate2"]).then_inc(small_loaded, 16)

            act.wait_ge(ang_ready, 1)
            nc.scalar.activation(sin2[:, :], ang[:, 0, :], ACT.Sin, scale=const("sgn")).then_inc(trig_ready, 1)
            act.wait_ge(ang_ready, 2)
            nc.scalar.activation(cos2[:, :], ang[:, 1, :], ACT.Sin).then_inc(trig_ready, 1)
            act.wait_ge(psm_free, PSM_X + 1)
            act.wait_ge(ps7_free, PS7_VEC + 1)
            squares(x)
            act.wait_ge(lam_arg, 1)
            nc.scalar.activation(sp_t[:, 1, :], sp_t[:, 0, :], ACT.Exp, scale=-1.0).then_inc(lam_exp, 1)
            hi(0)
            hi(1)
            norm_hi()
            for u in range(4):
                hi(u + 2)
                act.wait_ge(unit_used, u + 1)
                for half in range(2):
                    to, of = 64 * half, 64 * (1 - half)
                    nc.scalar.activation(qk_sw[to:to + 64, 2 * u:2 * u + 2, :], pair2(stream[u % 3][of:of + 64, :]),
                                         ACT.Copy).then_inc(swapped, 1)
            for u in range(4, 12):
                hi(u + 2)
            act.wait_ge(group_evac, 12)
            act.wait_ge(rot_done, 1)
            for k in range(KT):
                nc.scalar.activation(xc[:, k, :], xl[:, k, 3:3 + T], ACT.Identity,
                                     bias=vecs[:, 0, V1["lconv_b"] + k:V1["lconv_b"] + k + 1],
                                     scale=vecs[:, 0, V1["lconv_w"] + 24 + k:V1["lconv_w"] + 25 + k]).then_inc(lru_conv0, 1)
            for u in range(12, 16):
                hi(u + 2)
            operand_hi(b_hi[:, :, :], xc[:, :, :], op(1))
            act.wait_ge(psm_free, PSM_MEAN + 1)
            nc.scalar.activation(sq[:, :, :], o_ret[:, :, :], ACT.Square).then_inc(o_sq, 1)
            for n in range(4):
                u = 16 + n
                hi(u + 2)
                act.wait_ge(unit_used, u + 1)
                nc.scalar.activation(g_ret[:, 2 * n:2 * n + 2, :], pair2(stream[u % 3][:, :]), ACT.Tanh,
                                     scale=0.5).then_inc(act_gate, 1)
            act.wait_ge(group_evac, 16)
            nc.scalar.activation(gel[:, :, :], y_lru[:, :, :], ACT.Square).then_inc(ge_sq, 1)
            for n in range(8):
                if n % 4 == 0:
                    hi(U1_RG + n // 4 + 2)
                g = G1_RG + n
                if n % 4 < 3:
                    act.wait_ge(rg_done, 3 * (n // 4) + n % 4 + 1)
                else:
                    act.wait_ge(unit_used, U1_RG + n // 4 + 1)
                dst = la if n < 4 else i_gate
                for f in range(2):
                    k = 2 * (n % 4) + f
                    col = 8 * (n // 4) + k
                    nc.scalar.activation(dst[:, k, :], stream[g % 3][:, f * T:f * T + T], ACT.Tanh,
                                         bias=half_b[:, col:col + 1], scale=0.5).then_inc(act_gate, 1)
            act.wait_ge(ge_cube, 1)
            nc.scalar.activation(gel[:, :, :], gel[:, :, :], ACT.Tanh, scale=SQ2PI * GELU_C).then_inc(ge_th, 1)
            operand_hi(b_hi[:, :, :], o_ret[:, :, :], op(2), U1_GATES)
            act.wait_ge(group_evac, G1_RG + 4)
            nc.scalar.activation(a_lru[:, :, :], la, ACT.Exp).then_inc(lru_act, 1)
            nc.scalar.activation(la, la, ACT.Tanh).then_inc(lru_act, 1)
            act.wait_ge(ge_done, 1)
            for n in range(8):
                hi(U1_GATES + n + 2)
                g = G1_GATES + n
                act.wait_ge(unit_used, U1_GATES + n + 1)
                dst = ga if n < 4 else gb
                for f in range(2):
                    k = 2 * (n % 4) + f
                    col = 16 + 8 * (n // 4) + k
                    nc.scalar.activation(dst[:, k, :], stream[g % 3][:, f * T:f * T + T], ACT.Tanh,
                                         bias=half_b[:, col:col + 1], scale=0.5).then_inc(act_gate, 1)
                if n == 2:
                    act.wait_ge(v_ready, 1)
                    nc.scalar.activation(la, la, ACT.Sqrt).then_inc(sqrt_done, 1)
            operand_hi(a_hi[:, :, :], y_lru[:, :, :], op(3), U1_RETO)
            for n in range(8):
                hi(U1_RETO + n + 2)
                if n >= 4:
                    m = n - 4
                    operand_hi(b_hi[:, 2 * m:2 * m + 2, :], ga[:, 2 * m:2 * m + 2, :], op(4 + m), U1_LRUO)
            for n in range(4):
                hi(U1_OUT + n + 2)
                act.wait_ge(group_evac, G1_OUT + n + 1)
                squares(x, (2 * n, 2 * n + 1))
            norm_hi()

            def hidden_hi(j, e3, g0):
                after(act, group_evac, g0 + j + 1, e3)
                dst = h_hi[:, j, :] if isinstance(e3, int) else h_hi[:, bass.ds(e3 + j, 1), :].rearrange("p o n -> p (o n)")
                nc.scalar.activation(dst, hb[:, j % 3, :], ACT.Copy).then_inc(h_hi_ready, 1)

            def ff1_step(j, e, e3):
                def col(name, extra):
                    at = V1B[name] + extra + j
                    return vecs[:, 1, at:at + 1] if isinstance(e3, int) else vecs[:, 1, bass.ds(e3 + at, 1)]

                hi(U1_UP + j + 2, e)
                after(act, unit_used, U1_UP + j + 1, e3)
                nc.scalar.activation(cg[:, j % 3, :], stream[j % 3][:, 0:T], ACT.Identity, bias=col("fconv_b", 0),
                                     scale=col("fconv_w", 2 * NF1)).then_inc(tap_ready, 1)
                if j or not isinstance(e3, int):
                    gelu_tanh(j - 1, e3)
                after(act, conv_done, j + 1, e3)
                nc.scalar.activation(cub[:, j % 3, :], cg[:, j % 3, :], ACT.Square).then_inc(csq_ready, 1)
                if j or not isinstance(e3, int):
                    hidden_hi(j - 1, e3, G1_UP)

            def gelu_tanh(j, e3):
                after(act, cube_ready, j + 1, e3)
                nc.scalar.activation(th[:, j % 3, :], cub[:, j % 3, :], ACT.Tanh, scale=SQ2PI * GELU_C).then_inc(th_ready, 1)

            for j in range(3):
                ff1_step(j, 0, 0)
            with act.Fori(1, NF1 // 3) as i:
                for j in range(3):
                    ff1_step(j, i, i * 3)
            gelu_tanh(NF1 - 1, 0)
            hidden_hi(NF1 - 1, 0, G1_UP)
            for n in range(4):
                for m in range(3):
                    hi(U1_DOWN + 3 * n + m + 2)
                act.wait_ge(group_evac, G1_DOWN + n + 1)
                squares(x, (2 * n, 2 * n + 1))

            def ffn(c0, g0, bank0, h0):
                def unit(j, e, e3):
                    hi(c0 + j + 2, e)
                    after(act, unit_used, c0 + j + 1, e3)
                    nc.scalar.activation(th[:, j % 3, :], stream[(bank0 + j) % 3][:, 0:T], ACT.Tanh,
                                         scale=0.5).then_inc(th_ready, 1)
                    hidden_hi(j, e3, g0)

                unit(0, 0, 0)
                with act.Fori(0, (NF2 - 1) // 3) as i:
                    for j in range(1, 4):
                        unit(j, i, i * 3)
                for n in range(4):
                    for m in range(3):
                        hi(c0 + NF2 + 3 * n + m + 2)
                    act.wait_ge(group_evac, g0 + NF2 + n + 1)
                    squares(hn, (2 * n, 2 * n + 1))

            for l in range(LAYERS):
                c0, g0 = U1_END + UL * l, G1_END + GL * l
                psm0, ps70, op0 = PSM_1 + PSM_L * l, PS7_1 + PS7_L * l, 7 + 2 * l
                x_squares(3 * l)
                norm_hi()
                ffn(c0, g0, 0, 0)
                x_squares(3 * l + 1)
                norm_hi()
                cm, gm = c0 + UL_MIX, g0 + GL_MIX
                hi(cm + 2)
                hi(cm + 3)
                act.wait_ge(ps7_full, ps70 + PS7_Z + 1)
                link(nc.scalar.activation(lg[:, 0, :], ps7[:, 0:T], ACT.Abs))
                nc.scalar.activation(lg[:, 0, :], lg[:, 0, :], ACT.Exp, scale=-1.0).then_inc(ez_ready, 1)
                hi(cm + 4)
                hi(cm + 5)
                act.wait_ge(psm_full, psm0 + PSM_LEV + 1)
                for t in range(TT):
                    for m in range(2):
                        ins = nc.scalar.activation(ek[:, 0, t, 4 * m:4 * m + 4, :],
                                                   psm[:, 2 * t + m, :].rearrange("p (n i) -> p n i", n=4), ACT.Exp)
                    ins.then_inc(e_ready, 1)
                hi(cm + 6)
                hi(cm + 7)
                hi(cm + 8)
                hi(cm + 9)
                act.wait_ge(unit_used, cm + 8)
                nc.scalar.activation(th2[:, :, :], pair2(stream[(BANK_MIX + 7) % 3][:, :]), ACT.Tanh,
                                     scale=0.5).then_inc(act2, 1)
                hi(cm + 10)
                act.wait_ge(unit_used, cm + 9)
                nc.scalar.activation(gr[:, :, :], pair2(stream[(BANK_MIX + 8) % 3][:, :]), ACT.Tanh,
                                     scale=0.5).then_inc(act2, 1)
                act.wait_ge(ss_ready, l + 1)
                nc.scalar.activation(mx[:, 2, :], mx[:, 2, :], ACT.Exp)
                nc.scalar.activation(ss[:, :, :], ss[:, :, :], ACT.Exp).then_inc(ss_exp, 1)
                act.wait_ge(ps7_free, ps70 + PS7_PV + 1)
                nc.scalar.activation(sq2[:, :, :], og[:, :, :], ACT.Square).then_inc(og_sq, 1)
                for b, banks in enumerate((4, 2)):
                    act.wait_ge(psm_full, psm0 + PSM_PT + b + 1)
                    for m in range(banks):
                        at = 16 * b + 4 * m
                        ins = nc.scalar.activation(pt[:, at:at + 4, :], psm[:, m, :].rearrange("p (n i) -> p n i", n=4),
                                                   ACT.Copy)
                    ins.then_inc(psm_free, 1)
                operand_hi(b_hi[:, 0:2, :], hn[:, 0:2, :], op(op0 + 1))
                act.wait_ge(ps7_free, ps70 + PS7_CMEAN + 1)
                nc.scalar.activation(sq2[:, :, :], yc[0][:, :, :], ACT.Square).then_inc(yc_sq, 1)
                operand_hi(b_hi[:, 4:8, :], hn[:, 4:8, :], (psm_free, psm0 + PSM_PV + 1))
                act.wait_ge(silu_in, l + 1)
                nc.scalar.activation(th2[:, :, :], yc[0][:, :, :], ACT.Tanh, scale=0.5).then_inc(silu_th, 1)
                operand_hi(b_hi[:, 2:4, :], hn[:, 2:4, :], op(op0 + 2))
                for n in range(4):
                    hi(cm + 11 + n)
                    act.wait_ge(group_evac, g0 + GL_WOUT + n + 1)
                    squares(hn, (2 * n, 2 * n + 1))
                x_squares(3 * l + 2)
                norm_hi()
                ffn(c0 + UL_UP_B, g0 + GL_UP_B, BANK_UP_B, NF2)

        @block.vector
        def _(dve):
            V = nc.vector
            chain = {"n": 0, "e": 0}
            count = {"a_lo": 0, "op_lo": 0}

            def mark(ins):
                chain["n"] += 1
                ins.then_inc(dve_chain, 1)
                return chain["n"]

            def link(ins):
                after(dve, dve_chain, mark(ins), chain["e"])

            def lo(c, e=0):
                if isinstance(e, int) and c + NS * e >= TOTAL_UNITS:
                    return
                s = c % NS
                after(dve, w_hi_ready, c + 1, e * NS)
                V.tensor_tensor(w_lo[s][:, :, :], raw[s][:, :, :], w_hi[s][:, :, :].bitcast(F32),
                                ALU.subtract).then_inc(w_split, 1)

            def operand_lo(dst, src, hi_part):
                count["op_lo"] += 1
                dve.wait_ge(op_hi_ready, count["op_lo"])
                V.tensor_tensor(dst, src, hi_part.bitcast(F32), ALU.subtract).then_inc(op_split, 1)

            def inv_rms(st, p7):
                dve.wait_ge(stat_full, st + 1)
                V.tensor_scalar(var2[:, :], ps7[:, 0:2], RMS_EPS, None, ALU.add).then_inc(var_ready, 1)
                dve.wait_ge(ps7_full, p7 + 1)
                V.tensor_copy(rb[:, :], ps7[:, T:2 * T]).then_inc(ps7_free, 1)
                dve.wait_ge(ps7_free, p7 + 1)

            def pre_norm(st, p7, group, col):
                inv_rms(st, p7)

                def lo_tile(k):
                    count["a_lo"] += 1
                    dve.wait_ge(a_hi_ready, count["a_lo"])
                    V.tensor_tensor(a_lo[:, k, :], hn[:, k, :], a_hi[:, k, :].bitcast(F32),
                                    ALU.subtract).then_inc(a_split, 1)

                for k in range(KT):
                    V.scalar_tensor_tensor(out=hn[:, k, :], in0=x[:, k, :], scalar=vecs[:, group, col + k:col + k + 1],
                                           in1=rb[:, :], op0=ALU.mult, op1=ALU.mult).then_inc(normed, 1)
                    if k >= 2:
                        lo_tile(k - 2)
                lo_tile(KT - 2)
                lo_tile(KT - 1)

            def post_norm(st, p7, group, col, scale):
                inv_rms(st, p7)
                at = []
                for k in range(KT + 1):
                    if k < KT:
                        at.append(mark(V.scalar_tensor_tensor(
                            out=hn[:, k, :], in0=hn[:, k, :], scalar=vecs[:, group, col + k:col + k + 1],
                            in1=rb[:, :], op0=ALU.mult, op1=ALU.mult)))
                    if k:
                        dve.wait_ge(dve_chain, at[k - 1])
                        V.scalar_tensor_tensor(out=x[:, k - 1, :], in0=hn[:, k - 1, :], scalar=scale,
                                               in1=x[:, k - 1, :], op0=ALU.mult, op1=ALU.add).then_inc(x_ready, 1)

            def half_log1p(dst, s, s2, e):
                link(V.tensor_scalar(s, e, 2.0, None, ALU.add))
                link(V.reciprocal(s, s))
                link(V.tensor_tensor(s, s, e, ALU.mult))
                link(V.tensor_tensor(s2, s, s, ALU.mult))
                link(V.tensor_scalar(dst, s2, 1.0 / 17, None, ALU.mult))
                for n in (15, 13, 11, 9, 7, 5, 3):
                    link(V.scalar_tensor_tensor(out=dst, in0=dst, scalar=1.0 / n, in1=s2, op0=ALU.add, op1=ALU.mult))
                link(V.scalar_tensor_tensor(out=dst, in0=dst, scalar=1.0, in1=s, op0=ALU.add, op1=ALU.mult))

            dve.wait_ge(small_loaded, 16 * N_SMALL)
            two_pi = 2 * np.pi
            c1 = 6.28125
            c2 = round((two_pi - c1) * 2 ** 20) / 2 ** 20
            c3 = two_pi - c1 - c2
            link(V.tensor_copy(ang_t[:, 0, :], pos_i))
            link(V.tensor_scalar(ang_t[:, 1, :], ang_t[:, 0, :], const("invf"), None, ALU.mult))
            for n, (shift, offset) in enumerate(((0.0, 0.0), (0.25, np.pi / 2))):
                r = ang[:, n, :]
                link(V.tensor_scalar(ang_t[:, 2, :], ang_t[:, 1, :], 1 / two_pi, shift, ALU.mult, ALU.add))
                link(V.tensor_scalar(ang_t[:, 2, :], ang_t[:, 2, :], MAGIC, -MAGIC, ALU.add, ALU.add))
                link(V.scalar_tensor_tensor(out=r, in0=ang_t[:, 2, :], scalar=-c1, in1=ang_t[:, 1, :],
                                            op0=ALU.mult, op1=ALU.add))
                for cn in (c2, c3):
                    link(V.scalar_tensor_tensor(out=r, in0=ang_t[:, 2, :], scalar=-cn, in1=r, op0=ALU.mult, op1=ALU.add))
                link(V.tensor_scalar(r, r, offset, 3.1415925, ALU.add, ALU.min))
                V.tensor_scalar(r, r, -3.1415925, None, ALU.max).then_inc(ang_ready, 1)
            link(V.tensor_copy(masks[:, :, :].rearrange("p n i -> p (n i)"), masks_f32))
            dve.wait_ge(psm_full, PSM_X + 1)
            for n in range(4):
                ins = V.tensor_copy(x[:, 2 * n:2 * n + 2, :], pair2(psm[:, n, :]))
            ins.then_inc(psm_free, 1)
            dve.wait_ge(ps7_full, PS7_VEC + 1)
            V.tensor_copy(vecs[:, :, :], ps7[:, :].rearrange("p (g c) -> p g c", g=4)).then_inc(ps7_free, 1)
            dve.wait_ge(ps7_full, PS7_SINK + 1)
            V.tensor_copy(sinks[:, :, :], ps7[:, 0:LAYERS * 16].rearrange("p (l n) -> p l n", l=LAYERS)).then_inc(ps7_free, 1)
            dve.wait_ge(ps7_free, PS7_SINK + 1)
            for dst, name, n in ((0, "b_r", 16), (16, "gate_b", 16), (32, "gn", 8)):
                V.tensor_scalar(half_b[:, dst:dst + n], vecs[:, 0, V1[name]:V1[name] + n], 0.5, None, ALU.mult)
            lam = vecs[:, 0, V1["lam"]:V1["lam"] + KT]
            link(V.tensor_scalar(sp_t[:, 3, :], lam, -1.0, None, ALU.mult))
            V.tensor_tensor(sp_t[:, 0, :], lam, sp_t[:, 3, :], ALU.max).then_inc(lam_arg, 1)
            link(V.tensor_scalar(sp_t[:, 2, :], lam, 0.0, 4.0, ALU.min, ALU.mult))
            pre_norm(ST_N0, PS7_N0, 0, V1["norm1"])
            lo(0)
            lo(1)
            dve.wait_ge(lam_exp, 1)
            half_log1p(sp_t[:, 5, :], sp_t[:, 3, :], sp_t[:, 4, :], sp_t[:, 1, :])
            link(V.scalar_tensor_tensor(out=sp4[:, :], in0=sp_t[:, 5, :], scalar=-8.0, in1=sp_t[:, 2, :],
                                        op0=ALU.mult, op1=ALU.add))

            for u in range(4):
                lo(u + 2)
                dve.wait_ge(swapped, 2 * u + 2)
                V.tensor_copy(qk_raw[:, 2 * u:2 * u + 2, :], pair2(stream[u % 3][:, :])).then_inc(group_evac, 1)
            dve.wait_ge(trig_ready, 2)
            dve.wait_ge(group_evac, 4)

            def over_tiles(ap):
                return ap.rearrange("p (o n) -> p o n", o=1).broadcast_to([P, KT, T])

            for n in range(4):
                u = 4 + n
                if n == 0:
                    rot0 = mark(V.tensor_tensor(qk_raw, qk_raw, over_tiles(cos2[:, :]), ALU.mult))
                elif n == 1:
                    rot1 = mark(V.tensor_tensor(qk_sw[:, :, :], qk_sw[:, :, :], over_tiles(sin2[:, :]), ALU.mult))
                elif n == 2:
                    dve.wait_ge(dve_chain, rot1)
                    V.tensor_tensor(qk_rot[:, :, :], qk_raw, qk_sw[:, :, :], ALU.add).then_inc(rot_done, 1)
                lo(u + 2)
                dve.wait_ge(unit_used, u + 1)
                V.tensor_copy(v_ret[:, :, UC * n:UC * n + UC], pair2(stream[u % 3][:, :])).then_inc(group_evac, 1)
            dve.wait_ge(rot_done, 1)
            link(V.memset(xl[:, :, 0:3], 0.0))
            for n in range(4):
                u = 8 + n
                lo(u + 2)
                dve.wait_ge(unit_used, u + 1)
                V.tensor_copy(xl[:, 2 * n:2 * n + 2, 3:3 + T], pair2(stream[u % 3][:, :])).then_inc(group_evac, 1)
                if n == 2:
                    dve.wait_ge(psm_full, PSM_SC + 1)
                    for h in range(HEADS):
                        ins = V.tensor_tensor(st_ret[:, 384 * h:384 * h + 384], psm[:, h, 0:384], ret_d[:, h, :], ALU.mult)
                    ins.then_inc(psm_free, 1)

            at = [0] * KT
            for n in range(4):
                u = 12 + n
                lo(u + 2)
                dve.wait_ge(unit_used, u + 1)
                V.tensor_copy(y_lru[:, 2 * n:2 * n + 2, :], pair2(stream[u % 3][:, :])).then_inc(group_evac, 1)
                if n == 0:
                    dve.wait_ge(psm_full, PSM_O + 1)
                    for h in range(HEADS):
                        ins = V.tensor_copy(o_ret[:, 2 * h:2 * h + 2, :], pair2(psm[:, h, :]))
                    ins.then_inc(psm_free, 1)
                if n == 2:
                    dve.wait_ge(stat_full, ST_RMEAN + 1)
                    V.tensor_copy(var8[:, :], ps7[:, 0:8]).then_inc(mean_ready, 1)
                if n < 3:
                    tap = 2 - n
                    for k in range(KT):
                        if n == 0:
                            dve.wait_ge(lru_conv0, k + 1)
                        else:
                            dve.wait_ge(dve_chain, at[k])
                        col = V1["lconv_w"] + 8 * tap + k
                        ins = V.scalar_tensor_tensor(out=xc[:, k, :], in0=xl[:, k, tap:tap + T],
                                                     scalar=vecs[:, 0, col:col + 1], in1=xc[:, k, :],
                                                     op0=ALU.mult, op1=ALU.add)
                        if n < 2 or k < KT - 1:
                            at[k] = mark(ins)
                        else:
                            ins.then_inc(op_ready, 1)
            operand_lo(b_lo[:, :, :], xc[:, :, :], b_hi[:, :, :])

            def heads(tile, b):
                return tile[:, 4 * b:4 * b + 4, :].rearrange("p (h d) n -> p h d n", h=2)

            def over_halves(b):
                return psm[:, b, :].rearrange("p (h o n) -> p h o n", h=2, o=1).broadcast_to([P, 2, 2, T])

            dve.wait_ge(psm_full, PSM_MEAN + 1)
            for b in range(2):
                ins = V.tensor_tensor(heads(o_ret, b), heads(o_ret, b), over_halves(b), ALU.subtract)
            ins.then_inc(psm_free, 1)
            for n in range(4):
                u = 16 + n
                lo(u + 2)
                dve.wait_ge(act_gate, n + 1)
                V.scalar_tensor_tensor(out=g_ret[:, 2 * n:2 * n + 2, :], in0=g_ret[:, 2 * n:2 * n + 2, :], scalar=1.0,
                                       in1=pair2(stream[u % 3][:, :]), op0=ALU.add, op1=ALU.mult).then_inc(group_evac, 1)
                if n == 0:
                    dve.wait_ge(stat_full, ST_RVAR + 1)
                    V.tensor_scalar(var8[:, :], ps7[:, 0:8], RMS_EPS, None, ALU.add).then_inc(var8_ready, 1)
                if n == 1:
                    dve.wait_ge(psm_full, PSM_VAR + 1)
                    for b in range(2):
                        ins = V.tensor_tensor(heads(o_ret, b), heads(o_ret, b), over_halves(b), ALU.mult)
                    ins.then_inc(psm_free, 1)
            dve.wait_ge(ge_sq, 1)
            V.scalar_tensor_tensor(out=gel[:, :, :], in0=gel[:, :, :], scalar=1 / GELU_C, in1=y_lru[:, :, :],
                                   op0=ALU.add, op1=ALU.mult).then_inc(ge_cube, 1)
            dve.wait_ge(group_evac, 20)
            dve.wait_ge(psm_free, PSM_VAR + 1)
            for k in range(KT):
                ins = V.scalar_tensor_tensor(out=o_ret[:, k, :], in0=o_ret[:, k, :], scalar=half_b[:, 32 + k:33 + k],
                                             in1=g_ret[:, k, :], op0=ALU.mult, op1=ALU.mult)
            ins.then_inc(op_ready, 1)
            for n in range(8):
                if n % 4 == 0:
                    lo(U1_RG + n // 4 + 2)
                dve.wait_ge(act_gate, 4 + 2 * n + 2)
                for f in range(2):
                    k = 2 * (n % 4) + f
                    if n < 4:
                        ins = V.tensor_scalar(la[:, k, :], la[:, k, :], 1.0, sp4[:, k:k + 1], ALU.add, ALU.mult)
                    else:
                        ins = V.scalar_tensor_tensor(out=i_gate[:, k, :], in0=i_gate[:, k, :], scalar=1.0,
                                                     in1=xc[:, k, :], op0=ALU.add, op1=ALU.mult)
                ins.then_inc(group_evac, 1)
            operand_lo(b_lo[:, :, :], o_ret[:, :, :], b_hi[:, :, :])
            dve.wait_ge(ge_th, 1)
            V.scalar_tensor_tensor(out=y_lru[:, :, :], in0=gel[:, :, :], scalar=1.0, in1=y_lru[:, :, :],
                                   op0=ALU.add, op1=ALU.mult).then_inc(ge_done, 1)
            for n in range(8):
                lo(U1_GATES + n + 2)
                dve.wait_ge(act_gate, 20 + 2 * n + 2)
                dst = (ga if n < 4 else gb)[:, 2 * (n % 4):2 * (n % 4) + 2, :]
                V.tensor_scalar(dst, dst, 0.5, 0.5, ALU.mult, ALU.add).then_inc(group_evac, 1)
                if n == 0:
                    dve.wait_ge(lru_act, 2)
                    dve.wait_ge(op_split, 2)
                    link(V.tensor_scalar(tmp[:, :, :], la, -1.0, 1.0, ALU.mult, ALU.add))
                    link(V.reciprocal(tmp[:, :, :], tmp[:, :, :]))
                    link(V.scalar_tensor_tensor(out=la, in0=la, scalar=-2.0, in1=tmp[:, :, :], op0=ALU.mult, op1=ALU.mult))
                    V.tensor_scalar(la, la, 1e-30, None, ALU.max).then_inc(v_ready, 1)
                if n == 4:
                    dve.wait_ge(sqrt_done, 1)
                    link(V.scalar_tensor_tensor(out=i_gate[:, :, :], in0=i_gate[:, :, :], scalar=0.5, in1=la,
                                                op0=ALU.mult, op1=ALU.mult))
                if n == 5:
                    for k in range(KT):
                        at[k] = mark(V.tensor_tensor_scan(tmp[:, k, :], a_lru[:, k, :], i_gate[:, k, :], 0.0,
                                                          ALU.mult, ALU.add))
                if n == 6:
                    dve.wait_ge(dve_chain, at[KT - 1])
                    V.scalar_tensor_tensor(out=y_lru[:, :, :], in0=tmp[:, :, :], scalar=0.5, in1=y_lru[:, :, :],
                                           op0=ALU.mult, op1=ALU.mult).then_inc(op_ready, 1)
            for n in range(4):
                lo(U1_RETO + n + 2)
                if n == 0:
                    operand_lo(a_lo[:, :, :], y_lru[:, :, :], a_hi[:, :, :])
                g = G1_RETO + n
                dve.wait_ge(unit_used, U1_RETO + n + 1)
                dst = ga[:, 2 * n:2 * n + 2, :]
                V.tensor_tensor(dst, dst, pair2(stream[g % 3][:, :]), ALU.mult).then_inc(group_evac, 1)
            for n in range(4):
                lo(U1_LRUO + n + 2)
                g = G1_LRUO + n
                dve.wait_ge(unit_used, U1_LRUO + n + 1)
                dst, acc = gb[:, 2 * n:2 * n + 2, :], ga[:, 2 * n:2 * n + 2, :]
                V.tensor_tensor(dst, dst, pair2(stream[g % 3][:, :]), ALU.mult).then_inc(group_evac, 1)
                dve.wait_ge(group_evac, g + 1)
                V.tensor_tensor(acc, acc, dst, ALU.add).then_inc(op_ready, 1)
                if n:
                    operand_lo(b_lo[:, 2 * n - 2:2 * n, :], ga[:, 2 * n - 2:2 * n, :], b_hi[:, 2 * n - 2:2 * n, :])
            operand_lo(b_lo[:, 6:8, :], ga[:, 6:8, :], b_hi[:, 6:8, :])
            for n in range(4):
                lo(U1_OUT + n + 2)
                g = G1_OUT + n
                dve.wait_ge(unit_used, U1_OUT + n + 1)
                dst = x[:, 2 * n:2 * n + 2, :]
                V.tensor_tensor(dst, dst, pair2(stream[g % 3][:, :]), ALU.add).then_inc(group_evac, 1)

            dve.wait_ge(group_evac, G1_OUT + 4)
            pre_norm(ST_N1, PS7_N1, 0, V1["norm2"])

            def hidden_lo(j, e3, h0):
                after(dve, h_hi_ready, h0 + j + 1, e3)

                def tile(t):
                    return t[:, j, :] if isinstance(e3, int) else t[:, bass.ds(e3 + j, 1), :].rearrange("p o n -> p (o n)")

                V.tensor_tensor(tile(h_lo), hb[:, j % 3, :], tile(h_hi).bitcast(F32), ALU.subtract).then_inc(h_split, 1)

            def gated(j, e3, th0, val, factor):
                after(dve, th_ready, th0 + j + 1, e3)
                link(V.scalar_tensor_tensor(out=ab[:, j % 3, :], in0=th[:, j % 3, :], scalar=1.0, in1=factor,
                                            op0=ALU.add, op1=ALU.mult))
                V.scalar_tensor_tensor(out=hb[:, j % 3, :], in0=ab[:, j % 3, :], scalar=0.5, in1=val,
                                       op0=ALU.mult, op1=ALU.mult).then_inc(group_evac, 1)

            def ff1_step(j, e, e3):
                def col(tap):
                    at = V1B["fconv_w"] + NF1 * tap + j
                    return vecs[:, 1, at:at + 1] if isinstance(e3, int) else vecs[:, 1, bass.ds(e3 + at, 1)]

                before = j or not isinstance(e3, int)
                lo(U1_UP + j + 2, e)
                after(dve, tap_ready, j + 1, e3)
                bank, c = stream[j % 3], cg[:, j % 3, :]
                link(V.scalar_tensor_tensor(out=c[:, 1:T], in0=bank[:, 0:T - 1], scalar=col(1), in1=c[:, 1:T],
                                            op0=ALU.mult, op1=ALU.add))
                V.scalar_tensor_tensor(out=c[:, 2:T], in0=bank[:, 0:T - 2], scalar=col(0), in1=c[:, 2:T],
                                       op0=ALU.mult, op1=ALU.add).then_inc(conv_done, 1)
                if before:
                    ff1_product(j - 1, e3)
                after(dve, csq_ready, j + 1, e3)
                V.scalar_tensor_tensor(out=cub[:, j % 3, :], in0=cub[:, j % 3, :], scalar=1 / GELU_C, in1=c,
                                       op0=ALU.add, op1=ALU.mult).then_inc(cube_ready, 1)
                if before:
                    hidden_lo(j - 1, e3, 0)

            def ff1_product(j, e3):
                gated(j, e3, 0, stream[j % 3][:, T:2 * T], cg[:, j % 3, :])

            for j in range(3):
                ff1_step(j, 0, 0)
            n0 = chain["n"]
            with dve.Fori(1, NF1 // 3) as i:
                chain["e"] = (i - 1) * 6
                for j in range(3):
                    ff1_step(j, i, i * 3)
                assert chain["n"] - n0 == 6
            chain["n"], chain["e"] = n0 + 6 * (NF1 // 3 - 1), 0
            ff1_product(NF1 - 1, 0)
            hidden_lo(NF1 - 1, 0, 0)
            for n in range(4):
                for m in range(3):
                    lo(U1_DOWN + 3 * n + m + 2)
                dve.wait_ge(unit_used, U1_DOWN + 3 * n + 3)
                dst = x[:, 2 * n:2 * n + 2, :]
                V.tensor_tensor(dst, dst, pair2(psm[:, n % 2, :]), ALU.add).then_inc(group_evac, 1)
            dve.wait_ge(group_evac, G1_END)
            inv_rms(ST_NF, PS7_NF)
            for k in range(KT):
                V.scalar_tensor_tensor(out=x[:, k, :], in0=x[:, k, :], scalar=vecs[:, 0, V1["norm_f"] + k:V1["norm_f"] + k + 1],
                                       in1=rb[:, :], op0=ALU.mult, op1=ALU.mult).then_inc(x_ready, 1)

            def ffn(c0, g0, bank0, h0):
                def unit(j, e, e3):
                    lo(c0 + j + 2, e)
                    bank = stream[(bank0 + j) % 3]
                    gated(j, e3, h0, bank[:, T:2 * T], bank[:, 0:T])
                    hidden_lo(j, e3, h0)

                unit(0, 0, 0)
                n0 = chain["n"]
                with dve.Fori(0, (NF2 - 1) // 3) as i:
                    chain["e"] = i * 3
                    for j in range(1, 4):
                        unit(j, i, i * 3)
                    assert chain["n"] - n0 == 3
                chain["n"], chain["e"] = n0 + 3 * ((NF2 - 1) // 3), 0
                for n in range(4):
                    for m in range(3):
                        lo(c0 + NF2 + 3 * n + m + 2)
                    dve.wait_ge(unit_used, c0 + NF2 + 3 * n + 3)
                    V.tensor_copy(hn[:, 2 * n:2 * n + 2, :], pair2(psm[:, n % 2, :])).then_inc(group_evac, 1)
                dve.wait_ge(group_evac, g0 + NF2 + 4)

            for l in range(LAYERS):
                c0, g0 = U1_END + UL * l, G1_END + GL * l
                psm0, ps70, st0, h0 = PSM_1 + PSM_L * l, PS7_1 + PS7_L * l, ST_1 + ST_L * l, NF1 + 2 * NF2 * l
                group = 2 + l

                def vec(name, k):
                    return vecs[:, group, VL[name] + k:VL[name] + k + 1]

                dve.wait_ge(x_ready, KT * (3 * l + 1))
                pre_norm(st0 + ST_G0, ps70 + PS7_G0, group, 0)
                ffn(c0, g0, 0, h0)
                post_norm(st0 + ST_G1, ps70 + PS7_G1, group, 8, 0.5)
                dve.wait_ge(x_ready, KT * (3 * l + 2))
                pre_norm(st0 + ST_G2, ps70 + PS7_G2, group, 16)

                cm, gm = c0 + UL_MIX, g0 + GL_MIX

                def bank(n):
                    return stream[(BANK_MIX + n) % 3]

                def gla_scores(n):
                    dve.wait_ge(psm_full, psm0 + PSM_GLA + n + 1)
                    dve.wait_ge(zeroed, 2 * l + 1)
                    for m in range(4):
                        mask = masks[:, 4 * (n % 2) + m:4 * (n % 2) + m + 1, :].broadcast_to([P, GH, P])
                        ins = V.copy_predicated(s_gla[:, n // 2, :, :], mask, psm[:, :, m * P:m * P + P])
                        if m < 3:
                            link(ins)
                    ins.then_inc(psm_free, 1)
                    dve.wait_ge(psm_free, psm0 + PSM_GLA + n + 1)

                lo(cm + 2)
                dve.wait_ge(unit_used, cm + 1)
                V.tensor_copy(glr_t[0:16, :], bank(0)[0:16, 0:T]).then_inc(group_evac, 1)
                lo(cm + 3)
                dve.wait_ge(unit_used, cm + 2)
                V.tensor_scalar(qg[:, :], bank(1)[:, 0:T], GDK ** -0.5, None, ALU.mult)
                V.tensor_copy(kg[:, :], bank(1)[:, T:2 * T]).then_inc(group_evac, 1)
                dve.wait_ge(ez_ready, l + 1)
                V.tensor_scalar(lg[:, 1, :], ps7[:, 0:T], 0.0, None, ALU.min).then_inc(ps7_free, 1)
                half_log1p(lg[:, 4, :], lg[:, 2, :], lg[:, 3, :], lg[:, 0, :])
                dve.wait_ge(ps7_free, ps70 + PS7_Z + 1)
                V.scalar_tensor_tensor(out=lg[:, 1, :], in0=lg[:, 4, :], scalar=-2.0, in1=lg[:, 1, :],
                                       op0=ALU.mult, op1=ALU.add).then_inc(glog_ready, 1)
                lo(cm + 4)
                dve.wait_ge(unit_used, cm + 3)
                V.tensor_copy(vg[:, :, :], pair2(bank(2)[:, :])).then_inc(group_evac, 1)
                lo(cm + 5)
                dve.wait_ge(unit_used, cm + 4)
                V.tensor_copy(ks[:, :], bank(3)[:, 0:T])
                V.tensor_copy(vs[:, :, :], bank(3)[:, T:2 * T].rearrange("p (t n) -> p t n", t=TT)).then_inc(group_evac, 1)
                for t in range(TT):
                    dve.wait_ge(e_ready, TT * l + t + 1)
                    ins = V.tensor_tensor(qe[:, t, :, :], ek[:, 0, t, :, :],
                                          qg[:, t * P:t * P + P].rearrange("p (o i) -> p o i", o=1).broadcast_to([P, LEV, P]),
                                          ALU.mult)
                ins.then_inc(psm_free, 1)
                for n in range(2):
                    lo(cm + 6 + n)
                    dve.wait_ge(unit_used, cm + 5 + n)
                    V.tensor_scalar(qs[:, 2 * n:2 * n + 2, :], pair2(bank(4 + n)[:, :]), SWD ** -0.5, None,
                                    ALU.mult).then_inc(group_evac, 1)
                    gla_scores(n)
                lo(cm + 8)
                dve.wait_ge(unit_used, cm + 7)
                V.tensor_scalar(ca[:, :, :], pair2(bank(6)[:, :]), 0.5, None, ALU.mult).then_inc(group_evac, 1)
                gla_scores(2)
                lo(cm + 9)
                dve.wait_ge(zeroed, 2 * l + 2)
                dve.wait_ge(act2, 2 * l + 1)
                dve.wait_ge(group_evac, gm + 7)
                V.scalar_tensor_tensor(out=up[:, :, TAPS - 1:TAPS - 1 + T], in0=th2[:, :, :], scalar=1.0, in1=ca[:, :, :],
                                       op0=ALU.add, op1=ALU.mult).then_inc(group_evac, 1)
                gla_scores(3)
                lo(cm + 10)
                dve.wait_ge(act2, 2 * l + 2)
                V.scalar_tensor_tensor(out=gr[:, :, :], in0=gr[:, :, :], scalar=1.0, in1=pair2(bank(8)[:, :]),
                                       op0=ALU.add, op1=ALU.mult).then_inc(group_evac, 1)
                dve.wait_ge(psm_full, psm0 + PSM_CROSS + 1)
                V.tensor_copy(s_cross[:, :, :], psm[:, :, 0:P]).then_inc(psm_free, 1)
                for b in range(2):
                    dve.wait_ge(psm_full, psm0 + PSM_SWA + b + 1)
                    for n in range(4):
                        head = (n % 2) * 4 + 2 * b + n // 2
                        ins = V.scalar_tensor_tensor(out=ss[:, 4 * b + n, :], in0=const("alibi"), scalar=2.0 ** -(head + 1),
                                                     in1=psm[:, n, 0:384], op0=ALU.mult, op1=ALU.add)
                    ins.then_inc(psm_free, 1)
                dve.wait_ge(psm_free, psm0 + PSM_SWA + 2)
                V.tensor_reduce(mx[:, 0, 0:8], ss[:, :, 0:T], AX, ALU.max)
                link(V.tensor_reduce(mx[:, 0, 8:16], ss[:, :, T:384], AX, ALU.max))
                link(V.tensor_tensor(mx[:, 1, :], mx[:, 0, :], sinks[:, l, :], ALU.max))
                V.tensor_tensor(mx[:, 2, :], sinks[:, l, :], mx[:, 1, :], ALU.subtract)

                def per_row(n, a, width):
                    return mx[:, n, a:a + 8].rearrange("p (h o) -> p h o", o=1).broadcast_to([P, SWH, width])

                V.tensor_tensor(ss[:, :, 0:T], ss[:, :, 0:T], per_row(1, 0, T), ALU.subtract)
                V.tensor_tensor(ss[:, :, T:384], ss[:, :, T:384], per_row(1, 8, P), ALU.subtract).then_inc(ss_ready, 1)
                dve.wait_ge(ps7_full, ps70 + PS7_PV + 1)
                V.tensor_copy(og[:, :, :], pair2(ps7[:, :])).then_inc(ps7_free, 1)
                dve.wait_ge(group_evac, gm + 8)
                at = {}
                for tap in range(TAPS):
                    for f in range(2):
                        acc, src, w = yc[tap % 2][:, f, :], up[:, f, tap:tap + T], vec("conv_w", 2 * tap + f)
                        if tap == 0:
                            ins = V.tensor_scalar(acc, src, w, vec("conv_b", f), ALU.mult, ALU.add)
                        elif tap == 1:
                            ins = V.tensor_scalar(acc, src, w, None, ALU.mult)
                        else:
                            dve.wait_ge(dve_chain, at[tap - 2, f])
                            ins = V.scalar_tensor_tensor(out=acc, in0=src, scalar=w, in1=acc, op0=ALU.mult, op1=ALU.add)
                        at[tap, f] = mark(ins)
                dve.wait_ge(ss_exp, l + 1)
                V.tensor_reduce(mx[:, 0, 0:8], ss[:, :, 0:T], AX, ALU.add)
                link(V.tensor_reduce(mx[:, 0, 8:16], ss[:, :, T:384], AX, ALU.add))
                link(V.tensor_tensor(mx[:, 0, :], mx[:, 0, :], mx[:, 2, :], ALU.add))
                link(V.reciprocal(mx[:, 3, :], mx[:, 0, :]))
                V.tensor_tensor(ss[:, :, 0:T], ss[:, :, 0:T], per_row(3, 0, T), ALU.mult)
                V.tensor_tensor(ss[:, :, T:384], ss[:, :, T:384], per_row(3, 8, P), ALU.mult).then_inc(p_ready, 1)
                dve.wait_ge(stat_full, st0 + ST_GLA + 1)
                V.tensor_scalar(var8[:, :], ps7[:, 0:8], RMS_EPS, None, ALU.add).then_inc(var8_ready, 1)
                V.tensor_tensor(yc[0][:, :, :], yc[0][:, :, :], yc[1][:, :, :], ALU.add).then_inc(yc_ready, 1)
                dve.wait_ge(ps7_full, ps70 + PS7_GBC + 1)
                for f in range(2):
                    ins = V.scalar_tensor_tensor(out=og[:, f, :], in0=og[:, f, :], scalar=vec("gla_g", f),
                                                 in1=ps7[:, f * T:f * T + T], op0=ALU.mult, op1=ALU.mult)
                ins.then_inc(ps7_free, 1)
                dve.wait_ge(ps7_free, ps70 + PS7_GBC + 1)
                dve.wait_ge(group_evac, gm + 9)
                V.scalar_tensor_tensor(out=hn[:, 0:2, :], in0=og[:, :, :], scalar=0.5, in1=gr[:, :, :],
                                       op0=ALU.mult, op1=ALU.mult).then_inc(op_ready, 1)
                dve.wait_ge(stat_full, st0 + ST_CMEAN + 1)
                V.tensor_copy(var8[:, 0:2], ps7[:, 0:2]).then_inc(mean_ready, 1)
                operand_lo(b_lo[:, 0:2, :], hn[:, 0:2, :], b_hi[:, 0:2, :])

                def over_tiles2(ap):
                    return ap.rearrange("p (o n) -> p o n", o=1).broadcast_to([P, 2, T])

                dve.wait_ge(ps7_full, ps70 + PS7_CMEAN + 1)
                dve.wait_ge(yc_ready, l + 1)
                V.tensor_tensor(yc[0][:, :, :], yc[0][:, :, :], over_tiles2(ps7[:, T:2 * T]), ALU.subtract).then_inc(ps7_free, 1)
                dve.wait_ge(psm_full, psm0 + PSM_PV + 1)
                V.tensor_copy(hn[:, 4:6, :], pair2(psm[:, 0, :]))
                V.tensor_copy(hn[:, 6:8, :], pair2(psm[:, 1, :])).then_inc(psm_free, 1)
                dve.wait_ge(stat_full, st0 + ST_CVAR + 1)
                V.tensor_scalar(var8[:, 0:2], ps7[:, 0:2], LN_EPS, None, ALU.add).then_inc(var8_ready, 1)
                operand_lo(b_lo[:, 4:8, :], hn[:, 4:8, :], b_hi[:, 4:8, :])
                dve.wait_ge(ps7_full, ps70 + PS7_CVAR + 1)
                dve.wait_ge(ps7_free, ps70 + PS7_CMEAN + 1)
                for f in range(2):
                    ins = V.scalar_tensor_tensor(out=yc[0][:, f, :], in0=yc[0][:, f, :], scalar=vec("ln_g", f),
                                                 in1=ps7[:, T:2 * T], op0=ALU.mult, op1=ALU.mult)
                ins.then_inc(ps7_free, 1)
                dve.wait_ge(ps7_free, ps70 + PS7_CVAR + 1)
                for f in range(2):
                    ins = V.tensor_scalar(yc[0][:, f, :], yc[0][:, f, :], vec("ln_b", f), None, ALU.add)
                ins.then_inc(silu_in, 1)
                dve.wait_ge(silu_th, l + 1)
                link(V.scalar_tensor_tensor(out=yc[1][:, :, :], in0=th2[:, :, :], scalar=1.0, in1=yc[0][:, :, :],
                                            op0=ALU.add, op1=ALU.mult))
                V.tensor_scalar(hn[:, 2:4, :], yc[1][:, :, :], 0.5, None, ALU.mult).then_inc(op_ready, 1)
                operand_lo(b_lo[:, 2:4, :], hn[:, 2:4, :], b_hi[:, 2:4, :])
                for n in range(4):
                    lo(cm + 11 + n)
                    dve.wait_ge(unit_used, cm + 10 + n)
                    V.tensor_copy(hn[:, 2 * n:2 * n + 2, :],
                                  pair2(stream[(BANK_WOUT + n) % 3][:, :])).then_inc(group_evac, 1)
                dve.wait_ge(group_evac, g0 + GL_WOUT + 4)
                post_norm(st0 + ST_G3, ps70 + PS7_G3, group, 24, 1.0)
                dve.wait_ge(x_ready, KT * (3 * l + 3))
                pre_norm(st0 + ST_G4, ps70 + PS7_G4, group, 32)
                ffn(c0 + UL_UP_B, g0 + GL_UP_B, BANK_UP_B, h0 + NF2)
                post_norm(st0 + ST_G5, ps70 + PS7_G5, group, 40, 0.5)
            dve.wait_ge(psm_full, PSM_1 + PSM_L * LAYERS + 1)
            for n in range(4):
                ins = V.tensor_copy(hn[:, 2 * n:2 * n + 2, :], pair2(psm[:, n, :]))
            ins.then_inc(out_ready, 1)

        @block.tensor
        def _(pe):
            seen = {"sq": 0, "pow": 0}

            def mm(dst, lhs, rhs, start, stop):
                return nc.tensor.matmul(dst, lhs, rhs, start=start, stop=stop, skip_group_check=True)

            def split_unit(c, e=0):
                after(pe, w_split, c + 1, e * NS)

            def feature_major(s, dst, tiles, hi_t, lo_t, first, last, kts=range(KT), ready=None):
                for n, (lhs, at) in enumerate(tiles):
                    for k in kts:
                        if ready and n == 0:
                            ready(k)
                        to = dst[:, at:at + T]
                        begin, end = first and n == 0 and k == kts[0], last and n == len(tiles) - 1 and k == kts[-1]
                        mm(to, lhs(w_hi[s], k), hi_t[:, k, :], begin, False)
                        mm(to, lhs(w_hi[s], k), lo_t[:, k, :], False, False)
                        ins = mm(to, lhs(w_lo[s], k), hi_t[:, k, :], False, end)
                return ins

            def block_cols(f):
                return lambda w, k: w[:, k, f * P:f * P + P]

            BOTH = [(block_cols(0), 0), (block_cols(1), T)]

            def token_major(s, dst, col, width, at, begin):
                for t in range(TT):
                    to = dst[:, at + t * width:at + t * width + width]
                    tok = slice(t * P, t * P + P)
                    for k in range(KT):
                        w = slice(col, col + width)
                        mm(to, a_hi[:, k, tok], w_hi[s][:, k, w], begin and t == 0 and k == 0, False)
                        mm(to, a_lo[:, k, tok], w_hi[s][:, k, w], False, False)
                        ins = mm(to, a_hi[:, k, tok], w_lo[s][:, k, w], False, t == TT - 1 and k == KT - 1)
                return ins

            def bank_free(g, e3=0, back=2):
                after(pe, group_evac, g - back, e3)

            def a_ready(n):
                return lambda k: pe.wait_ge(a_split, KT * n + k + 1)

            def norm(st, p7):
                after(pe, ps7_free, p7)
                for k in range(KT):
                    seen["sq"] += 1
                    pe.wait_ge(sq_ready, seen["sq"])
                    for t in range(TT):
                        ins = mm(ps7[:, t:t + 1], sq[:, k, t * P:t * P + P], means[:, 0:1], k == 0 and t == 0,
                                 k == KT - 1 and t == TT - 1)
                ins.then_inc(stat_full, 1)
                seen["pow"] += 1
                pe.wait_ge(rstd_ready, seen["pow"])
                for t in range(TT):
                    ins = mm(ps7[:, T + t * P:T + t * P + P], rstd2[:, t:t + 1].broadcast_to([P, P]), ident, t == 0, t == 1)
                ins.then_inc(ps7_full, 1)

            pe.wait_ge(small_loaded, 16 * N_SMALL)
            pe.wait_ge(x_loaded, 16)
            pe.wait_ge(pool_init, 2)
            xin = hn[:, :, :].rearrange("p (t a) n -> p t (a n)", t=TT)
            for k in range(KT):
                for t in range(TT):
                    at = (k % 2) * T + t * P
                    ins = nc.tensor.transpose(psm[:, k // 2, at:at + P], xin[:, t, k * P:k * P + P], ident)
            ins.then_inc(psm_full, 1)
            staged = sq[:, 0:2, :].rearrange("p a (b c) -> p (a b) c", b=2)
            for n in range(4):
                ins = nc.tensor.transpose(ps7[:, n * P:n * P + P], staged[:, n, :], ident)
            ins.then_inc(ps7_full, 1)
            pe.wait_ge(ps7_free, PS7_VEC + 1)
            mm(ps7[:, 0:LAYERS * 16], ones_row[:, :], sink_row[:, :], True, True).then_inc(ps7_full, 1)
            norm(ST_N0, PS7_N0)

            def project(c, g, bank, hi_t, lo_t, ready=None):
                split_unit(c)
                bank_free(g)
                feature_major(c % NS, bank, BOTH[0:1], hi_t, lo_t, True, False, ready=ready)
                ins = feature_major(c % NS, bank, BOTH[1:2], hi_t, lo_t, False, True)
                ins.then_inc(unit_used, 1)

            for u in range(8):
                if u < 4:
                    project(u, u, stream[u % 3], a_hi, a_lo, a_ready(0) if u == 0 else None)
                else:
                    split_unit(u)
                    bank_free(u)
                    token_major(u % NS, stream[u % 3], 0, UC, 0, True).then_inc(unit_used, 1)
            for u in range(8, 20):
                project(u, u, stream[u % 3], a_hi, a_lo)
                if u == 9:
                    pe.wait_ge(rot_done, 1)
                    pe.wait_ge(psm_free, PSM_SC)
                    for h in range(HEADS):
                        mm(psm[:, h, 0:T], qk_rot[:, 4 + h, 0:P], qk_rot[:, h, :], True, False)
                        ins = mm(psm[:, h, T:384], qk_rot[:, 4 + h, P:T], qk_rot[:, h, P:T], False, True)
                    ins.then_inc(psm_full, 1)
                if u == 11:
                    pe.wait_ge(psm_free, PSM_O)
                    for h in range(HEADS):
                        for d in range(2):
                            v = slice(h * DV + d * P, h * DV + d * P + P)
                            mm(psm[:, h, d * T:d * T + T], v_ret[:, 0, v], st_ret[:, 384 * h:384 * h + T], d == 0, False)
                            ins = mm(psm[:, h, d * T + P:d * T + T], v_ret[:, 1, v], st_ret[:, 384 * h + T:384 * h + 384],
                                     False, d == 1)
                    ins.then_inc(psm_full, 1)
                if u in (13, 16):
                    pe.wait_ge(psm_free, PSM_O + 1)
                    if u == 16:
                        pe.wait_ge(o_sq, 1)
                    src = o_ret if u == 13 else sq
                    after(pe, ps7_free, PS7_N1)
                    for t in range(TT):
                        for h in range(HEADS):
                            for d in range(2):
                                ins = mm(ps7[:, 4 * t + h:4 * t + h + 1], src[:, 2 * h + d, t * P:t * P + P], means[:, 1:2],
                                         t + h + d == 0, t == 1 and h == 3 and d == 1)
                    ins.then_inc(stat_full, 1)
                if u in (15, 17):
                    if u == 15:
                        pe.wait_ge(mean_ready, 1)
                    else:
                        pe.wait_ge(rstd8_ready, 1)
                    pe.wait_ge(psm_free, PSM_MEAN if u == 15 else PSM_VAR)
                    src = var8 if u == 15 else rstd8
                    for h in range(HEADS):
                        for t in range(TT):
                            at = (h % 2) * T + t * P
                            ins = mm(psm[:, h // 2, at:at + P], src[:, 4 * t + h:4 * t + h + 1].broadcast_to([P, P]), ident,
                                     h % 2 == 0 and t == 0, h % 2 == 1 and t == 1)
                    ins.then_inc(psm_full, 1)
            pe.wait_ge(op_split, 1)
            for m in range(2):
                c = U1_RG + m
                split_unit(c)
                for n in range(4):
                    g = G1_RG + 4 * m + n
                    bank_free(g)
                    ins = feature_major(c % NS, stream[g % 3], BOTH, b_hi, b_lo, True, True, kts=(2 * n, 2 * n + 1))
                    if n < 3:
                        ins.then_inc(rg_done, 1)
                ins.then_inc(unit_used, 1)
            for n in range(8):
                project(U1_GATES + n, G1_GATES + n, stream[(G1_GATES + n) % 3], a_hi, a_lo)
            pe.wait_ge(op_split, 2)
            for n in range(4):
                project(U1_RETO + n, G1_RETO + n, stream[(G1_RETO + n) % 3], b_hi, b_lo)
            pe.wait_ge(op_split, 3)
            for n in range(4):
                project(U1_LRUO + n, G1_LRUO + n, stream[(G1_LRUO + n) % 3], a_hi, a_lo)
            for n in range(4):
                project(U1_OUT + n, G1_OUT + n, stream[(G1_OUT + n) % 3], b_hi, b_lo,
                        (lambda k: pe.wait_ge(op_split, 4 + k // 2)) if n == 0 else None)
            norm(ST_N1, PS7_N1)

            def hidden(c, e, g, e3, bank, ready=None):
                split_unit(c, e)
                bank_free(g, e3)
                feature_major(c % NS, bank, BOTH[0:1], a_hi, a_lo, True, False, ready=ready)
                ins = feature_major(c % NS, bank, BOTH[1:2], a_hi, a_lo, False, True)
                ins.then_inc(unit_used, 1)

            def down(c, g, nf):
                with pe.Fori(0, 2) as i:
                    for j in range(6):
                        n, m = j // 3, j % 3
                        split_unit(c + j, i * 2)
                        if m == 0:
                            bank_free(g + n, i * 2, back=1)
                        k0 = KT * m
                        kts = range(min(KT, nf - k0))
                        hi_t, lo_t = h_hi[:, k0:k0 + len(kts), :], h_lo[:, k0:k0 + len(kts), :]
                        ins = feature_major((c + j) % NS, psm[:, n, :], BOTH, hi_t, lo_t, m == 0, m == 2, kts=kts)
                        ins.then_inc(unit_used, 1)

            for j in range(3):
                hidden(U1_UP + j, 0, G1_UP + j, 0, stream[j % 3], a_ready(1) if j == 0 else None)
            with pe.Fori(1, NF1 // 3) as i:
                for j in range(3):
                    hidden(U1_UP + j, i, G1_UP + j, i * 3, stream[j % 3])
            pe.wait_ge(h_split, NF1)
            down(U1_DOWN, G1_DOWN, NF1)
            norm(ST_NF, PS7_NF)

            def ffn(c, g, bank0, norm_no, h_done):
                hidden(c, 0, g, 0, stream[bank0], a_ready(norm_no))
                with pe.Fori(0, (NF2 - 1) // 3) as i:
                    for j in range(1, 4):
                        hidden(c + j, i, g + j, i * 3, stream[(bank0 + j) % 3])
                pe.wait_ge(h_split, h_done)
                down(c + NF2, g + NF2, NF2)

            for l in range(LAYERS):
                c0, g0 = U1_END + UL * l, G1_END + GL * l
                psm0, ps70, st0 = PSM_1 + PSM_L * l, PS7_1 + PS7_L * l, ST_1 + ST_L * l
                norm(st0 + ST_G0, ps70 + PS7_G0)
                ffn(c0, g0, 0, 2 + 3 * l, NF1 + NF2 * (2 * l + 1))
                norm(st0 + ST_G1, ps70 + PS7_G1)
                norm(st0 + ST_G2, ps70 + PS7_G2)
                cm, gm = c0 + UL_MIX, g0 + GL_MIX

                def bank(n):
                    return stream[(BANK_MIX + n) % 3]

                def psm_ready(n):
                    pe.wait_ge(psm_free, psm0 + n)

                def cols(tile, n):
                    return tile[:, n * P:n * P + P]

                split_unit(cm)
                bank_free(gm)
                feature_major(cm % NS, bank(0), BOTH[0:1], a_hi, a_lo, True, True, ready=a_ready(3 + 3 * l)).then_inc(unit_used, 1)
                project(cm + 1, gm + 1, bank(1), a_hi, a_lo)
                pe.wait_ge(group_evac, gm + 1)
                pe.wait_ge(ps7_free, ps70 + PS7_Z)
                for t in range(TT):
                    ins = mm(cols(ps7, t), cols(glr_t[0:17, :], t), w2aug[:, l, :], t == 0, t == 1)
                ins.then_inc(ps7_full, 1)
                split_unit(cm + 2)
                bank_free(gm + 2)
                token_major((cm + 2) % NS, bank(2), 0, 256, 0, True).then_inc(unit_used, 1)
                split_unit(cm + 3)
                bank_free(gm + 3)
                feature_major((cm + 3) % NS, bank(3), BOTH[0:1], a_hi, a_lo, True, False)
                token_major((cm + 3) % NS, bank(3), P, P, T, False).then_inc(unit_used, 1)
                pe.wait_ge(glog_ready, l + 1)
                psm_ready(PSM_LEV)
                lev = const("lev")
                for t in range(TT):
                    g_t = cols(lg[:, 1, :], t)
                    mm(psm[:, 2 * t, :], g_t, lev[:, 0:4 * P], True, True)
                    mm(psm[:, 2 * t + 1, 0:3 * P], g_t, lev[:, 4 * P:7 * P], True, False)
                    ins = mm(psm[:, 2 * t + 1, 3 * P:4 * P], g_t, cols(lev, 7 + t), False, True)
                ins.then_inc(psm_full, 1)

                def head(tile, h):
                    return tile[GDK * h:GDK * h + GDK]

                def gla_scores(n):
                    t = n // 2
                    psm_ready(PSM_GLA + n)
                    pe.wait_ge(ke_ready, TT * l + t + 1)
                    for m in range(4):
                        level = 4 * (n % 2) + m
                        for h in range(GH):
                            if level < LEV - 1:
                                k_t, q_t = head(ek[:, 1, t, level, :], h), head(qe[:, t, level, :], h)
                            else:
                                k_t, q_t = head(cols(kg, t), h), head(cols(qg, t), h)
                            ins = mm(psm[:, h, m * P:m * P + P], k_t, q_t, m == 0, m == 3)
                    ins.then_inc(psm_full, 1)

                for n in range(2):
                    split_unit(cm + 4 + n)
                    bank_free(gm + 4 + n)
                    feature_major((cm + 4 + n) % NS, bank(4 + n), BOTH, a_hi, a_lo, True, True).then_inc(unit_used, 1)
                    gla_scores(n)
                for n in range(3):
                    project(cm + 6 + n, gm + 6 + n, bank(6 + n), a_hi, a_lo)
                    if n < 2:
                        gla_scores(2 + n)
                psm_ready(PSM_CROSS)
                for h in range(GH):
                    ins = mm(psm[:, h, 0:P], head(ek[:, 1, 0, LEV - 1, :], h), head(qe[:, 1, LEV - 1, :], h), True, True)
                ins.then_inc(psm_full, 1)

                def window_scores(b):
                    psm_ready(PSM_SWA + b)
                    for n in range(4):
                        half, j = n % 2, 2 * b + n // 2
                        part = slice(SWD * half, SWD * half + SWD)
                        mm(psm[:, n, 0:T], qs[part, j, P:T], ks[part, :], True, False)
                        ins = mm(psm[:, n, T:384], qs[part, j, 0:P], ks[part, 0:P], False, True)
                    ins.then_inc(psm_full, 1)

                window_scores(0)
                pe.wait_ge(ps7_free, ps70 + PS7_PV)
                for h in range(GH):
                    part, f = slice(GDV * (h % 2), GDV * (h % 2) + GDV), h // 2
                    v = slice(GDV * h, GDV * h + GDV)
                    mm(ps7[part, f * T:f * T + P], vg[:, 0, v], s_gla[:, 0, h, :], f == 0, False)
                    mm(ps7[part, f * T + P:f * T + T], vg[:, 1, v], s_gla[:, 1, h, :], False, False)
                    ins = mm(ps7[part, f * T + P:f * T + T], vg[:, 0, v], s_cross[:, h, :], False, f == 1)
                ins.then_inc(ps7_full, 1)
                window_scores(1)
                pe.wait_ge(og_sq, l + 1)
                pe.wait_ge(ps7_free, ps70 + PS7_GBC)
                for t in range(TT):
                    for f in range(2):
                        at = 4 * t + 2 * f
                        ins = mm(ps7[:, at:at + 2], cols(sq2[:, f, :], t), headsel, at == 0, at == 6)
                ins.then_inc(stat_full, 1)
                pe.wait_ge(p_ready, l + 1)
                psm_ready(PSM_PT)
                for n in range(16):
                    ins = nc.tensor.transpose(cols(psm[:, n // 4, :], n % 4), cols(ss[:, n // 2, 0:T], n % 2), ident)
                ins.then_inc(psm_full, 1)
                psm_ready(PSM_PT + 1)
                for n in range(8):
                    ins = nc.tensor.transpose(cols(psm[:, n // 4, :], n % 4), ss[:, n, T:384], ident)
                ins.then_inc(psm_full, 1)
                pe.wait_ge(rstd8_ready, 2 * l + 2)
                for f in range(2):
                    for t in range(TT):
                        for h in range(2):
                            at, part = 4 * t + 2 * f + h, slice(GDV * h, GDV * h + GDV)
                            ins = mm(cols(ps7[part, :], TT * f + t), rstd8[:, at:at + 1].broadcast_to([P, GDV]), ident,
                                     f + t == 0, f + t == 2)
                ins.then_inc(ps7_full, 1)
                psm_ready(PSM_PV)
                for h in range(SWH):
                    f, part = h // 2, slice(SWD * (h % 2), SWD * (h % 2) + SWD)
                    half, j = h // 4, h % 4
                    slot = 4 * (j // 2) + 2 * (j % 2) + half
                    at = (f % 2) * T
                    v = slice(SWD * half, SWD * half + SWD)
                    mm(psm[part, f // 2, at:at + P], vs[:, 0, v], pt[:, 16 + slot, :], f % 2 == 0, False)
                    for t in range(TT):
                        ins = mm(psm[part, f // 2, at + P:at + T], vs[:, t, v], pt[:, 2 * slot + t, :], False,
                                 f % 2 == 1 and t == 1)
                ins.then_inc(psm_full, 1)
                for n in range(2):
                    pe.wait_ge(ps7_free, ps70 + PS7_CMEAN + n)
                    if n == 0:
                        pe.wait_ge(yc_ready, l + 1)
                    else:
                        pe.wait_ge(yc_sq, l + 1)
                    src = yc[0] if n == 0 else sq2
                    for t in range(TT):
                        for f in range(2):
                            ins = mm(ps7[:, t:t + 1], cols(src[:, f, :], t), means[:, 1:2], t + f == 0, t + f == 2)
                    ins.then_inc(stat_full, 1)
                    if n == 0:
                        pe.wait_ge(mean_ready, l + 2)
                    else:
                        pe.wait_ge(rstd8_ready, 2 * l + 3)
                    per = var8 if n == 0 else rstd8
                    for t in range(TT):
                        ins = mm(ps7[:, T + t * P:T + t * P + P], per[:, t:t + 1].broadcast_to([P, P]), ident, t == 0, t == 1)
                    ins.then_inc(ps7_full, 1)
                pe.wait_ge(op_split, 7 + 3 * l + 3)
                for n in range(4):
                    project(cm + 9 + n, g0 + GL_WOUT + n, stream[(BANK_WOUT + n) % 3], b_hi, b_lo)
                norm(st0 + ST_G3, ps70 + PS7_G3)
                norm(st0 + ST_G4, ps70 + PS7_G4)
                ffn(c0 + UL_UP_B, g0 + GL_UP_B, BANK_UP_B, 4 + 3 * l, NF1 + NF2 * (2 * l + 2))
                norm(st0 + ST_G5, ps70 + PS7_G5)
            pe.wait_ge(x_ready, KT * (3 * LAYERS + 1))
            pe.wait_ge(psm_free, PSM_1 + PSM_L * LAYERS)
            for t in range(TT):
                for k in range(KT):
                    n = KT * t + k
                    ins = nc.tensor.transpose(psm[:, n // 4, (n % 4) * P:(n % 4) * P + P], x[:, k, t * P:t * P + P], ident)
            ins.then_inc(psm_full, 1)


def kernel(**inputs):
    import concourse.bacc as bacc
    from concourse.bass_utils import run_bass_kernel_spmd as run

    def rows(name, *index):
        return np.asarray(inputs[name])[index].reshape(-1, P)

    vec_rows = np.zeros((P, 4, VCOL), np.float32)
    for name, src in (("norm1", "norm1_w"), ("gate_b", "merge_gate_b"), ("gn", "ret_gn_w"), ("lconv_w", "lru_conv_w"),
                      ("lconv_b", "lru_conv_b"), ("b_r", "lru_b_r"), ("b_i", "lru_b_i"), ("lam", "lru_lambda"),
                      ("norm2", "norm2_w"), ("norm_f", "norm_f_w")):
        r = rows(src)
        vec_rows[V1[name]:V1[name] + len(r), 0] = r
    for name, src in (("fconv_w", "ffn_conv_w"), ("fconv_b", "ffn_conv_b")):
        r = rows(src)
        vec_rows[V1B[name]:V1B[name] + len(r), 1] = r
    for l in range(LAYERS):
        for name, src in (("norm", "norm_g_2"), ("conv_w", "conv_w_2"), ("conv_b", "conv_b_2"), ("ln_g", "conv_ln_g_2"),
                          ("ln_b", "conv_ln_b_2"), ("gla_g", "gla_norm_g_2")):
            r = rows(src, l)
            vec_rows[VL[name]:VL[name] + len(r), 2 + l] = r
    gate2 = np.concatenate([np.asarray(inputs["gla_w_gate2_2"]), np.asarray(inputs["gla_b_gate_2"])[:, None]], axis=1)
    sink = np.asarray(inputs["swa_sinks_2"]).reshape(LAYERS, 2, 2, 2).transpose(0, 2, 3, 1).reshape(LAYERS, 1, 8)
    sent = {
        "table": TABLE, "masks": MASKS, "vec_rows": vec_rows.reshape(P, -1),
        "gate2": np.ascontiguousarray(gate2.transpose(1, 0, 2)).reshape(17, -1),
        "sink_row": np.ascontiguousarray(np.concatenate([sink, sink], axis=1)).reshape(1, -1),
    }
    for name in ("x", "positions", "w_in", "w_ret_o", "lru_w_r", "lru_w_i", "w_lru_o", "w_out", "ffn_w_up", "ffn_w_down",
                 "ffn_w_gate_2", "ffn_w_up_2", "ffn_w_down_2", "w_in_2", "w_out_2"):
        sent[name] = np.ascontiguousarray(inputs[name])
    nc = bacc.Bacc("TRN2", target_bir_lowering=False, num_devices=1)
    io = {name: nc.dram_tensor(f"in_{name}", a.shape, mybir.dt.from_np(a.dtype), kind="ExternalInput").ap()
          for name, a in sent.items()}
    out = nc.dram_tensor("out", (1, T, D), F32, kind="ExternalOutput").ap()
    build(nc, io, out)
    result = run(nc, [{f"in_{name}": a for name, a in sent.items()}], core_ids=[0])
    return result.results[0]["out"]
```

```python
from contextlib import ExitStack

import numpy as np
import concourse.bass as bass
from concourse import mybir

F32 = mybir.dt.float32
F32R = mybir.dt.float32r
I32 = mybir.dt.int32
U8 = mybir.dt.uint8
ACT = mybir.ActivationFunctionType
ALU = mybir.AluOpType
AX = mybir.AxisListType.X

P = 128
T = 256
TT = T // P
D = 1024
KT = D // P
UC = 256
FT = UC // P
NS = 3
HEADS, DK, DV, CH = 4, 128, 256, 64
DFF1, DFF2 = 3072, 2816
NF1, NF2 = DFF1 // P, DFF2 // P
DIN2 = 2064
LAYERS = 2
SWH, SWD = 8, 64
GH, GDK, GDV = 4, 32, 64
TAPS = 31
LEV = 8
RMS_EPS = 1e-6
LN_EPS = 1e-5
SQ2PI = 0.7978845608028654
GELU_C = 0.044715
MAGIC = 12582912.0

UNITS_IN1 = 28
U1_RG = 20
U1_GATES = 22
U1_RETO = 30
U1_LRUO = 34
U1_OUT = 38
U1_UP = 42
U1_DOWN = U1_UP + NF1
U1_END = U1_DOWN + 12
UL_DOWN_A = NF2
UL_MIX = NF2 + 12
UL_WOUT = UL_MIX + 9
UL_UP_B = UL_WOUT + 4
UL_DOWN_B = UL_UP_B + NF2
UL = UL_DOWN_B + 12
G1_RG = 20
G1_GATES = 28
G1_RETO = 36
G1_LRUO = 40
G1_OUT = 44
G1_UP = 48
G1_DOWN = G1_UP + NF1
G1_END = G1_DOWN + 4
GL_DOWN_A = NF2
GL_MIX = NF2 + 4
GL_WOUT = GL_MIX + 9
GL_UP_B = GL_WOUT + 4
GL_DOWN_B = GL_UP_B + NF2
GL = GL_DOWN_B + 4
TOTAL_UNITS = U1_END + LAYERS * UL
QUERY_UNITS = [U1_END + UL * l + UL_MIX + 5 + n for l in range(LAYERS) for n in range(2)]

PSM_X, PSM_SC, PSM_O, PSM_MEAN, PSM_VAR, PSM_1 = range(6)
(PSM_SWA, PSM_GLA, PSM_CROSS, PSM_L) = (0, 2, 10, 11)
PS7_VEC, PS7_SINK, PS7_N0, PS7_N1, PS7_NF, PS7_1 = range(6)
(PS7_G0, PS7_G1, PS7_G2, PS7_Z, PS7_PV, PS7_GBC, PS7_G3, PS7_G4, PS7_G5, PS7_L) = range(10)
ST_N0, ST_RMEAN, ST_RVAR, ST_N1, ST_NF, ST_1 = range(6)
(ST_G0, ST_G1, ST_G2, ST_GLA, ST_CVAR, ST_G3, ST_G4, ST_G5, ST_L) = range(9)
BANK_MIX, BANK_WOUT, BANK_UP_B = NF2 % 3, (NF2 + 9) % 3, (NF2 + 13) % 3

VCOL = 128
V1 = {"norm1": 0, "gate_b": 8, "gn": 24, "lconv_w": 32, "lconv_b": 64, "b_r": 72, "b_i": 80, "lam": 88,
      "norm2": 96, "norm_f": 104}
V1B = {"fconv_w": 0, "fconv_b": 72}
VL = {"norm": 0, "conv_w": 48, "conv_b": 110, "ln_g": 112, "ln_b": 114, "gla_g": 116}


def tables():
    t = {}
    a = np.arange(P)
    t["ident"] = np.eye(P)
    t["means"] = np.stack([np.full(P, 1 / D), np.full(P, 1 / 256)], axis=1)
    t["headsel"] = np.stack([a < 64, a >= 64], axis=1) / 64.0
    t["invf"] = np.power(np.float32(10000.0), -(a % 64).astype(np.float32) / np.float32(64))[:, None]
    t["sgn"] = np.where(a < 64, -1.0, 1.0)[:, None]
    lev = np.zeros((9, P, P))
    mask = np.zeros((LEV, P, P))
    for n in range(LEV - 1):
        m = P >> n
        mid = (a // m) * m + m // 2 - 1
        after = (a[:, None] > mid[None, :]) & (a[:, None] <= a[None, :])
        before = (a[:, None] > a[None, :]) & (a[:, None] <= mid[None, :])
        lev[n] = after | before
        mask[n] = ((a[:, None] // m) == (a[None, :] // m)) & (a[:, None] <= mid[None, :]) & (a[None, :] > mid[None, :])
    lev[7] = a[:, None] > a[None, :]
    lev[8] = a[:, None] <= a[None, :]
    mask[LEV - 1] = np.eye(P)
    t["lev"] = (lev / 16.0).transpose(1, 0, 2).reshape(P, -1)
    d = a[:, None] - np.arange(T)[None, :] + P
    alibi = np.where((d >= 0) & (d < P), -d, -1e30)
    t["alibi"] = np.concatenate([alibi, alibi[:, P:]], axis=1)
    i = np.arange(T)
    log_gamma = np.log1p(-np.power(2.0, -5.0 - np.arange(HEADS)))
    seen = (i[:, None] // CH) <= (i[None, :] // CH)
    dec = np.exp(log_gamma[:, None, None] * np.abs(i[:, None] - i[None, :])) * seen * DK ** -0.5
    t["ret"] = np.concatenate([dec[:, :P, :], dec[:, P:, P:]], axis=2).transpose(1, 0, 2).reshape(P, -1)
    names, at, parts = {}, 0, []
    for k, v in t.items():
        names[k] = (at, at + v.shape[1])
        at += v.shape[1]
        parts.append(v.astype(np.float32))
    return names, np.concatenate(parts, axis=1), mask.transpose(1, 0, 2).reshape(P, -1).astype(np.float32)


COLS, TABLE, MASKS = tables()
NKEEP = COLS["alibi"][1]


def after(eng, s, n, e=0):
    if not isinstance(e, int):
        eng.wait_ge(s, e + n)
    elif n + e > 0:
        eng.wait_ge(s, n + e)


def build(nc, io, out):
    with ExitStack() as ctx:
        def sb(name, shape, dt=F32, scope=ctx):
            return scope.enter_context(nc.sbuf_tensor(name, shape, dt))

        def sem(name):
            return ctx.enter_context(nc.semaphore(name))

        x = sb("x", [P, KT, T])
        hn = sb("hn", [P, KT, T])
        sq = sb("sq", [P, KT, T])
        a_hi, a_lo = sb("a_hi", [P, KT, T], F32R), sb("a_lo", [P, KT, T], F32R)
        b_hi, b_lo = sb("b_hi", [P, KT, T], F32R), sb("b_lo", [P, KT, T], F32R)
        raw = [sb(f"raw{s}", [P, KT, UC]) for s in range(NS)]
        w_hi = [sb(f"w_hi{s}", [P, KT, UC], F32R) for s in range(NS)]
        w_lo = [sb(f"w_lo{s}", [P, KT, UC], F32R) for s in range(NS)]
        keep = sb("keep", [P, NKEEP])

        def const(name):
            return keep[:, COLS[name][0]:COLS[name][1]]

        ident, means, headsel = const("ident"), const("means"), const("headsel")
        masks = sb("masks", [P, LEV, P], U8)
        vecs = sb("vecs", [P, 4, VCOL])
        var2, rstd2 = sb("var2", [P, 2]), sb("rstd2", [P, 2])
        var8, rstd8 = sb("var8", [P, 8]), sb("rstd8", [P, 8])
        rb = sb("rb", [P, T])
        mhalf = sb("mhalf", [P, 1])
        ones_row = sb("ones_row", [1, P])
        sink_row = sb("sink_row", [1, LAYERS * 16])
        sinks = sb("sinks", [P, LAYERS, 16])
        glr_t = sb("glr_t", [32, T])
        w2aug = sb("w2aug", [17, LAYERS, P])

        m1 = ExitStack()
        ret_d = sb("ret_d", [P, HEADS, 384], scope=m1)
        cos2, sin2 = sb("cos2", [P, T], scope=m1), sb("sin2", [P, T], scope=m1)
        e_xl = sb("e_xl", [P, KT, T + 3], scope=m1)
        e2, e3, e4, e5, e6, e7 = (sb(f"e{n}", [P, KT, T], scope=m1) for n in range(2, 8))
        half_b = sb("half_b", [P, 40], scope=m1)
        sp4 = sb("sp4", [P, 8], scope=m1)
        sp_t = sb("sp_t", [P, 6, 8], scope=m1)
        m1.close()
        qk_raw, qk_sw, qk_rot = e_xl[:, :, 0:T], e2, e3
        xl, xc, la = e_xl, e2, e_xl[:, :, 3:T + 3]
        o_ret, g_ret, y_lru, i_gate = e5, e6, e7, e3
        tmp, ga, gb, gel, a_lru = e5, e4, hn, hn, sq
        v_ret = e4[:, :, :].rearrange("p (t a) n -> p t (a n)", t=TT)
        st_ret = sq[:, :, :].rearrange("p a b -> p (a b)")
        masks_f32 = e7[:, 0:4, :].rearrange("p k n -> p (k n)")
        pos_i, ang_t, ang = e4[:, 0, :].bitcast(I32), e5, e6

        ff = ExitStack()
        h_hi, h_lo = sb("h_hi", [P, NF1, T], F32R, scope=ff), sb("h_lo", [P, NF1, T], F32R, scope=ff)
        th, hb, ab = (sb(n, [P, NS, T], scope=ff) for n in ("th", "hb", "ab"))
        gu = sb("gu", [P, NS, 2, T], scope=ff)
        ff.close()

        m2 = ExitStack()
        ek = sb("ek", [P, 2, TT, LEV, P], scope=m2)
        qg, kg = sb("qg", [P, T], scope=m2), sb("kg", [P, T], scope=m2)
        vg = sb("vg", [P, TT, 256], scope=m2)
        s_gla = sb("s_gla", [P, TT, GH, P], scope=m2)
        s_cross = sb("s_cross", [P, GH, P], scope=m2)
        pt = sb("pt", [P, 24, P], scope=m2)
        vs = sb("vs", [P, TT, P], scope=m2)
        ss = sb("ss", [P, SWH, 384], scope=m2)
        mx = sb("mx", [P, 4, 16], scope=m2)
        up = sb("up", [P, 2, T + TAPS - 1], scope=m2)
        yc = [sb(f"yc{n}", [P, 2, T], scope=m2) for n in range(2)]
        gr, og, th2, sq2 = (sb(n, [P, 2, T], scope=m2) for n in ("gr", "og", "th2", "sq2"))
        m2.close()
        cg, cub = gu[:, :, 0, :], gu[:, :, 1, :]
        qe = sq[:, :, :].rearrange("p (t a) (b i) -> p t (a b) i", t=TT, b=2)
        lg, qs, ca, ks = (pt[:, a:a + 2 * n, :].rearrange("p (n b) i -> p n (b i)", b=2)
                          for a, n in ((0, 5), (10, 4), (18, 2), (22, 1)))
        ks = ks[:, 0, :]

        stream = [ctx.enter_context(nc.psum_tensor(f"stream{n}", [P, 512], F32)) for n in range(3)]
        psm = ctx.enter_context(nc.psum_tensor("psm", [P, 4, 512], F32))
        ps7 = ctx.enter_context(nc.psum_tensor("ps7", [P, 512], F32))

        raw_loaded = [sem(f"raw_loaded{s}") for s in range(NS)]
        w_hi_ready, w_split, unit_used = sem("w_hi_ready"), sem("w_split"), sem("unit_used")
        rg_done, group_evac = sem("rg_done"), sem("group_evac")
        psm_full, psm_free, ps7_full, ps7_free, stat_full = (sem(n) for n in (
            "psm_full", "psm_free", "ps7_full", "ps7_free", "stat_full"))
        x_loaded, small_loaded, out_ready, out_stored = (sem(n) for n in (
            "x_loaded", "small_loaded", "out_ready", "out_stored"))
        pool_init, dve_chain, act_chain = sem("pool_init"), sem("dve_chain"), sem("act_chain")
        sq_sum, hb_ready = sem("sq_sum"), sem("hb_ready")
        x_ready, sq_ready, var_ready, rstd_ready, normed, a_hi_ready, a_split = (sem(n) for n in (
            "x_ready", "sq_ready", "var_ready", "rstd_ready", "normed", "a_hi_ready", "a_split"))
        mean_ready, var8_ready, rstd8_ready = sem("mean_ready"), sem("var8_ready"), sem("rstd8_ready")
        op_ready, op_hi_ready, op_split = sem("op_ready"), sem("op_hi_ready"), sem("op_split")
        th_ready, h_hi_ready, h_split, tap_ready, conv_done, csq_ready, cube_ready = (sem(n) for n in (
            "th_ready", "h_hi_ready", "h_split", "tap_ready", "conv_done", "csq_ready", "cube_ready"))
        ang_ready, trig_ready, swapped, rot_done, act_gate, lam_arg, lam_exp, lru_conv0, lru_act = (sem(n) for n in (
            "ang_ready", "trig_ready", "swapped", "rot_done", "act_gate", "lam_arg", "lam_exp", "lru_conv0", "lru_act"))
        o_sq, ge_sq, ge_cube, ge_th, ge_done, v_ready, sqrt_done = (sem(n) for n in (
            "o_sq", "ge_sq", "ge_cube", "ge_th", "ge_done", "v_ready", "sqrt_done"))
        ez_ready, glog_ready, lev_ready, e_ready, qe_ready, ke_ready, zeroed, gate_ready, sums_ready, pv_full, pt_full, pt_free = (sem(n) for n in (
            "ez_ready", "glog_ready", "lev_ready", "e_ready", "qe_ready", "ke_ready", "zeroed", "gate_ready", "sums_ready", "pv_full",
            "pt_full", "pt_free"))
        conv_full, centred, centred_var, conv_rstd = (sem(n) for n in (
            "conv_full", "centred", "centred_var", "conv_rstd"))
        og_sq, yc_ready, yc_sq, silu_in, silu_th, ss_ready, ss_exp, p_ready = (sem(n) for n in (
            "og_sq", "yc_ready", "yc_sq", "silu_in", "silu_th", "ss_ready", "ss_exp", "p_ready"))
        N_SMALL = 7

        def rows(ap, r0=0, n=KT):
            return ap[r0:r0 + n * P, :].rearrange("(k p) n -> p k n", p=P)

        def pair2(bank):
            return bank.rearrange("p (a b) -> p a b", a=2)

        block = ctx.enter_context(nc.Block())

        @block.sync
        def _(sp):
            def fill(c, e, halves):
                s = c % NS
                if not (isinstance(e, int) and c + NS * e < NS):
                    after(sp, w_split, c - NS + 1, e * NS)
                for dst, src in halves(raw[s]):
                    sp.dma_start(dst, src).then_inc(raw_loaded[s], 16)

            def plain(src, n=KT):
                return lambda r: [(r[:, 0:4, :], src[:, 0:4, :]), (r[:, 4:n, :], src[:, 4:n, :])]

            def pair(first, second):
                return lambda r: [(r[:, :, 0:P], first), (r[:, :, P:UC], second)]

            def interleaved(first, second):
                return lambda r: [(r[:, :, SWD * (2 * j + g):SWD * (2 * j + g) + SWD], src[:, :, SWD * j:SWD * j + SWD])
                                  for j in range(2) for g, src in enumerate((first, second))]

            sp.dma_start(hn[:, :, :].rearrange("p (t a) n -> p t (a n)", t=TT),
                         io["x"][0].rearrange("(t p) d -> p t d", p=P)).then_inc(x_loaded, 16)
            w_in = rows(io["w_in"][0])
            cols = [at + UC * i for at, m in ((0, 2), (512, 2), (1024, 4), (3072, 4), (4096, 4), (2048, 4))
                    for i in range(m)]
            c = 0
            for col in cols:
                fill(c, 0, plain(w_in[:, :, col:col + UC]))
                c += 1
            for name in ("lru_w_r", "lru_w_i"):
                fill(c, 0, plain(io[name][0].rearrange("b (k p) n -> p (b k) n", p=P)))
                c += 1
            for i in range(8):
                fill(c, 0, plain(w_in[:, :, 5120 + UC * i:5120 + UC * i + UC]))
                c += 1
            for name in ("w_ret_o", "w_lru_o", "w_out"):
                for i in range(4):
                    fill(c, 0, plain(rows(io[name][0])[:, :, UC * i:UC * i + UC]))
                    c += 1
            w_up = rows(io["ffn_w_up"][0])
            with sp.Fori(0, NF1 // 3) as i:
                for j in range(3):
                    fill(U1_UP + j, i, pair(w_up[:, :, bass.ds(i * (3 * P) + j * P, P)],
                                            w_up[:, :, bass.ds(i * (3 * P) + (j * P + DFF1), P)]))
            with sp.Fori(0, 2) as i:
                for j in range(6):
                    src = rows(io["ffn_w_down"][0], KT * P * (j % 3))
                    fill(U1_DOWN + j, i * 2, plain(src[:, :, bass.ds(i * 512 + UC * (j // 3), UC)]))

            def ffn(c, l, f):
                g_rows, u_rows = rows(io["ffn_w_gate_2"][l, f]), rows(io["ffn_w_up_2"][l, f])
                fill(c, 0, pair(g_rows[:, :, 0:P], u_rows[:, :, 0:P]))
                with sp.Fori(0, (NF2 - 1) // 3) as i:
                    for j in range(3):
                        at = bass.ds(i * (3 * P) + (j + 1) * P, P)
                        fill(c + 1 + j, i, pair(g_rows[:, :, at], u_rows[:, :, at]))
                with sp.Fori(0, 2) as i:
                    for j in range(6):
                        n = min(KT, NF2 - KT * (j % 3))
                        src = rows(io["ffn_w_down_2"][l, f], KT * P * (j % 3), n)
                        fill(c + NF2 + j, i * 2, plain(src[:, :, bass.ds(i * 512 + UC * (j // 3), UC)], n))

            for l in range(LAYERS):
                c0 = U1_END + UL * l
                ffn(c0, l, 0)
                c = c0 + UL_MIX
                wi = rows(io["w_in_2"][l])
                fill(c, 0, lambda r: [(r[:, 0:4, 0:P], wi[:, 0:4, 768:768 + P]), (r[:, 4:8, 0:P], wi[:, 4:8, 768:768 + P])])
                for n, col in enumerate((0, 784, 1040, 1808)):
                    fill(c + 1 + n, 0, plain(wi[:, :, col:col + UC]))
                for n in range(2):
                    col = 1296 + P * n
                    fill(c + 5 + n, 0, interleaved(wi[:, :, col:col + P], wi[:, :, col + 256:col + 256 + P]))
                for n, col in enumerate((256, 512)):
                    fill(c + 7 + n, 0, plain(wi[:, :, col:col + UC]))
                for n in range(4):
                    fill(c + 9 + n, 0, plain(rows(io["w_out_2"][l])[:, :, UC * n:UC * n + UC]))
                ffn(c0 + UL_UP_B, l, 1)
            sp.wait_ge(out_ready, 1)
            sp.dma_start(out[0].rearrange("(t p) d -> p t d", p=P),
                         hn[:, :, :].rearrange("p (t a) n -> p t (a n)", t=TT)).then_inc(out_stored, 16)
            sp.wait_ge(out_stored, 16)

        @block.gpsimd
        def _(pool):
            done = {"norm": 0, "head": 0}
            nc.gpsimd.memset(mhalf[:, :], -0.5).then_inc(pool_init, 1)
            nc.gpsimd.memset(ones_row[:, :], 1.0).then_inc(pool_init, 1)
            nc.gpsimd.memset(glr_t[:, :], 1.0).then_inc(pool_init, 1)
            pool.wait_ge(pool_init, 3)

            def power_norm():
                for k in range(1, 6):
                    pool.wait_ge(sq_ready, KT * done["norm"] + k + 1)
                    if k > 1:
                        pool.wait_ge(sq_sum, 5 * done["norm"] + k - 1)
                    nc.gpsimd.tensor_tensor(sq[:, 0, :], sq[:, 0, :], sq[:, k, :], ALU.add).then_inc(sq_sum, 1)
                done["norm"] += 1
                pool.wait_ge(var_ready, done["norm"])
                nc.gpsimd.tensor_tensor(rstd2[:, :], var2[:, :], mhalf[:, 0:1].broadcast_to([P, 2]),
                                        ALU.pow).then_inc(rstd_ready, 1)

            def power_heads(n):
                done["head"] += 1
                pool.wait_ge(var8_ready, done["head"])
                nc.gpsimd.tensor_tensor(rstd8[:, 0:n], var8[:, 0:n], mhalf[:, 0:1].broadcast_to([P, n]),
                                        ALU.pow).then_inc(rstd8_ready, 1)

            power_norm()
            power_heads(8)
            power_norm()
            power_norm()
            for l in range(LAYERS):
                power_norm()
                power_norm()
                power_norm()
                g_mix = G1_END + GL * l + GL_MIX
                pool.wait_ge(group_evac, g_mix)
                nc.gpsimd.memset(s_gla[:, :, :, :], 0.0).then_inc(zeroed, 1)
                nc.gpsimd.memset(up[:, :, 0:TAPS - 1], 0.0).then_inc(zeroed, 1)
                for t in range(TT):
                    pool.wait_ge(group_evac, g_mix + 2)
                    pool.wait_ge(e_ready, TT * l + t + 1)
                    nc.gpsimd.tensor_tensor(
                        ek[:, 1, t], ek[:, 0, t],
                        kg[:, t * P:t * P + P].rearrange("p (o i) -> p o i", o=1).broadcast_to([P, LEV, P]),
                        ALU.mult).then_inc(ke_ready, 1)
                power_heads(8)
                pool.wait_ge(centred_var, l + 1)
                nc.gpsimd.tensor_tensor(rstd2[:, :], var2[:, :], mhalf[:, 0:1].broadcast_to([P, 2]),
                                        ALU.pow).then_inc(conv_rstd, 1)
                power_norm()
                power_norm()
                power_norm()

        @block.scalar
        def _(act):
            count = {"chain": 0, "normed": 0}

            def link(ins):
                count["chain"] += 1
                ins.then_inc(act_chain, 1)
                act.wait_ge(act_chain, count["chain"])

            def hi(c, e=0):
                if isinstance(e, int) and c + NS * e >= TOTAL_UNITS:
                    return
                s = c % NS
                queries = sum(q <= c and q % NS == s for q in QUERY_UNITS)
                after(act, raw_loaded[s], 32 * (c // NS + 1 + queries), e * 32)
                if not (isinstance(e, int) and c + NS * e < NS):
                    after(act, unit_used, c - NS + 1, e * NS)
                nc.scalar.activation(w_hi[s][:, :, :], raw[s][:, :, :], ACT.Copy).then_inc(w_hi_ready, 1)

            def squares(src, tiles=range(KT)):
                for k in tiles:
                    nc.scalar.activation(sq[:, k, :], src[:, k, :], ACT.Square).then_inc(sq_ready, 1)

            def x_squares(n):
                for k in range(KT):
                    act.wait_ge(x_ready, KT * n + k + 1)
                    squares(x, (k,))

            def bank_squares(unit, bank, n):
                act.wait_ge(unit_used, unit + 1)
                for f in range(FT):
                    nc.scalar.activation(sq[:, FT * n + f, :], bank[:, f * T:f * T + T], ACT.Square).then_inc(sq_ready, 1)

            def x_hi(n, group, col):
                for k in range(KT):
                    act.wait_ge(x_ready, KT * n + k + 1)
                    nc.scalar.activation(a_hi[:, k, :], x[:, k, :], ACT.Identity,
                                         scale=vecs[:, group, col + k:col + k + 1]).then_inc(a_hi_ready, 1)
                    squares(x, (k,))

            def norm_hi():
                for k in range(KT):
                    count["normed"] += 1
                    act.wait_ge(normed, count["normed"])
                    nc.scalar.activation(a_hi[:, k, :], hn[:, k, :], ACT.Copy).then_inc(a_hi_ready, 1)

            def operand_hi(dst, src, ready, used=0):
                act.wait_ge(*ready)
                after(act, unit_used, used)
                nc.scalar.activation(dst, src, ACT.Copy).then_inc(op_hi_ready, 1)

            def op(n):
                return op_ready, n

            act.dma_start(keep[:, :], io["table"][:, 0:NKEEP]).then_inc(small_loaded, 16)
            act.dma_start(sq[:, 0:2, :].rearrange("p a b -> p (a b)"), io["vec_rows"]).then_inc(small_loaded, 16)
            act.dma_start(pos_i, io["positions"].broadcast_to([P, T])).then_inc(small_loaded, 16)
            act.dma_start(masks_f32, io["masks"]).then_inc(small_loaded, 16)
            act.dma_start(ret_d[:, :, :].rearrange("p h n -> p (h n)"),
                          io["table"][:, COLS["ret"][0]:COLS["ret"][1]]).then_inc(small_loaded, 16)
            act.dma_start(sink_row[:, :], io["sink_row"]).then_inc(small_loaded, 16)
            act.dma_start(w2aug[:, :, :].rearrange("p l n -> p (l n)"), io["gate2"]).then_inc(small_loaded, 16)

            act.wait_ge(ang_ready, 1)
            nc.scalar.activation(sin2[:, :], ang[:, 0, :], ACT.Sin, scale=const("sgn")).then_inc(trig_ready, 1)
            act.wait_ge(ang_ready, 2)
            nc.scalar.activation(cos2[:, :], ang[:, 1, :], ACT.Sin).then_inc(trig_ready, 1)
            act.wait_ge(psm_free, PSM_X + 1)
            act.wait_ge(ps7_free, PS7_VEC + 1)
            squares(x)
            act.wait_ge(lam_arg, 1)
            nc.scalar.activation(sp_t[:, 1, :], sp_t[:, 0, :], ACT.Exp, scale=-1.0).then_inc(lam_exp, 1)
            hi(0)
            hi(1)
            norm_hi()
            for u in range(4):
                hi(u + 2)
                act.wait_ge(unit_used, u + 1)
                for half in range(2):
                    to, of = 64 * half, 64 * (1 - half)
                    nc.scalar.activation(qk_sw[to:to + 64, 2 * u:2 * u + 2, :], pair2(stream[u % 3][of:of + 64, :]),
                                         ACT.Copy).then_inc(swapped, 1)
            for u in range(4, 12):
                hi(u + 2)
            act.wait_ge(group_evac, 12)
            act.wait_ge(rot_done, 1)
            for k in range(KT):
                nc.scalar.activation(xc[:, k, :], xl[:, k, 3:3 + T], ACT.Identity,
                                     bias=vecs[:, 0, V1["lconv_b"] + k:V1["lconv_b"] + k + 1],
                                     scale=vecs[:, 0, V1["lconv_w"] + 24 + k:V1["lconv_w"] + 25 + k]).then_inc(lru_conv0, 1)
            for u in range(12, 16):
                hi(u + 2)
            operand_hi(b_hi[:, :, :], xc[:, :, :], op(1))
            act.wait_ge(psm_free, PSM_MEAN + 1)
            nc.scalar.activation(sq[:, :, :], o_ret[:, :, :], ACT.Square).then_inc(o_sq, 1)
            for n in range(4):
                u = 16 + n
                hi(u + 2)
                act.wait_ge(unit_used, u + 1)
                nc.scalar.activation(g_ret[:, 2 * n:2 * n + 2, :], pair2(stream[u % 3][:, :]), ACT.Tanh,
                                     scale=0.5).then_inc(act_gate, 1)
            act.wait_ge(group_evac, 16)
            nc.scalar.activation(gel[:, :, :], y_lru[:, :, :], ACT.Square).then_inc(ge_sq, 1)
            for n in range(8):
                if n % 4 == 0:
                    hi(U1_RG + n // 4 + 2)
                g = G1_RG + n
                if n % 4 < 3:
                    act.wait_ge(rg_done, 3 * (n // 4) + n % 4 + 1)
                else:
                    act.wait_ge(unit_used, U1_RG + n // 4 + 1)
                dst = la if n < 4 else i_gate
                for f in range(2):
                    k = 2 * (n % 4) + f
                    col = 8 * (n // 4) + k
                    nc.scalar.activation(dst[:, k, :], stream[g % 3][:, f * T:f * T + T], ACT.Tanh,
                                         bias=half_b[:, col:col + 1], scale=0.5).then_inc(act_gate, 1)
            act.wait_ge(ge_cube, 1)
            nc.scalar.activation(gel[:, :, :], gel[:, :, :], ACT.Tanh, scale=SQ2PI * GELU_C).then_inc(ge_th, 1)
            operand_hi(b_hi[:, :, :], o_ret[:, :, :], op(2), U1_GATES)
            act.wait_ge(group_evac, G1_RG + 4)
            nc.scalar.activation(a_lru[:, :, :], la, ACT.Exp).then_inc(lru_act, 1)
            nc.scalar.activation(la, la, ACT.Tanh).then_inc(lru_act, 1)
            act.wait_ge(ge_done, 1)
            for n in range(8):
                hi(U1_GATES + n + 2)
                g = G1_GATES + n
                act.wait_ge(unit_used, U1_GATES + n + 1)
                dst = ga if n < 4 else gb
                for f in range(2):
                    k = 2 * (n % 4) + f
                    col = 16 + 8 * (n // 4) + k
                    nc.scalar.activation(dst[:, k, :], stream[g % 3][:, f * T:f * T + T], ACT.Tanh,
                                         bias=half_b[:, col:col + 1], scale=0.5).then_inc(act_gate, 1)
                if n == 2:
                    act.wait_ge(v_ready, 1)
                    nc.scalar.activation(la, la, ACT.Sqrt).then_inc(sqrt_done, 1)
            operand_hi(a_hi[:, :, :], y_lru[:, :, :], op(3), U1_RETO)
            for n in range(8):
                hi(U1_RETO + n + 2)
                if n >= 4:
                    m = n - 4
                    operand_hi(b_hi[:, 2 * m:2 * m + 2, :], ga[:, 2 * m:2 * m + 2, :], op(4 + m), U1_LRUO)
            for n in range(4):
                hi(U1_OUT + n + 2)
                act.wait_ge(group_evac, G1_OUT + n + 1)
                squares(x, (2 * n, 2 * n + 1))
            norm_hi()

            def hidden_hi(j, e3, ready, before):
                after(act, ready, before + j + 1, e3)
                dst = h_hi[:, j, :] if isinstance(e3, int) else h_hi[:, bass.ds(e3 + j, 1), :].rearrange("p o n -> p (o n)")
                nc.scalar.activation(dst, hb[:, j % 3, :], ACT.Copy).then_inc(h_hi_ready, 1)

            def ff1_step(j, e, e3):
                def col(name, extra):
                    at = V1B[name] + extra + j
                    return vecs[:, 1, at:at + 1] if isinstance(e3, int) else vecs[:, 1, bass.ds(e3 + at, 1)]

                after(act, unit_used, U1_UP + j + 1, e3)
                nc.scalar.activation(cg[:, j % 3, :], stream[j % 3][:, 0:T], ACT.Identity, bias=col("fconv_b", 0),
                                     scale=col("fconv_w", 2 * NF1)).then_inc(tap_ready, 1)
                before = j or not isinstance(e3, int)
                if before:
                    gelu_tanh(j - 1, e3)
                hi(U1_UP + j + 3, e)
                after(act, conv_done, j + 1, e3)
                nc.scalar.activation(cub[:, j % 3, :], cg[:, j % 3, :], ACT.Square).then_inc(csq_ready, 1)
                if before:
                    hidden_hi(j - 1, e3, group_evac, G1_UP)

            def gelu_tanh(j, e3):
                after(act, cube_ready, j + 1, e3)
                nc.scalar.activation(th[:, j % 3, :], cub[:, j % 3, :], ACT.Tanh, scale=SQ2PI * GELU_C).then_inc(th_ready, 1)

            hi(U1_UP + 2)
            for j in range(3):
                ff1_step(j, 0, 0)
            with act.Fori(1, NF1 // 3) as i:
                for j in range(3):
                    ff1_step(j, i, i * 3)
            gelu_tanh(NF1 - 1, 0)
            hidden_hi(NF1 - 1, 0, group_evac, G1_UP)
            for n in range(4):
                for m in range(3 if n < 3 else 2):
                    hi(U1_DOWN + 3 * n + m + 3)
                act.wait_ge(group_evac, G1_DOWN + n + 1)
                squares(x, (2 * n, 2 * n + 1))

            def ffn(c0, g0, b0):
                def unit(j, e, e3):
                    after(act, group_evac, g0 + j + 1, e3)
                    nc.scalar.activation(th[:, j % 3, :], gu[:, j % 3, 0, :], ACT.Tanh, scale=0.5).then_inc(th_ready, 1)
                    if j:
                        hi(c0 + j + 3, e)
                    hidden_hi(j, e3, hb_ready, b0)

                hi(c0 + 2)
                hi(c0 + 3)
                for j in range(4):
                    unit(j, 0, 0)
                with act.Fori(0, (NF2 - 4) // 3) as i:
                    for j in range(4, 7):
                        unit(j, i, i * 3)
                for n in range(4):
                    for m in range(3 if n < 3 else 2):
                        hi(c0 + NF2 + 3 * n + m + 3)
                    bank_squares(c0 + NF2 + 3 * n + 2, psm[:, n % 2, :], n)

            for l in range(LAYERS):
                c0, g0 = U1_END + UL * l, G1_END + GL * l
                psm0, ps70, st0, op0 = PSM_1 + PSM_L * l, PS7_1 + PS7_L * l, ST_1 + ST_L * l, 7 + 2 * l
                x_hi(3 * l, 2 + l, 0)
                ffn(c0, g0, 2 * l * NF2)
                x_squares(3 * l + 1)
                norm_hi()
                cm, gm = c0 + UL_MIX, g0 + GL_MIX

                def bank(n):
                    return stream[(BANK_MIX + n) % 3]

                def read_out(n, *parts):
                    act.wait_ge(unit_used, cm + n + 1)
                    for dst, src, scale in parts:
                        ins = nc.scalar.activation(dst, src, ACT.Copy, scale=scale)
                    ins.then_inc(group_evac, 1)

                hi(cm + 2)
                hi(cm + 3)
                act.wait_ge(pool_init, 3)
                read_out(0, (glr_t[0:16, :], bank(0)[0:16, 0:T], 1.0))
                read_out(1, (qg[:, :], bank(1)[:, 0:T], GDK ** -0.5), (kg[:, :], bank(1)[:, T:2 * T], 1.0))
                act.wait_ge(ps7_full, ps70 + PS7_Z + 1)
                link(nc.scalar.activation(lg[:, 0, :], ps7[:, 0:T], ACT.Abs))
                nc.scalar.activation(lg[:, 0, :], lg[:, 0, :], ACT.Exp, scale=-1.0).then_inc(ez_ready, 1)
                hi(cm + 4)
                read_out(2, (ca[:, :, :], pair2(bank(2)[:, :]), 0.5))
                hi(cm + 5)
                act.wait_ge(unit_used, cm + 4)
                nc.scalar.activation(th2[:, :, :], pair2(bank(3)[:, :]), ACT.Tanh, scale=0.5).then_inc(group_evac, 1)
                hi(cm + 6)
                act.wait_ge(lev_ready, l + 1)
                for t in range(TT):
                    for m in range(2):
                        ins = nc.scalar.activation(ek[:, 0, t, 4 * m:4 * m + 4, :],
                                                   psm[:, 2 * t + m, :].rearrange("p (n i) -> p n i", n=4), ACT.Exp)
                    ins.then_inc(e_ready, 1)
                read_out(4, (ks[:, :], bank(4)[:, 0:T], 1.0),
                         (vs[:, :, :], bank(4)[:, T:2 * T].rearrange("p (t n) -> p t n", t=TT), 1.0))
                hi(cm + 7)
                for n in range(2):
                    read_out(5 + n, (qs[:, 2 * n:2 * n + 2, :], pair2(bank(5 + n)[:, :]), SWD ** -0.5))
                    hi(cm + 8 + n)
                def softmax_rows():
                    for n in range(2 * SWH):
                        yield n, ss[:, n, 0:T] if n < SWH else ss[:, n - SWH, T:384]

                act.wait_ge(ss_ready, l + 1)
                nc.scalar.activation(mx[:, 2, :], mx[:, 2, :], ACT.Exp)
                for n, scores in softmax_rows():
                    ins = nc.scalar.activation(scores, scores, ACT.Exp, bias=mx[:, 3, n:n + 1], accum_out=mx[:, 0, n:n + 1])
                ins.then_inc(ss_exp, 1)
                read_out(7, (vg[:, :, :], pair2(bank(7)[:, :]), 1.0))
                hi(cm + 10)
                act.wait_ge(sums_ready, l + 1)
                for n, scores in softmax_rows():
                    ins = nc.scalar.activation(scores, scores, ACT.Identity, scale=mx[:, 3, n:n + 1])
                ins.then_inc(p_ready, 1)
                act.wait_ge(unit_used, cm + 9)
                nc.scalar.activation(sq2[:, :, :], pair2(bank(8)[:, :]), ACT.Tanh, scale=0.5)
                read_out(8, (gr[:, :, :], pair2(bank(8)[:, :]), 1.0))
                for r in range(2):
                    act.wait_ge(pt_full, 2 * l + r + 1)
                    for m in range(3):
                        at = 12 * r + 4 * m
                        ins = nc.scalar.activation(pt[:, at:at + 4, :], stream[m].rearrange("p (n i) -> p n i", n=4), ACT.Copy)
                    ins.then_inc(pt_free, 1)
                act.wait_ge(centred, l + 1)
                nc.scalar.activation(th2[:, :, :], yc[0][:, :, :], ACT.Square).then_inc(yc_sq, 1)
                act.wait_ge(ps7_free, ps70 + PS7_PV + 1)
                nc.scalar.activation(sq2[:, :, :], og[:, :, :], ACT.Square).then_inc(og_sq, 1)
                operand_hi(b_hi[:, 0:2, :], hn[:, 0:2, :], op(op0 + 1))
                act.wait_ge(silu_in, l + 1)
                nc.scalar.activation(th2[:, :, :], yc[0][:, :, :], ACT.Tanh).then_inc(silu_th, 1)
                operand_hi(b_hi[:, 2:4, :], hn[:, 2:4, :], op(op0 + 2))
                operand_hi(b_hi[:, 4:8, :].rearrange("p (b f) n -> p b (f n)", b=2), psm[:, 0:2, :], (pv_full, l + 1))
                for n in range(4):
                    hi(cm + 11 + n)
                    bank_squares(cm + 9 + n, stream[(BANK_WOUT + n) % 3], n)
                x_hi(3 * l + 2, 2 + l, 32)
                ffn(c0 + UL_UP_B, g0 + GL_UP_B, (2 * l + 1) * NF2)

        @block.vector
        def _(dve):
            V = nc.vector
            chain = {"n": 0, "e": 0}
            count = {"a_lo": 0, "op_lo": 0}

            def mark(ins):
                chain["n"] += 1
                ins.then_inc(dve_chain, 1)
                return chain["n"]

            def link(ins):
                after(dve, dve_chain, mark(ins), chain["e"])

            def lo(c, e=0):
                if isinstance(e, int) and c + NS * e >= TOTAL_UNITS:
                    return
                s = c % NS
                after(dve, w_hi_ready, c + 1, e * NS)
                V.tensor_tensor(w_lo[s][:, :, :], raw[s][:, :, :], w_hi[s][:, :, :].bitcast(F32),
                                ALU.subtract).then_inc(w_split, 1)

            def operand_lo(dst, src, hi_part):
                count["op_lo"] += 1
                dve.wait_ge(op_hi_ready, count["op_lo"])
                V.tensor_tensor(dst, src, hi_part.bitcast(F32), ALU.subtract).then_inc(op_split, 1)

            def variance(st):
                dve.wait_ge(stat_full, st + 1)
                V.tensor_scalar(var2[:, :], ps7[:, 0:2], RMS_EPS, None, ALU.add).then_inc(var_ready, 1)

            def inv_rms(st, p7):
                variance(st)
                dve.wait_ge(ps7_full, p7 + 1)
                V.tensor_copy(rb[:, :], ps7[:, T:2 * T]).then_inc(ps7_free, 1)
                dve.wait_ge(ps7_free, p7 + 1)

            def pre_norm(st, p7, group, col):
                inv_rms(st, p7)

                def lo_tile(k):
                    count["a_lo"] += 1
                    dve.wait_ge(a_hi_ready, count["a_lo"])
                    V.tensor_tensor(a_lo[:, k, :], hn[:, k, :], a_hi[:, k, :].bitcast(F32),
                                    ALU.subtract).then_inc(a_split, 1)

                for k in range(KT):
                    V.scalar_tensor_tensor(out=hn[:, k, :], in0=x[:, k, :], scalar=vecs[:, group, col + k:col + k + 1],
                                           in1=rb[:, :], op0=ALU.mult, op1=ALU.mult).then_inc(normed, 1)
                    if k >= 2:
                        lo_tile(k - 2)
                lo_tile(KT - 2)
                lo_tile(KT - 1)

            def x_lo(k, group, col):
                count["a_lo"] += 1
                dve.wait_ge(a_hi_ready, count["a_lo"])
                V.scalar_tensor_tensor(out=a_lo[:, k, :], in0=x[:, k, :], scalar=vecs[:, group, col + k:col + k + 1],
                                       in1=a_hi[:, k, :].bitcast(F32), op0=ALU.mult, op1=ALU.subtract).then_inc(a_split, 1)

            def branch(bank, n, group, col, scale, norms):
                dve.wait_ge(sq_ready, KT * norms + FT * n + FT)
                for f in range(FT):
                    k = FT * n + f
                    ins = V.tensor_scalar(hn[:, k, :], bank[:, f * T:f * T + T], vecs[:, group, col + k:col + k + 1], scale,
                                          ALU.mult, ALU.mult)
                ins.then_inc(group_evac, 1)

            def post_norm(st, p7, next_gain=None):
                variance(st)
                dve.wait_ge(ps7_full, p7 + 1)
                at = []
                for k in range(KT + 2):
                    if k < KT:
                        ins = V.tensor_tensor(hn[:, k, :], hn[:, k, :], ps7[:, T:2 * T], ALU.mult)
                        if k < KT - 1:
                            at.append(mark(ins))
                        else:
                            ins.then_inc(ps7_free, 1)
                    if 1 <= k <= KT:
                        if k < KT:
                            dve.wait_ge(dve_chain, at[k - 1])
                        else:
                            dve.wait_ge(ps7_free, p7 + 1)
                        V.tensor_tensor(x[:, k - 1, :], x[:, k - 1, :], hn[:, k - 1, :], ALU.add).then_inc(x_ready, 1)
                    if k >= 2 and next_gain:
                        x_lo(k - 2, *next_gain)

            def half_log1p(dst, s, s2, e):
                link(V.tensor_scalar(s, e, 2.0, None, ALU.add))
                link(V.reciprocal(s, s))
                link(V.tensor_tensor(s, s, e, ALU.mult))
                link(V.tensor_tensor(s2, s, s, ALU.mult))
                link(V.tensor_scalar(dst, s2, 1.0 / 17, None, ALU.mult))
                for n in (15, 13, 11, 9, 7, 5, 3):
                    link(V.scalar_tensor_tensor(out=dst, in0=dst, scalar=1.0 / n, in1=s2, op0=ALU.add, op1=ALU.mult))
                link(V.scalar_tensor_tensor(out=dst, in0=dst, scalar=1.0, in1=s, op0=ALU.add, op1=ALU.mult))

            dve.wait_ge(small_loaded, 16 * N_SMALL)
            two_pi = 2 * np.pi
            c1 = 6.28125
            c2 = round((two_pi - c1) * 2 ** 20) / 2 ** 20
            c3 = two_pi - c1 - c2
            link(V.tensor_copy(ang_t[:, 0, :], pos_i))
            link(V.tensor_scalar(ang_t[:, 1, :], ang_t[:, 0, :], const("invf"), None, ALU.mult))
            for n, (shift, offset) in enumerate(((0.0, 0.0), (0.25, np.pi / 2))):
                r = ang[:, n, :]
                link(V.tensor_scalar(ang_t[:, 2, :], ang_t[:, 1, :], 1 / two_pi, shift, ALU.mult, ALU.add))
                link(V.tensor_scalar(ang_t[:, 2, :], ang_t[:, 2, :], MAGIC, -MAGIC, ALU.add, ALU.add))
                link(V.scalar_tensor_tensor(out=r, in0=ang_t[:, 2, :], scalar=-c1, in1=ang_t[:, 1, :],
                                            op0=ALU.mult, op1=ALU.add))
                for cn in (c2, c3):
                    link(V.scalar_tensor_tensor(out=r, in0=ang_t[:, 2, :], scalar=-cn, in1=r, op0=ALU.mult, op1=ALU.add))
                link(V.tensor_scalar(r, r, offset, 3.1415925, ALU.add, ALU.min))
                V.tensor_scalar(r, r, -3.1415925, None, ALU.max).then_inc(ang_ready, 1)
            link(V.tensor_copy(masks[:, :, :].rearrange("p n i -> p (n i)"), masks_f32))
            dve.wait_ge(psm_full, PSM_X + 1)
            for n in range(4):
                ins = V.tensor_copy(x[:, 2 * n:2 * n + 2, :], pair2(psm[:, n, :]))
            ins.then_inc(psm_free, 1)
            dve.wait_ge(ps7_full, PS7_VEC + 1)
            V.tensor_copy(vecs[:, :, :], ps7[:, :].rearrange("p (g c) -> p g c", g=4)).then_inc(ps7_free, 1)
            dve.wait_ge(ps7_full, PS7_SINK + 1)
            V.tensor_copy(sinks[:, :, :], ps7[:, 0:LAYERS * 16].rearrange("p (l n) -> p l n", l=LAYERS)).then_inc(ps7_free, 1)
            dve.wait_ge(ps7_free, PS7_SINK + 1)
            for dst, name, n in ((0, "b_r", 16), (16, "gate_b", 16), (32, "gn", 8)):
                V.tensor_scalar(half_b[:, dst:dst + n], vecs[:, 0, V1[name]:V1[name] + n], 0.5, None, ALU.mult)
            lam = vecs[:, 0, V1["lam"]:V1["lam"] + KT]
            link(V.tensor_scalar(sp_t[:, 3, :], lam, -1.0, None, ALU.mult))
            V.tensor_tensor(sp_t[:, 0, :], lam, sp_t[:, 3, :], ALU.max).then_inc(lam_arg, 1)
            link(V.tensor_scalar(sp_t[:, 2, :], lam, 0.0, 4.0, ALU.min, ALU.mult))
            pre_norm(ST_N0, PS7_N0, 0, V1["norm1"])
            lo(0)
            lo(1)
            dve.wait_ge(lam_exp, 1)
            half_log1p(sp_t[:, 5, :], sp_t[:, 3, :], sp_t[:, 4, :], sp_t[:, 1, :])
            link(V.scalar_tensor_tensor(out=sp4[:, :], in0=sp_t[:, 5, :], scalar=-8.0, in1=sp_t[:, 2, :],
                                        op0=ALU.mult, op1=ALU.add))

            for u in range(4):
                lo(u + 2)
                dve.wait_ge(swapped, 2 * u + 2)
                V.tensor_copy(qk_raw[:, 2 * u:2 * u + 2, :], pair2(stream[u % 3][:, :])).then_inc(group_evac, 1)
            dve.wait_ge(trig_ready, 2)
            dve.wait_ge(group_evac, 4)

            def over_tiles(ap):
                return ap.rearrange("p (o n) -> p o n", o=1).broadcast_to([P, KT, T])

            for n in range(4):
                u = 4 + n
                if n == 0:
                    rot0 = mark(V.tensor_tensor(qk_raw, qk_raw, over_tiles(cos2[:, :]), ALU.mult))
                elif n == 1:
                    rot1 = mark(V.tensor_tensor(qk_sw[:, :, :], qk_sw[:, :, :], over_tiles(sin2[:, :]), ALU.mult))
                elif n == 2:
                    dve.wait_ge(dve_chain, rot1)
                    V.tensor_tensor(qk_rot[:, :, :], qk_raw, qk_sw[:, :, :], ALU.add).then_inc(rot_done, 1)
                lo(u + 2)
                dve.wait_ge(unit_used, u + 1)
                V.tensor_copy(v_ret[:, :, UC * n:UC * n + UC], pair2(stream[u % 3][:, :])).then_inc(group_evac, 1)
            dve.wait_ge(rot_done, 1)
            link(V.memset(xl[:, :, 0:3], 0.0))
            for n in range(4):
                u = 8 + n
                lo(u + 2)
                dve.wait_ge(unit_used, u + 1)
                V.tensor_copy(xl[:, 2 * n:2 * n + 2, 3:3 + T], pair2(stream[u % 3][:, :])).then_inc(group_evac, 1)
                if n == 2:
                    dve.wait_ge(psm_full, PSM_SC + 1)
                    for h in range(HEADS):
                        ins = V.tensor_tensor(st_ret[:, 384 * h:384 * h + 384], psm[:, h, 0:384], ret_d[:, h, :], ALU.mult)
                    ins.then_inc(psm_free, 1)

            at = [0] * KT
            for n in range(4):
                u = 12 + n
                lo(u + 2)
                dve.wait_ge(unit_used, u + 1)
                V.tensor_copy(y_lru[:, 2 * n:2 * n + 2, :], pair2(stream[u % 3][:, :])).then_inc(group_evac, 1)
                if n == 0:
                    dve.wait_ge(psm_full, PSM_O + 1)
                    for h in range(HEADS):
                        ins = V.tensor_copy(o_ret[:, 2 * h:2 * h + 2, :], pair2(psm[:, h, :]))
                    ins.then_inc(psm_free, 1)
                if n == 2:
                    dve.wait_ge(stat_full, ST_RMEAN + 1)
                    V.tensor_copy(var8[:, :], ps7[:, 0:8]).then_inc(mean_ready, 1)
                if n < 3:
                    tap = 2 - n
                    for k in range(KT):
                        if n == 0:
                            dve.wait_ge(lru_conv0, k + 1)
                        else:
                            dve.wait_ge(dve_chain, at[k])
                        col = V1["lconv_w"] + 8 * tap + k
                        ins = V.scalar_tensor_tensor(out=xc[:, k, :], in0=xl[:, k, tap:tap + T],
                                                     scalar=vecs[:, 0, col:col + 1], in1=xc[:, k, :],
                                                     op0=ALU.mult, op1=ALU.add)
                        if n < 2 or k < KT - 1:
                            at[k] = mark(ins)
                        else:
                            ins.then_inc(op_ready, 1)
            operand_lo(b_lo[:, :, :], xc[:, :, :], b_hi[:, :, :])

            def heads(tile, b):
                return tile[:, 4 * b:4 * b + 4, :].rearrange("p (h d) n -> p h d n", h=2)

            def over_halves(b):
                return psm[:, b, :].rearrange("p (h o n) -> p h o n", h=2, o=1).broadcast_to([P, 2, 2, T])

            dve.wait_ge(psm_full, PSM_MEAN + 1)
            for b in range(2):
                ins = V.tensor_tensor(heads(o_ret, b), heads(o_ret, b), over_halves(b), ALU.subtract)
            ins.then_inc(psm_free, 1)
            for n in range(4):
                u = 16 + n
                lo(u + 2)
                dve.wait_ge(act_gate, n + 1)
                V.scalar_tensor_tensor(out=g_ret[:, 2 * n:2 * n + 2, :], in0=g_ret[:, 2 * n:2 * n + 2, :], scalar=1.0,
                                       in1=pair2(stream[u % 3][:, :]), op0=ALU.add, op1=ALU.mult).then_inc(group_evac, 1)
                if n == 0:
                    dve.wait_ge(stat_full, ST_RVAR + 1)
                    V.tensor_scalar(var8[:, :], ps7[:, 0:8], RMS_EPS, None, ALU.add).then_inc(var8_ready, 1)
                if n == 1:
                    dve.wait_ge(psm_full, PSM_VAR + 1)
                    for b in range(2):
                        ins = V.tensor_tensor(heads(o_ret, b), heads(o_ret, b), over_halves(b), ALU.mult)
                    ins.then_inc(psm_free, 1)
            dve.wait_ge(ge_sq, 1)
            V.scalar_tensor_tensor(out=gel[:, :, :], in0=gel[:, :, :], scalar=1 / GELU_C, in1=y_lru[:, :, :],
                                   op0=ALU.add, op1=ALU.mult).then_inc(ge_cube, 1)
            dve.wait_ge(group_evac, 20)
            dve.wait_ge(psm_free, PSM_VAR + 1)
            for k in range(KT):
                ins = V.scalar_tensor_tensor(out=o_ret[:, k, :], in0=o_ret[:, k, :], scalar=half_b[:, 32 + k:33 + k],
                                             in1=g_ret[:, k, :], op0=ALU.mult, op1=ALU.mult)
            ins.then_inc(op_ready, 1)
            for n in range(8):
                if n % 4 == 0:
                    lo(U1_RG + n // 4 + 2)
                dve.wait_ge(act_gate, 4 + 2 * n + 2)
                for f in range(2):
                    k = 2 * (n % 4) + f
                    if n < 4:
                        ins = V.tensor_scalar(la[:, k, :], la[:, k, :], 1.0, sp4[:, k:k + 1], ALU.add, ALU.mult)
                    else:
                        ins = V.scalar_tensor_tensor(out=i_gate[:, k, :], in0=i_gate[:, k, :], scalar=1.0,
                                                     in1=xc[:, k, :], op0=ALU.add, op1=ALU.mult)
                ins.then_inc(group_evac, 1)
            operand_lo(b_lo[:, :, :], o_ret[:, :, :], b_hi[:, :, :])
            dve.wait_ge(ge_th, 1)
            V.scalar_tensor_tensor(out=y_lru[:, :, :], in0=gel[:, :, :], scalar=1.0, in1=y_lru[:, :, :],
                                   op0=ALU.add, op1=ALU.mult).then_inc(ge_done, 1)
            for n in range(8):
                lo(U1_GATES + n + 2)
                dve.wait_ge(act_gate, 20 + 2 * n + 2)
                dst = (ga if n < 4 else gb)[:, 2 * (n % 4):2 * (n % 4) + 2, :]
                V.tensor_scalar(dst, dst, 0.5, 0.5, ALU.mult, ALU.add).then_inc(group_evac, 1)
                if n == 0:
                    dve.wait_ge(lru_act, 2)
                    dve.wait_ge(op_split, 2)
                    link(V.tensor_scalar(tmp[:, :, :], la, -1.0, 1.0, ALU.mult, ALU.add))
                    link(V.reciprocal(tmp[:, :, :], tmp[:, :, :]))
                    link(V.scalar_tensor_tensor(out=la, in0=la, scalar=-2.0, in1=tmp[:, :, :], op0=ALU.mult, op1=ALU.mult))
                    V.tensor_scalar(la, la, 1e-30, None, ALU.max).then_inc(v_ready, 1)
                if n == 4:
                    dve.wait_ge(sqrt_done, 1)
                    link(V.scalar_tensor_tensor(out=i_gate[:, :, :], in0=i_gate[:, :, :], scalar=0.5, in1=la,
                                                op0=ALU.mult, op1=ALU.mult))
                if n == 5:
                    for k in range(KT):
                        at[k] = mark(V.tensor_tensor_scan(tmp[:, k, :], a_lru[:, k, :], i_gate[:, k, :], 0.0,
                                                          ALU.mult, ALU.add))
                if n == 6:
                    dve.wait_ge(dve_chain, at[KT - 1])
                    V.scalar_tensor_tensor(out=y_lru[:, :, :], in0=tmp[:, :, :], scalar=0.5, in1=y_lru[:, :, :],
                                           op0=ALU.mult, op1=ALU.mult).then_inc(op_ready, 1)
            for n in range(4):
                lo(U1_RETO + n + 2)
                if n == 0:
                    operand_lo(a_lo[:, :, :], y_lru[:, :, :], a_hi[:, :, :])
                g = G1_RETO + n
                dve.wait_ge(unit_used, U1_RETO + n + 1)
                dst = ga[:, 2 * n:2 * n + 2, :]
                V.tensor_tensor(dst, dst, pair2(stream[g % 3][:, :]), ALU.mult).then_inc(group_evac, 1)
            for n in range(4):
                lo(U1_LRUO + n + 2)
                g = G1_LRUO + n
                dve.wait_ge(unit_used, U1_LRUO + n + 1)
                dst, acc = gb[:, 2 * n:2 * n + 2, :], ga[:, 2 * n:2 * n + 2, :]
                V.tensor_tensor(dst, dst, pair2(stream[g % 3][:, :]), ALU.mult).then_inc(group_evac, 1)
                dve.wait_ge(group_evac, g + 1)
                V.tensor_tensor(acc, acc, dst, ALU.add).then_inc(op_ready, 1)
                if n:
                    operand_lo(b_lo[:, 2 * n - 2:2 * n, :], ga[:, 2 * n - 2:2 * n, :], b_hi[:, 2 * n - 2:2 * n, :])
            operand_lo(b_lo[:, 6:8, :], ga[:, 6:8, :], b_hi[:, 6:8, :])
            for n in range(4):
                lo(U1_OUT + n + 2)
                g = G1_OUT + n
                dve.wait_ge(unit_used, U1_OUT + n + 1)
                dst = x[:, 2 * n:2 * n + 2, :]
                V.tensor_tensor(dst, dst, pair2(stream[g % 3][:, :]), ALU.add).then_inc(group_evac, 1)

            dve.wait_ge(group_evac, G1_OUT + 4)
            pre_norm(ST_N1, PS7_N1, 0, V1["norm2"])

            def hidden_lo(j, e3, h0):
                after(dve, h_hi_ready, h0 + j + 1, e3)

                def tile(t):
                    return t[:, j, :] if isinstance(e3, int) else t[:, bass.ds(e3 + j, 1), :].rearrange("p o n -> p (o n)")

                V.tensor_tensor(tile(h_lo), hb[:, j % 3, :], tile(h_hi).bitcast(F32), ALU.subtract).then_inc(h_split, 1)

            def gated(j, e3, th0, val, factor, ready):
                after(dve, th_ready, th0 + j + 1, e3)
                link(V.scalar_tensor_tensor(out=ab[:, j % 3, :], in0=th[:, j % 3, :], scalar=1.0, in1=factor,
                                            op0=ALU.add, op1=ALU.mult))
                V.scalar_tensor_tensor(out=hb[:, j % 3, :], in0=ab[:, j % 3, :], scalar=0.5, in1=val,
                                       op0=ALU.mult, op1=ALU.mult).then_inc(ready, 1)

            def ff1_step(j, e, e3):
                def col(tap):
                    at = V1B["fconv_w"] + NF1 * tap + j
                    return vecs[:, 1, at:at + 1] if isinstance(e3, int) else vecs[:, 1, bass.ds(e3 + at, 1)]

                before = j or not isinstance(e3, int)
                after(dve, tap_ready, j + 1, e3)
                bank, c = stream[j % 3], cg[:, j % 3, :]
                link(V.scalar_tensor_tensor(out=c[:, 1:T], in0=bank[:, 0:T - 1], scalar=col(1), in1=c[:, 1:T],
                                            op0=ALU.mult, op1=ALU.add))
                V.scalar_tensor_tensor(out=c[:, 2:T], in0=bank[:, 0:T - 2], scalar=col(0), in1=c[:, 2:T],
                                       op0=ALU.mult, op1=ALU.add).then_inc(conv_done, 1)
                if before:
                    ff1_product(j - 1, e3)
                if j > 1 or not isinstance(e3, int):
                    hidden_lo(j - 2, e3, 0)
                lo(U1_UP + j + 3, e)
                after(dve, csq_ready, j + 1, e3)
                V.scalar_tensor_tensor(out=cub[:, j % 3, :], in0=cub[:, j % 3, :], scalar=1 / GELU_C, in1=c,
                                       op0=ALU.add, op1=ALU.mult).then_inc(cube_ready, 1)

            def ff1_product(j, e3):
                gated(j, e3, 0, stream[j % 3][:, T:2 * T], cg[:, j % 3, :], group_evac)

            lo(U1_UP + 2)
            for j in range(3):
                ff1_step(j, 0, 0)
            n0 = chain["n"]
            with dve.Fori(1, NF1 // 3) as i:
                chain["e"] = (i - 1) * 6
                for j in range(3):
                    ff1_step(j, i, i * 3)
                assert chain["n"] - n0 == 6
            chain["n"], chain["e"] = n0 + 6 * (NF1 // 3 - 1), 0
            ff1_product(NF1 - 1, 0)
            hidden_lo(NF1 - 2, 0, 0)
            hidden_lo(NF1 - 1, 0, 0)
            for n in range(4):
                for m in range(3 if n < 3 else 2):
                    lo(U1_DOWN + 3 * n + m + 3)
                dve.wait_ge(unit_used, U1_DOWN + 3 * n + 3)
                dst = x[:, 2 * n:2 * n + 2, :]
                V.tensor_tensor(dst, dst, pair2(psm[:, n % 2, :]), ALU.add).then_inc(group_evac, 1)
            dve.wait_ge(group_evac, G1_END)
            inv_rms(ST_NF, PS7_NF)
            for k in range(KT):
                V.scalar_tensor_tensor(out=x[:, k, :], in0=x[:, k, :], scalar=vecs[:, 0, V1["norm_f"] + k:V1["norm_f"] + k + 1],
                                       in1=rb[:, :], op0=ALU.mult, op1=ALU.mult).then_inc(x_ready, 1)
                if k >= 2:
                    x_lo(k - 2, 2, 0)
            x_lo(KT - 2, 2, 0)
            x_lo(KT - 1, 2, 0)

            def ffn(c0, g0, bank0, h0, st, p7, group, col, norms):
                def unit(j, e, e3):
                    after(dve, unit_used, c0 + j + 1, e3)
                    V.tensor_tensor(gu[:, j % 3, :, :], pair2(stream[(bank0 + j) % 3][:, :]),
                                    rb[:, :].rearrange("p (o n) -> p o n", o=1).broadcast_to([P, 2, T]),
                                    ALU.mult).then_inc(group_evac, 1)
                    if j >= 2:
                        lo(c0 + j + 2, e)
                    gated(j, e3, h0, gu[:, j % 3, 1, :], gu[:, j % 3, 0, :], hb_ready)
                    if j:
                        hidden_lo(j - 1, e3, h0)

                lo(c0 + 2)
                lo(c0 + 3)
                inv_rms(st, p7)
                for j in range(4):
                    unit(j, 0, 0)
                n0 = chain["n"]
                with dve.Fori(0, (NF2 - 4) // 3) as i:
                    chain["e"] = i * 3
                    for j in range(4, 7):
                        unit(j, i, i * 3)
                    assert chain["n"] - n0 == 3
                chain["n"], chain["e"] = n0 + NF2 - 4, 0
                hidden_lo(NF2 - 1, 0, h0)
                for n in range(4):
                    for m in range(3):
                        lo(c0 + NF2 + 3 * n + m + 2)
                    branch(psm[:, n % 2, :], n, group, col, 0.5, norms)
                dve.wait_ge(group_evac, g0 + NF2 + 4)

            for l in range(LAYERS):
                c0, g0 = U1_END + UL * l, G1_END + GL * l
                psm0, ps70, st0, h0 = PSM_1 + PSM_L * l, PS7_1 + PS7_L * l, ST_1 + ST_L * l, NF1 + 2 * NF2 * l
                group = 2 + l

                def vec(name, k):
                    return vecs[:, group, VL[name] + k:VL[name] + k + 1]

                ffn(c0, g0, 0, h0, st0 + ST_G0, ps70 + PS7_G0, group, 8, 4 + 6 * l)
                post_norm(st0 + ST_G1, ps70 + PS7_G1)
                dve.wait_ge(x_ready, KT * (3 * l + 2))
                pre_norm(st0 + ST_G2, ps70 + PS7_G2, group, 16)

                cm, gm = c0 + UL_MIX, g0 + GL_MIX

                def bank(n):
                    return stream[(BANK_MIX + n) % 3]

                conv_at = []

                def conv(steps):
                    for _ in range(steps):
                        n = len(conv_at)
                        tap, f = n // 2, n % 2
                        acc, src, w = yc[tap % 2][:, f, :], up[:, f, tap:tap + T], vec("conv_w", n)
                        if tap == 0:
                            ins = V.tensor_scalar(acc, src, w, vec("conv_b", f), ALU.mult, ALU.add)
                        elif tap == 1:
                            ins = V.tensor_scalar(acc, src, w, None, ALU.mult)
                        else:
                            dve.wait_ge(dve_chain, conv_at[n - 4])
                            ins = V.scalar_tensor_tensor(out=acc, in0=src, scalar=w, in1=acc, op0=ALU.mult, op1=ALU.add)
                        conv_at.append(mark(ins))

                def gla_scores(n):
                    t, heads = n // 4, slice(2 * (n % 2), 2 * (n % 2) + 2)
                    dve.wait_ge(zeroed, 2 * l + 1)
                    if n >= 2:
                        dve.wait_ge(psm_free, psm0 + PSM_GLA + n - 1)
                    dve.wait_ge(psm_full, psm0 + PSM_GLA + n + 1)
                    for m in range(4):
                        level = 4 * (n // 2 % 2) + m
                        ins = V.copy_predicated(s_gla[:, t, heads, :], masks[:, level:level + 1, :].broadcast_to([P, 2, P]),
                                                psm[:, heads, m * P:m * P + P])
                        if m < 3:
                            written = mark(ins)
                            conv(1)
                            dve.wait_ge(dve_chain, written)
                    ins.then_inc(psm_free, 1)
                    conv(1)

                def window_scores(b):
                    dve.wait_ge(psm_full, psm0 + PSM_SWA + b + 1)
                    for n in range(4):
                        head = (n % 2) * 4 + 2 * b + n // 2
                        ins = V.scalar_tensor_tensor(out=ss[:, 4 * b + n, :], in0=const("alibi"), scalar=2.0 ** -(head + 1),
                                                     in1=psm[:, n, 0:384], op0=ALU.mult, op1=ALU.add)
                    ins.then_inc(psm_free, 1)

                lo(cm + 2)
                lo(cm + 3)
                dve.wait_ge(ez_ready, l + 1)
                V.tensor_scalar(lg[:, 1, :], ps7[:, 0:T], 0.0, None, ALU.min).then_inc(ps7_free, 1)
                half_log1p(lg[:, 4, :], lg[:, 2, :], lg[:, 3, :], lg[:, 0, :])
                dve.wait_ge(ps7_free, ps70 + PS7_Z + 1)
                V.scalar_tensor_tensor(out=lg[:, 1, :], in0=lg[:, 4, :], scalar=-2.0, in1=lg[:, 1, :],
                                       op0=ALU.mult, op1=ALU.add).then_inc(glog_ready, 1)
                lo(cm + 4)
                dve.wait_ge(zeroed, 2 * l + 2)
                dve.wait_ge(group_evac, gm + 4)
                link(V.scalar_tensor_tensor(out=up[:, :, TAPS - 1:TAPS - 1 + T], in0=th2[:, :, :], scalar=1.0,
                                            in1=ca[:, :, :], op0=ALU.add, op1=ALU.mult))
                lo(cm + 5)
                conv(12)
                lo(cm + 6)
                conv(6)
                lo(cm + 7)
                for t in range(TT):
                    dve.wait_ge(e_ready, TT * l + t + 1)
                    ins = V.tensor_tensor(qe[:, t, :, :], ek[:, 0, t, :, :],
                                          qg[:, t * P:t * P + P].rearrange("p (o i) -> p o i", o=1).broadcast_to([P, LEV, P]),
                                          ALU.mult)
                ins.then_inc(qe_ready, 1)
                window_scores(0)
                conv(4)
                lo(cm + 8)
                conv(6)
                window_scores(1)
                dve.wait_ge(psm_free, psm0 + PSM_SWA + 2)
                V.tensor_reduce(mx[:, 0, 0:8], ss[:, :, 0:T], AX, ALU.max)
                link(V.tensor_reduce(mx[:, 0, 8:16], ss[:, :, T:384], AX, ALU.max))
                link(V.tensor_tensor(mx[:, 1, :], mx[:, 0, :], sinks[:, l, :], ALU.max))
                V.tensor_tensor(mx[:, 2, :], sinks[:, l, :], mx[:, 1, :], ALU.subtract)
                V.tensor_scalar(mx[:, 3, :], mx[:, 1, :], -1.0, None, ALU.mult).then_inc(ss_ready, 1)
                for n in range(8):
                    gla_scores(n)
                    if n == 2:
                        dve.wait_ge(ss_exp, l + 1)
                        link(V.tensor_tensor(mx[:, 0, :], mx[:, 0, :], mx[:, 2, :], ALU.add))
                        V.reciprocal(mx[:, 3, :], mx[:, 0, :]).then_inc(sums_ready, 1)
                    if n == 5:
                        dve.wait_ge(group_evac, gm + 9)
                        V.scalar_tensor_tensor(out=gr[:, :, :], in0=sq2[:, :, :], scalar=1.0, in1=gr[:, :, :],
                                               op0=ALU.add, op1=ALU.mult).then_inc(gate_ready, 1)
                conv(2 * TAPS - len(conv_at))
                dve.wait_ge(dve_chain, conv_at[-1])
                V.tensor_tensor(yc[0][:, :, :], yc[0][:, :, :], yc[1][:, :, :], ALU.add).then_inc(yc_ready, 1)
                dve.wait_ge(psm_full, psm0 + PSM_CROSS + 1)
                V.tensor_copy(s_cross[:, :, :], psm[:, :, 0:P]).then_inc(psm_free, 1)
                def over_tiles2(ap):
                    return ap.rearrange("p (o n) -> p o n", o=1).broadcast_to([P, 2, T])

                cbank = stream[(BANK_WOUT + 2) % 3]
                dve.wait_ge(conv_full, 2 * l + 1)
                dve.wait_ge(yc_ready, l + 1)
                V.tensor_tensor(yc[0][:, :, :], yc[0][:, :, :], over_tiles2(cbank[:, T:2 * T]), ALU.subtract).then_inc(centred, 1)
                lo(cm + 9)
                dve.wait_ge(ps7_full, ps70 + PS7_PV + 1)
                V.tensor_copy(og[:, :, :], pair2(ps7[:, :])).then_inc(ps7_free, 1)
                lo(cm + 10)
                dve.wait_ge(stat_full, st0 + ST_GLA + 1)
                V.tensor_scalar(var8[:, :], ps7[:, 0:8], RMS_EPS, None, ALU.add).then_inc(var8_ready, 1)
                dve.wait_ge(stat_full, st0 + ST_CVAR + 1)
                V.tensor_scalar(var2[:, :], cbank[:, 0:2], LN_EPS, None, ALU.add).then_inc(centred_var, 1)
                dve.wait_ge(ps7_full, ps70 + PS7_GBC + 1)
                for f in range(2):
                    ins = V.scalar_tensor_tensor(out=og[:, f, :], in0=og[:, f, :], scalar=vec("gla_g", f),
                                                 in1=ps7[:, f * T:f * T + T], op0=ALU.mult, op1=ALU.mult)
                ins.then_inc(ps7_free, 1)
                dve.wait_ge(ps7_free, ps70 + PS7_GBC + 1)
                dve.wait_ge(gate_ready, l + 1)
                V.scalar_tensor_tensor(out=hn[:, 0:2, :], in0=og[:, :, :], scalar=0.5, in1=gr[:, :, :],
                                       op0=ALU.mult, op1=ALU.mult).then_inc(op_ready, 1)
                dve.wait_ge(conv_full, 2 * l + 2)
                for f in range(2):
                    ins = V.scalar_tensor_tensor(out=yc[0][:, f, :], in0=yc[0][:, f, :], scalar=vec("ln_g", f),
                                                 in1=cbank[:, T:2 * T], op0=ALU.mult, op1=ALU.mult)
                link(ins)
                for f in range(2):
                    ins = V.tensor_scalar(yc[0][:, f, :], yc[0][:, f, :], vec("ln_b", f), 0.5, ALU.add, ALU.mult)
                ins.then_inc(silu_in, 1)
                operand_lo(b_lo[:, 0:2, :], hn[:, 0:2, :], b_hi[:, 0:2, :])
                dve.wait_ge(silu_th, l + 1)
                V.scalar_tensor_tensor(out=hn[:, 2:4, :], in0=th2[:, :, :], scalar=1.0, in1=yc[0][:, :, :],
                                       op0=ALU.add, op1=ALU.mult).then_inc(op_ready, 1)
                operand_lo(b_lo[:, 2:4, :], hn[:, 2:4, :], b_hi[:, 2:4, :])
                operand_lo(b_lo[:, 4:8, :].rearrange("p (b f) n -> p b (f n)", b=2), psm[:, 0:2, :],
                           b_hi[:, 4:8, :].rearrange("p (b f) n -> p b (f n)", b=2))
                for n in range(4):
                    lo(cm + 11 + n)
                    branch(stream[(BANK_WOUT + n) % 3], n, group, 24, 1.0, 6 + 6 * l)
                dve.wait_ge(group_evac, g0 + GL_WOUT + 4)
                post_norm(st0 + ST_G3, ps70 + PS7_G3, (group, 32))
                ffn(c0 + UL_UP_B, g0 + GL_UP_B, BANK_UP_B, h0 + NF2, st0 + ST_G4, ps70 + PS7_G4, group, 40, 8 + 6 * l)
                post_norm(st0 + ST_G5, ps70 + PS7_G5, (group + 1, 0) if l < LAYERS - 1 else None)
            dve.wait_ge(psm_full, PSM_1 + PSM_L * LAYERS + 1)
            for n in range(4):
                ins = V.tensor_copy(hn[:, 2 * n:2 * n + 2, :], pair2(psm[:, n, :]))
            ins.then_inc(out_ready, 1)

        @block.tensor
        def _(pe):
            seen = {"norm": 0}

            def mm(dst, lhs, rhs, start, stop):
                return nc.tensor.matmul(dst, lhs, rhs, start=start, stop=stop, skip_group_check=True)

            def split_unit(c, e=0):
                after(pe, w_split, c + 1, e * NS)

            def feature_major(s, dst, tiles, hi_t, lo_t, first, last, kts=range(KT), ready=None):
                for n, (lhs, at) in enumerate(tiles):
                    for k in kts:
                        if ready and n == 0:
                            ready(k)
                        to = dst[:, at:at + T]
                        begin, end = first and n == 0 and k == kts[0], last and n == len(tiles) - 1 and k == kts[-1]
                        mm(to, lhs(w_hi[s], k), hi_t[:, k, :], begin, False)
                        mm(to, lhs(w_hi[s], k), lo_t[:, k, :], False, False)
                        ins = mm(to, lhs(w_lo[s], k), hi_t[:, k, :], False, end)
                return ins

            def block_cols(f):
                return lambda w, k: w[:, k, f * P:f * P + P]

            BOTH = [(block_cols(0), 0), (block_cols(1), T)]

            def token_major(s, dst, col, width, at, begin, tiles=range(TT)):
                for t in tiles:
                    to = dst[:, at + t * width:at + t * width + width]
                    tok = slice(t * P, t * P + P)
                    for k in range(KT):
                        w = slice(col, col + width)
                        mm(to, a_hi[:, k, tok], w_hi[s][:, k, w], begin and t == 0 and k == 0, False)
                        mm(to, a_lo[:, k, tok], w_hi[s][:, k, w], False, False)
                        ins = mm(to, a_hi[:, k, tok], w_lo[s][:, k, w], False, t == TT - 1 and k == KT - 1)
                return ins

            def bank_free(g, e3=0, back=2):
                after(pe, group_evac, g - back, e3)

            def a_ready(n):
                return lambda k: pe.wait_ge(a_split, KT * n + k + 1)

            def mean_squares(p7):
                seen["norm"] += 1
                after(pe, ps7_free, p7)
                pe.wait_ge(sq_sum, 5 * seen["norm"])
                for k in (0, KT - 2, KT - 1):
                    pe.wait_ge(sq_ready, KT * (seen["norm"] - 1) + k + 1)
                    for t in range(TT):
                        ins = mm(ps7[:, t:t + 1], sq[:, k, t * P:t * P + P], means[:, 0:1], k == 0 and t == 0,
                                 k == KT - 1 and t == TT - 1)
                ins.then_inc(stat_full, 1)

            def inverse_rms():
                pe.wait_ge(rstd_ready, seen["norm"])
                for t in range(TT):
                    ins = mm(ps7[:, T + t * P:T + t * P + P], rstd2[:, t:t + 1].broadcast_to([P, P]), ident, t == 0, t == 1)
                ins.then_inc(ps7_full, 1)

            def norm(p7):
                mean_squares(p7)
                inverse_rms()

            pe.wait_ge(small_loaded, 16 * N_SMALL)
            pe.wait_ge(x_loaded, 16)
            pe.wait_ge(pool_init, 2)
            xin = hn[:, :, :].rearrange("p (t a) n -> p t (a n)", t=TT)
            for k in range(KT):
                for t in range(TT):
                    at = (k % 2) * T + t * P
                    ins = nc.tensor.transpose(psm[:, k // 2, at:at + P], xin[:, t, k * P:k * P + P], ident)
            ins.then_inc(psm_full, 1)
            staged = sq[:, 0:2, :].rearrange("p a (b c) -> p (a b) c", b=2)
            for n in range(4):
                ins = nc.tensor.transpose(ps7[:, n * P:n * P + P], staged[:, n, :], ident)
            ins.then_inc(ps7_full, 1)
            pe.wait_ge(ps7_free, PS7_VEC + 1)
            mm(ps7[:, 0:LAYERS * 16], ones_row[:, :], sink_row[:, :], True, True).then_inc(ps7_full, 1)
            norm(PS7_N0)

            def project(c, g, bank, hi_t, lo_t, ready=None):
                split_unit(c)
                bank_free(g)
                feature_major(c % NS, bank, BOTH[0:1], hi_t, lo_t, True, False, ready=ready)
                ins = feature_major(c % NS, bank, BOTH[1:2], hi_t, lo_t, False, True)
                ins.then_inc(unit_used, 1)

            for u in range(8):
                if u < 4:
                    project(u, u, stream[u % 3], a_hi, a_lo, a_ready(0) if u == 0 else None)
                else:
                    split_unit(u)
                    bank_free(u)
                    token_major(u % NS, stream[u % 3], 0, UC, 0, True).then_inc(unit_used, 1)
            for u in range(8, 20):
                project(u, u, stream[u % 3], a_hi, a_lo)
                if u == 9:
                    pe.wait_ge(rot_done, 1)
                    pe.wait_ge(psm_free, PSM_SC)
                    for h in range(HEADS):
                        mm(psm[:, h, 0:T], qk_rot[:, 4 + h, 0:P], qk_rot[:, h, :], True, False)
                        ins = mm(psm[:, h, T:384], qk_rot[:, 4 + h, P:T], qk_rot[:, h, P:T], False, True)
                    ins.then_inc(psm_full, 1)
                if u == 11:
                    pe.wait_ge(psm_free, PSM_O)
                    for h in range(HEADS):
                        for d in range(2):
                            v = slice(h * DV + d * P, h * DV + d * P + P)
                            mm(psm[:, h, d * T:d * T + T], v_ret[:, 0, v], st_ret[:, 384 * h:384 * h + T], d == 0, False)
                            ins = mm(psm[:, h, d * T + P:d * T + T], v_ret[:, 1, v], st_ret[:, 384 * h + T:384 * h + 384],
                                     False, d == 1)
                    ins.then_inc(psm_full, 1)
                if u in (13, 16):
                    pe.wait_ge(psm_free, PSM_O + 1)
                    if u == 16:
                        pe.wait_ge(o_sq, 1)
                    src = o_ret if u == 13 else sq
                    after(pe, ps7_free, PS7_N1)
                    for t in range(TT):
                        for h in range(HEADS):
                            for d in range(2):
                                ins = mm(ps7[:, 4 * t + h:4 * t + h + 1], src[:, 2 * h + d, t * P:t * P + P], means[:, 1:2],
                                         t + h + d == 0, t == 1 and h == 3 and d == 1)
                    ins.then_inc(stat_full, 1)
                if u in (15, 17):
                    if u == 15:
                        pe.wait_ge(mean_ready, 1)
                    else:
                        pe.wait_ge(rstd8_ready, 1)
                    pe.wait_ge(psm_free, PSM_MEAN if u == 15 else PSM_VAR)
                    src = var8 if u == 15 else rstd8
                    for h in range(HEADS):
                        for t in range(TT):
                            at = (h % 2) * T + t * P
                            ins = mm(psm[:, h // 2, at:at + P], src[:, 4 * t + h:4 * t + h + 1].broadcast_to([P, P]), ident,
                                     h % 2 == 0 and t == 0, h % 2 == 1 and t == 1)
                    ins.then_inc(psm_full, 1)
            pe.wait_ge(op_split, 1)
            for m in range(2):
                c = U1_RG + m
                split_unit(c)
                for n in range(4):
                    g = G1_RG + 4 * m + n
                    bank_free(g)
                    ins = feature_major(c % NS, stream[g % 3], BOTH, b_hi, b_lo, True, True, kts=(2 * n, 2 * n + 1))
                    if n < 3:
                        ins.then_inc(rg_done, 1)
                ins.then_inc(unit_used, 1)
            for n in range(8):
                project(U1_GATES + n, G1_GATES + n, stream[(G1_GATES + n) % 3], a_hi, a_lo)
            pe.wait_ge(op_split, 2)
            for n in range(4):
                project(U1_RETO + n, G1_RETO + n, stream[(G1_RETO + n) % 3], b_hi, b_lo)
            pe.wait_ge(op_split, 3)
            for n in range(4):
                project(U1_LRUO + n, G1_LRUO + n, stream[(G1_LRUO + n) % 3], a_hi, a_lo)
            for n in range(4):
                project(U1_OUT + n, G1_OUT + n, stream[(G1_OUT + n) % 3], b_hi, b_lo,
                        (lambda k: pe.wait_ge(op_split, 4 + k // 2)) if n == 0 else None)
            norm(PS7_N1)

            def hidden(c, e, g, e3, bank, ready=None):
                split_unit(c, e)
                bank_free(g, e3)
                feature_major(c % NS, bank, BOTH[0:1], a_hi, a_lo, True, False, ready=ready)
                ins = feature_major(c % NS, bank, BOTH[1:2], a_hi, a_lo, False, True)
                ins.then_inc(unit_used, 1)

            def down(c, g, nf, h0):
                with pe.Fori(0, 2) as i:
                    for j in range(6):
                        n, m = j // 3, j % 3
                        split_unit(c + j, i * 2)
                        if m == 0:
                            bank_free(g + n, i * 2, back=1)
                        k0 = KT * m
                        kts = range(min(KT, nf - k0))
                        pe.wait_ge(h_split, h0 + k0 + len(kts))
                        hi_t, lo_t = h_hi[:, k0:k0 + len(kts), :], h_lo[:, k0:k0 + len(kts), :]
                        ins = feature_major((c + j) % NS, psm[:, n, :], BOTH, hi_t, lo_t, m == 0, m == 2, kts=kts)
                        ins.then_inc(unit_used, 1)

            for j in range(3):
                hidden(U1_UP + j, 0, G1_UP + j, 0, stream[j % 3], a_ready(1) if j == 0 else None)
            with pe.Fori(1, NF1 // 3) as i:
                for j in range(3):
                    hidden(U1_UP + j, i, G1_UP + j, i * 3, stream[j % 3])
            down(U1_DOWN, G1_DOWN, NF1, 0)
            norm(PS7_NF)

            def two_units(c, g, banks, hi_t, lo_t, ready):
                for n in range(2):
                    split_unit(c + n)
                    bank_free(g + n)
                for k in range(KT):
                    ready(k)
                    for n in range(2):
                        ins = feature_major((c + n) % NS, banks[n], BOTH, hi_t, lo_t, k == 0, k == KT - 1, kts=(k,))
                        if k == KT - 1:
                            ins.then_inc(unit_used, 1)

            def ffn(c, g, bank0, norm_no, h0, p7):
                two_units(c, g, [stream[(bank0 + n) % 3] for n in range(2)], a_hi, a_lo, a_ready(norm_no))
                mean_squares(p7)
                s, bank = (c + 2) % NS, stream[(bank0 + 2) % 3]
                split_unit(c + 2)
                bank_free(g + 2)
                feature_major(s, bank, BOTH[0:1], a_hi, a_lo, True, False)
                inverse_rms()
                feature_major(s, bank, BOTH[1:2], a_hi, a_lo, False, True).then_inc(unit_used, 1)
                hidden(c + 3, 0, g + 3, 0, stream[bank0])
                with pe.Fori(0, (NF2 - 4) // 3) as i:
                    for j in range(4, 7):
                        hidden(c + j, i, g + j, i * 3, stream[(bank0 + j) % 3])
                down(c + NF2, g + NF2, NF2, h0)

            for l in range(LAYERS):
                c0, g0 = U1_END + UL * l, G1_END + GL * l
                psm0, ps70, st0 = PSM_1 + PSM_L * l, PS7_1 + PS7_L * l, ST_1 + ST_L * l
                ffn(c0, g0, 0, 2 + 3 * l, NF1 + NF2 * (2 * l), ps70 + PS7_G0)
                norm(ps70 + PS7_G1)
                norm(ps70 + PS7_G2)
                cm, gm = c0 + UL_MIX, g0 + GL_MIX

                def bank(n):
                    return stream[(BANK_MIX + n) % 3]

                def psm_ready(n):
                    pe.wait_ge(psm_free, psm0 + n)

                def cols(tile, n):
                    return tile[:, n * P:n * P + P]

                split_unit(cm)
                bank_free(gm)
                feature_major(cm % NS, bank(0), BOTH[0:1], a_hi, a_lo, True, True, ready=a_ready(3 + 3 * l)).then_inc(unit_used, 1)
                project(cm + 1, gm + 1, bank(1), a_hi, a_lo)
                pe.wait_ge(group_evac, gm + 1)
                pe.wait_ge(ps7_free, ps70 + PS7_Z)
                for t in range(TT):
                    ins = mm(cols(ps7, t), cols(glr_t[0:17, :], t), w2aug[:, l, :], t == 0, t == 1)
                ins.then_inc(ps7_full, 1)
                project(cm + 2, gm + 2, bank(2), a_hi, a_lo)
                project(cm + 3, gm + 3, bank(3), a_hi, a_lo)
                pe.wait_ge(glog_ready, l + 1)
                psm_ready(0)
                lev = const("lev")
                for t in range(TT):
                    g_t = cols(lg[:, 1, :], t)
                    mm(psm[:, 2 * t, :], g_t, lev[:, 0:4 * P], True, True)
                    mm(psm[:, 2 * t + 1, 0:3 * P], g_t, lev[:, 4 * P:7 * P], True, False)
                    ins = mm(psm[:, 2 * t + 1, 3 * P:4 * P], g_t, cols(lev, 7 + t), False, True)
                ins.then_inc(lev_ready, 1)
                split_unit(cm + 4)
                bank_free(gm + 4)
                feature_major((cm + 4) % NS, bank(4), BOTH[0:1], a_hi, a_lo, True, False)
                token_major((cm + 4) % NS, bank(4), P, P, T, False).then_inc(unit_used, 1)

                def head(tile, h):
                    return tile[GDK * h:GDK * h + GDK]

                def gla_scores(n):
                    t = n // 4
                    psm_ready(PSM_GLA + max(n - 1, 0))
                    pe.wait_ge(ke_ready, TT * l + t + 1)
                    for m in range(4):
                        level = 4 * (n // 2 % 2) + m
                        for h in (2 * (n % 2), 2 * (n % 2) + 1):
                            if level < LEV - 1:
                                k_t, q_t = head(ek[:, 1, t, level, :], h), head(qe[:, t, level, :], h)
                            else:
                                k_t, q_t = head(cols(kg, t), h), head(cols(qg, t), h)
                            ins = mm(psm[:, h, m * P:m * P + P], k_t, q_t, m == 0, m == 3)
                    ins.then_inc(psm_full, 1)

                def window_scores(b):
                    psm_ready(PSM_SWA + b)
                    pe.wait_ge(e_ready, TT * (l + 1))
                    pe.wait_ge(group_evac, gm + 6 + b)
                    for n in range(4):
                        half, j = n % 2, 2 * b + n // 2
                        part = slice(SWD * half, SWD * half + SWD)
                        mm(psm[:, n, 0:T], qs[part, j, P:T], ks[part, :], True, False)
                        ins = mm(psm[:, n, T:384], qs[part, j, 0:P], ks[part, 0:P], False, True)
                    ins.then_inc(psm_full, 1)

                for n in range(2):
                    project(cm + 5 + n, gm + 5 + n, bank(5 + n), a_hi, a_lo)
                    window_scores(n)
                def probabilities(r):
                    for n in range(12 * r, 12 * r + 12):
                        src = cols(ss[:, n // 2, 0:T], n % 2) if n < 2 * SWH else ss[:, n - 2 * SWH, T:384]
                        ins = nc.tensor.transpose(cols(stream[n // 4 % 3], n % 4), src, ident)
                    ins.then_inc(pt_full, 1)

                s = (cm + 7) % NS
                split_unit(cm + 7)
                bank_free(gm + 7)
                token_major(s, bank(7), 0, 256, 0, True, (0,))
                pe.wait_ge(qe_ready, l + 1)
                gla_scores(0)
                gla_scores(1)
                token_major(s, bank(7), 0, 256, 0, True, (1,)).then_inc(unit_used, 1)
                gla_scores(2)
                s = (cm + 8) % NS
                split_unit(cm + 8)
                bank_free(gm + 8)
                feature_major(s, bank(8), BOTH[0:1], a_hi, a_lo, True, False)
                gla_scores(3)
                gla_scores(4)
                feature_major(s, bank(8), BOTH[1:2], a_hi, a_lo, False, True).then_inc(unit_used, 1)
                gla_scores(5)
                gla_scores(6)
                gla_scores(7)
                pe.wait_ge(group_evac, gm + 9)
                pe.wait_ge(p_ready, l + 1)
                probabilities(0)
                pe.wait_ge(pt_free, 2 * l + 1)
                probabilities(1)
                psm_ready(PSM_CROSS)
                for h in range(GH):
                    ins = mm(psm[:, h, 0:P], head(ek[:, 1, 0, LEV - 1, :], h), head(qe[:, 1, LEV - 1, :], h), True, True)
                ins.then_inc(psm_full, 1)

                cbank = stream[(BANK_WOUT + 2) % 3]

                pe.wait_ge(pt_free, 2 * l + 2)
                pe.wait_ge(yc_ready, l + 1)
                for f in range(2):
                    ins = mm(cbank[:, T:2 * T], means[:, 1:2].broadcast_to([P, P]), yc[0][:, f, :], f == 0, f == 1)
                ins.then_inc(conv_full, 1)
                psm_ready(PSM_CROSS + 1)
                pe.wait_ge(ps7_free, ps70 + PS7_PV)
                for h in range(GH):
                    part, f = slice(GDV * (h % 2), GDV * (h % 2) + GDV), h // 2
                    v = slice(GDV * h, GDV * h + GDV)
                    mm(ps7[part, f * T:f * T + P], vg[:, 0, v], s_gla[:, 0, h, :], f == 0, False)
                    mm(ps7[part, f * T + P:f * T + T], vg[:, 1, v], s_gla[:, 1, h, :], False, False)
                    ins = mm(ps7[part, f * T + P:f * T + T], vg[:, 0, v], s_cross[:, h, :], False, f == 1)
                ins.then_inc(ps7_full, 1)
                def window_out(heads):
                    for h in heads:
                        f, part = h // 2, slice(SWD * (h % 2), SWD * (h % 2) + SWD)
                        half, j = h // 4, h % 4
                        slot = 4 * (j // 2) + 2 * (j % 2) + half
                        at = (f % 2) * T
                        v = slice(SWD * half, SWD * half + SWD)
                        mm(psm[part, f // 2, at:at + P], vs[:, 0, v], pt[:, 16 + slot, :], f % 2 == 0, False)
                        for t in range(TT):
                            ins = mm(psm[part, f // 2, at + P:at + T], vs[:, t, v], pt[:, 2 * slot + t, :], False,
                                     f % 2 == 1 and t == 1)
                    return ins

                window_out(range(4))
                pe.wait_ge(og_sq, l + 1)
                pe.wait_ge(ps7_free, ps70 + PS7_GBC)
                for t in range(TT):
                    for f in range(2):
                        at = 4 * t + 2 * f
                        ins = mm(ps7[:, at:at + 2], cols(sq2[:, f, :], t), headsel, at == 0, at == 6)
                ins.then_inc(stat_full, 1)

                pe.wait_ge(yc_sq, l + 1)
                for t in range(TT):
                    for f in range(2):
                        ins = mm(cbank[:, t:t + 1], cols(th2[:, f, :], t), means[:, 1:2], t + f == 0, t + f == 2)
                ins.then_inc(stat_full, 1)
                window_out(range(4, SWH)).then_inc(pv_full, 1)
                pe.wait_ge(rstd8_ready, l + 2)
                for f in range(2):
                    for t in range(TT):
                        for h in range(2):
                            at, part = 4 * t + 2 * f + h, slice(GDV * h, GDV * h + GDV)
                            ins = mm(cols(ps7[part, :], TT * f + t), rstd8[:, at:at + 1].broadcast_to([P, GDV]), ident,
                                     f + t == 0, f + t == 2)
                ins.then_inc(ps7_full, 1)
                pe.wait_ge(conv_rstd, l + 1)
                for t in range(TT):
                    ins = mm(cols(cbank, TT + t), rstd2[:, t:t + 1].broadcast_to([P, P]), ident, t == 0, t == 1)
                ins.then_inc(conv_full, 1)
                def branch_ready(k):
                    pe.wait_ge(op_split, 7 + 3 * l + min(k // 2 + 1, 3))

                two_units(cm + 9, g0 + GL_WOUT, [stream[(BANK_WOUT + n) % 3] for n in range(2)], b_hi, b_lo, branch_ready)
                for n in range(2, 4):
                    project(cm + 9 + n, g0 + GL_WOUT + n, stream[(BANK_WOUT + n) % 3], b_hi, b_lo)
                norm(ps70 + PS7_G3)
                ffn(c0 + UL_UP_B, g0 + GL_UP_B, BANK_UP_B, 4 + 3 * l, NF1 + NF2 * (2 * l + 1), ps70 + PS7_G4)
                norm(ps70 + PS7_G5)
            pe.wait_ge(x_ready, KT * (3 * LAYERS + 1))
            pe.wait_ge(psm_free, PSM_1 + PSM_L * LAYERS)
            for t in range(TT):
                for k in range(KT):
                    n = KT * t + k
                    ins = nc.tensor.transpose(psm[:, n // 4, (n % 4) * P:(n % 4) * P + P], x[:, k, t * P:t * P + P], ident)
            ins.then_inc(psm_full, 1)


def kernel(**inputs):
    import concourse.bacc as bacc
    from concourse.bass_utils import run_bass_kernel_spmd as run

    def rows(name, *index):
        return np.asarray(inputs[name])[index].reshape(-1, P)

    vec_rows = np.zeros((P, 4, VCOL), np.float32)
    for name, src in (("norm1", "norm1_w"), ("gate_b", "merge_gate_b"), ("gn", "ret_gn_w"), ("lconv_w", "lru_conv_w"),
                      ("lconv_b", "lru_conv_b"), ("b_r", "lru_b_r"), ("b_i", "lru_b_i"), ("lam", "lru_lambda"),
                      ("norm2", "norm2_w"), ("norm_f", "norm_f_w")):
        r = rows(src)
        vec_rows[V1[name]:V1[name] + len(r), 0] = r
    for name, src in (("fconv_w", "ffn_conv_w"), ("fconv_b", "ffn_conv_b")):
        r = rows(src)
        vec_rows[V1B[name]:V1B[name] + len(r), 1] = r
    for l in range(LAYERS):
        for name, src in (("norm", "norm_g_2"), ("conv_w", "conv_w_2"), ("conv_b", "conv_b_2"), ("ln_g", "conv_ln_g_2"),
                          ("ln_b", "conv_ln_b_2"), ("gla_g", "gla_norm_g_2")):
            r = rows(src, l)
            vec_rows[VL[name]:VL[name] + len(r), 2 + l] = r
    gate2 = np.concatenate([np.asarray(inputs["gla_w_gate2_2"]), np.asarray(inputs["gla_b_gate_2"])[:, None]], axis=1)
    sink = np.asarray(inputs["swa_sinks_2"]).reshape(LAYERS, 2, 2, 2).transpose(0, 2, 3, 1).reshape(LAYERS, 1, 8)
    sent = {
        "table": TABLE, "masks": MASKS, "vec_rows": vec_rows.reshape(P, -1),
        "gate2": np.ascontiguousarray(gate2.transpose(1, 0, 2)).reshape(17, -1),
        "sink_row": np.ascontiguousarray(np.concatenate([sink, sink], axis=1)).reshape(1, -1),
    }
    for name in ("x", "positions", "w_in", "w_ret_o", "lru_w_r", "lru_w_i", "w_lru_o", "w_out", "ffn_w_up", "ffn_w_down",
                 "ffn_w_gate_2", "ffn_w_up_2", "ffn_w_down_2", "w_in_2", "w_out_2"):
        sent[name] = np.ascontiguousarray(inputs[name])
    nc = bacc.Bacc("TRN2", target_bir_lowering=False, num_devices=1)
    io = {name: nc.dram_tensor(f"in_{name}", a.shape, mybir.dt.from_np(a.dtype), kind="ExternalInput").ap()
          for name, a in sent.items()}
    out = nc.dram_tensor("out", (1, T, D), F32, kind="ExternalOutput").ap()
    build(nc, io, out)
    result = run(nc, [{f"in_{name}": a for name, a in sent.items()}], core_ids=[0])
    return result.results[0]["out"]
```

```python
from contextlib import ExitStack

import numpy as np
import concourse.bass as bass
from concourse import mybir

F32 = mybir.dt.float32
F32R = mybir.dt.float32r
I32 = mybir.dt.int32
U8 = mybir.dt.uint8
ACT = mybir.ActivationFunctionType
ALU = mybir.AluOpType
AX = mybir.AxisListType.X

P = 128
T = 256
TT = T // P
D = 1024
KT = D // P
UC = 256
FT = UC // P
NS = 3
HEADS, DK, DV, CH = 4, 128, 256, 64
DFF1, DFF2 = 3072, 2816
NF1, NF2 = DFF1 // P, DFF2 // P
LAYERS = 2
SWH, SWD = 8, 64
GH, GDK, GDV = 4, 32, 64
TAPS = 31
TAPS_DVE = 9
LEV = 8
RMS_EPS = 1e-6
LN_EPS = 1e-5
SQ2PI = 0.7978845608028654
GELU_C = 0.044715
MAGIC = 12582912.0

U1_RG = 20
U1_GATES = 22
U1_RETO = 30
U1_LRUO = 34
U1_OUT = 38
U1_UP = 42
U1_DOWN = U1_UP + NF1
U1_END = U1_DOWN + 12
UL_MIX = NF2 + 12
UL_WOUT = UL_MIX + 9
UL_UP_B = UL_WOUT + 4
UL_DOWN_B = UL_UP_B + NF2
UL = UL_DOWN_B + 12
G1_RG = 20
G1_GATES = 28
G1_RETO = 36
G1_LRUO = 40
G1_OUT = 44
G1_UP = 48
G1_DOWN = G1_UP + NF1
G1_END = G1_DOWN + 4
GL_MIX = NF2 + 4
GL_WOUT = GL_MIX + 9
GL_UP_B = GL_WOUT + 4
GL_DOWN_B = GL_UP_B + NF2
GL = GL_DOWN_B + 4
TOTAL_UNITS = U1_END + LAYERS * UL
QUERY_UNITS = [U1_END + UL * l + UL_MIX + 5 + n for l in range(LAYERS) for n in range(2)]

PSM_SC, PSM_O, PSM_MEAN, PSM_VAR, PSM_1 = range(5)
(PSM_SWA, PSM_GLA, PSM_CROSS, PSM_L) = (0, 2, 10, 11)
PS7_N0, PS7_SINK, PS7_N1, PS7_NF, PS7_1 = range(5)
(PS7_G0, PS7_G1, PS7_G2, PS7_Z, PS7_PV, PS7_GBC, PS7_G3, PS7_G4, PS7_G5, PS7_L) = range(10)
ST_RMEAN, ST_RVAR, ST_N1, ST_NF, ST_1 = range(5)
(ST_G0, ST_G1, ST_G2, ST_GLA, ST_CVAR, ST_G3, ST_G4, ST_G5, ST_L) = range(9)
BANK_MIX, BANK_WOUT, BANK_UP_B = NF2 % 3, (NF2 + 9) % 3, (NF2 + 13) % 3

VCOL = 128
V1 = {"norm1": 0, "gate_b": 8, "gn": 24, "lconv_w": 32, "lconv_b": 64, "b_r": 72, "b_i": 80, "lam": 88,
      "norm2": 96, "norm_f": 104}
V1B = {"fconv_w": 0, "fconv_b": 72}
VL = {"norm": 0, "conv_w": 48, "conv_b": 110, "ln_g": 112, "ln_b": 114, "gla_g": 116}


def tables():
    t = {}
    a = np.arange(P)
    t["ident"] = np.eye(P)
    t["means"] = np.stack([np.full(P, 1 / D), np.full(P, 1 / 256)], axis=1)
    t["headsel"] = np.stack([a < 64, a >= 64], axis=1) / 64.0
    t["invf"] = np.power(np.float32(10000.0), -(a % 64).astype(np.float32) / np.float32(64))[:, None]
    t["sgn"] = np.where(a < 64, -1.0, 1.0)[:, None]
    lev = np.zeros((9, P, P))
    mask = np.zeros((LEV, P, P))
    for n in range(LEV - 1):
        m = P >> n
        mid = (a // m) * m + m // 2 - 1
        after = (a[:, None] > mid[None, :]) & (a[:, None] <= a[None, :])
        before = (a[:, None] > a[None, :]) & (a[:, None] <= mid[None, :])
        lev[n] = after | before
        mask[n] = ((a[:, None] // m) == (a[None, :] // m)) & (a[:, None] <= mid[None, :]) & (a[None, :] > mid[None, :])
    lev[7] = a[:, None] > a[None, :]
    lev[8] = a[:, None] <= a[None, :]
    mask[LEV - 1] = np.eye(P)
    t["lev"] = (lev / 16.0).transpose(1, 0, 2).reshape(P, -1)
    d = a[:, None] - np.arange(T)[None, :] + P
    alibi = np.where((d >= 0) & (d < P), -d, -1e30)
    t["alibi"] = np.concatenate([alibi, alibi[:, P:]], axis=1)
    i = np.arange(T)
    log_gamma = np.log1p(-np.power(2.0, -5.0 - np.arange(HEADS)))
    seen = (i[:, None] // CH) <= (i[None, :] // CH)
    dec = np.exp(log_gamma[:, None, None] * np.abs(i[:, None] - i[None, :])) * seen * DK ** -0.5
    t["ret"] = np.concatenate([dec[:, :P, :], dec[:, P:, P:]], axis=2).transpose(1, 0, 2).reshape(P, -1)
    names, at, parts = {}, 0, []
    for k, v in t.items():
        names[k] = (at, at + v.shape[1])
        at += v.shape[1]
        parts.append(v.astype(np.float32))
    return names, np.concatenate(parts, axis=1), mask.transpose(1, 0, 2).reshape(P, -1).astype(np.float32)


COLS, TABLE, MASKS = tables()
NKEEP = COLS["alibi"][1]
NFIRST = COLS["lev"][0]


def after(eng, s, n, e=0):
    if not isinstance(e, int):
        eng.wait_ge(s, e + n)
    elif n + e > 0:
        eng.wait_ge(s, n + e)


def build(nc, io, out):
    with ExitStack() as ctx:
        def sb(name, shape, dt=F32, scope=ctx):
            return scope.enter_context(nc.sbuf_tensor(name, shape, dt))

        def sem(name):
            return ctx.enter_context(nc.semaphore(name))

        x = sb("x", [P, KT, T])
        hn = sb("hn", [P, KT, T])
        sq = sb("sq", [P, KT, T])
        a_hi, a_lo = sb("a_hi", [P, KT, T], F32R), sb("a_lo", [P, KT, T], F32R)
        b_hi, b_lo = sb("b_hi", [P, KT, T], F32R), sb("b_lo", [P, KT, T], F32R)
        raw = [sb(f"raw{s}", [P, KT, UC]) for s in range(NS)]
        w_hi = [sb(f"w_hi{s}", [P, KT, UC], F32R) for s in range(NS)]
        w_lo = [sb(f"w_lo{s}", [P, KT, UC], F32R) for s in range(NS)]
        keep = sb("keep", [P, NKEEP])

        def const(name):
            return keep[:, COLS[name][0]:COLS[name][1]]

        ident, means, headsel = const("ident"), const("means"), const("headsel")
        masks = sb("masks", [P, LEV, P], U8)
        vecs = sb("vecs", [P, 4, VCOL])
        var2, rstd2 = sb("var2", [P, 2]), sb("rstd2", [P, 2])
        var8, rstd8 = sb("var8", [P, 8]), sb("rstd8", [P, 8])
        rb = sb("rb", [P, T])
        mhalf = sb("mhalf", [P, 1])
        ms2 = sb("ms2", [P, 2])
        ones_row = sb("ones_row", [1, P])
        sink_row = sb("sink_row", [1, LAYERS * 16])
        sinks = sb("sinks", [P, LAYERS, 16])
        glr_t = sb("glr_t", [32, T])
        w2aug = sb("w2aug", [17, LAYERS, P])

        m1 = ExitStack()
        ret_d = sb("ret_d", [P, HEADS, 384], scope=m1)
        cos2, sin2 = sb("cos2", [P, T], scope=m1), sb("sin2", [P, T], scope=m1)
        e_xl = sb("e_xl", [P, KT, T + 3], scope=m1)
        e2, e3, e4, e5, e6, e7 = (sb(f"e{n}", [P, KT, T], scope=m1) for n in range(2, 8))
        half_b = sb("half_b", [P, 40], scope=m1)
        sp4 = sb("sp4", [P, 8], scope=m1)
        sp_t = sb("sp_t", [P, 6, 8], scope=m1)
        m1.close()
        x_in, x_scrap, x_out = (tile[:, :, :].rearrange("p (t a) n -> p t (a n)", t=TT) for tile in (hn, e3, sq))
        qk_raw, qk_sw, qk_rot = e_xl[:, :, 0:T], e2, e3
        xl, xc, la = e_xl, e2, e_xl[:, :, 3:T + 3]
        o_ret, g_ret, y_lru, i_gate = e5, e6, e7, e3
        h_lru, a_sq, ga, gb, gel, a_lru = e5, e6, e4, hn, hn, sq
        v_ret = e4[:, :, :].rearrange("p (t a) n -> p t (a n)", t=TT)
        st_ret = sq[:, :, :].rearrange("p a b -> p (a b)")
        masks_f32 = e7[:, 0:4, :].rearrange("p k n -> p (k n)")
        pos_i, ang_t, ang = e4[:, 0, :].bitcast(I32), e5, e6

        ff = ExitStack()
        h_hi, h_lo = sb("h_hi", [P, NF1, T], F32R, scope=ff), sb("h_lo", [P, NF1, T], F32R, scope=ff)
        th, hb, ab = (sb(n, [P, NS, T], scope=ff) for n in ("th", "hb", "ab"))
        gu = sb("gu", [P, NS, 2, T], scope=ff)
        ff.close()

        m2 = ExitStack()
        ek = sb("ek", [P, 2, TT, LEV, P], scope=m2)
        qg, kg = sb("qg", [P, T], scope=m2), sb("kg", [P, T], scope=m2)
        vg = sb("vg", [P, TT, 256], scope=m2)
        s_gla = sb("s_gla", [P, TT, GH, P], scope=m2)
        s_cross = sb("s_cross", [P, GH, P], scope=m2)
        pt = sb("pt", [P, 24, P], scope=m2)
        vs = sb("vs", [P, TT, P], scope=m2)
        ss = sb("ss", [P, SWH, 384], scope=m2)
        mx = sb("mx", [P, 4, 16], scope=m2)
        up = sb("up", [P, 2, T + TAPS - 1], scope=m2)
        yc = [sb(f"yc{n}", [P, 2, T], scope=m2) for n in range(2)]
        gr, og, th2, sq2 = (sb(n, [P, 2, T], scope=m2) for n in ("gr", "og", "th2", "sq2"))
        m2.close()
        cg, cub = gu[:, :, 0, :], gu[:, :, 1, :]
        qe = sq[:, :, :].rearrange("p (t a) (b i) -> p t (a b) i", t=TT, b=2)
        lg, qs, ca, ks = (pt[:, a:a + 2 * n, :].rearrange("p (n b) i -> p n (b i)", b=2)
                          for a, n in ((0, 5), (10, 4), (18, 2), (22, 1)))
        ks = ks[:, 0, :]
        y_pool, y_tap = hn[:, 4, :], hn[:, 5:7, :]

        stream = [ctx.enter_context(nc.psum_tensor(f"stream{n}", [P, 512], F32)) for n in range(3)]
        psm = ctx.enter_context(nc.psum_tensor("psm", [P, 4, 512], F32))
        ps7 = ctx.enter_context(nc.psum_tensor("ps7", [P, 512], F32))

        raw_loaded = [sem(f"raw_loaded{s}") for s in range(NS)]
        w_hi_ready, w_split, unit_used = sem("w_hi_ready"), sem("w_split"), sem("unit_used")
        rg_done, group_evac = sem("rg_done"), sem("group_evac")
        psm_full, psm_free, ps7_full, ps7_free, stat_full = (sem(n) for n in (
            "psm_full", "psm_free", "ps7_full", "ps7_free", "stat_full"))
        x_loaded, ident_loaded, vecs_loaded, small_loaded, late_loaded = (sem(n) for n in (
            "x_loaded", "ident_loaded", "vecs_loaded", "small_loaded", "late_loaded"))
        x_turned, x_stat, vecs_turned, out_turned, out_ready, out_stored = (sem(n) for n in (
            "x_turned", "x_stat", "vecs_turned", "out_turned", "out_ready", "out_stored"))
        pool_init, dve_chain, act_chain = sem("pool_init"), sem("dve_chain"), sem("act_chain")
        sq_sum = sem("sq_sum")
        x_ready, sq_ready, var_ready, rstd_ready, normed, a_hi_ready, a_split = (sem(n) for n in (
            "x_ready", "sq_ready", "var_ready", "rstd_ready", "normed", "a_hi_ready", "a_split"))
        mean_ready, var8_ready, rstd8_ready = sem("mean_ready"), sem("var8_ready"), sem("rstd8_ready")
        op_ready, op_hi_ready, op_split = sem("op_ready"), sem("op_hi_ready"), sem("op_split")
        hb_ready = sem("hb_ready")
        th_ready, h_hi_ready, h_split, tap_ready, conv_done, csq_ready, cube_ready = (sem(n) for n in (
            "th_ready", "h_hi_ready", "h_split", "tap_ready", "conv_done", "csq_ready", "cube_ready"))
        ang_ready, trig_ready, swapped, rot_done, act_gate, lam_arg, lam_exp, lru_conv0, lru_act = (sem(n) for n in (
            "ang_ready", "trig_ready", "swapped", "rot_done", "act_gate", "lam_arg", "lam_exp", "lru_conv0", "lru_act"))
        o_sq, ge_sq, ge_cube, ge_th, ge_done, v_ready, sqrt_done = (sem(n) for n in (
            "o_sq", "ge_sq", "ge_cube", "ge_th", "ge_done", "v_ready", "sqrt_done"))
        ez_ready, glog_ready, lev_ready, e_ready, qe_ready, ke_ready, zeroed, gate_ready = (sem(n) for n in (
            "ez_ready", "glog_ready", "lev_ready", "e_ready", "qe_ready", "ke_ready", "zeroed", "gate_ready"))
        sums_ready, pv_full, pt_full, pt_free = (sem(n) for n in ("sums_ready", "pv_full", "pt_full", "pt_free"))
        conv_full, centred, centred_var, conv_rstd = (sem(n) for n in (
            "conv_full", "centred", "centred_var", "conv_rstd"))
        og_sq, yc_ready, yc_sq, silu_in, silu_th, glu_th, gr_th = (sem(n) for n in (
            "og_sq", "yc_ready", "yc_sq", "silu_in", "silu_th", "glu_th", "gr_th"))
        up_ready, tap_product, tap_sum, ss_ready, ss_exp, p_ready = (sem(n) for n in (
            "up_ready", "tap_product", "tap_sum", "ss_ready", "ss_exp", "p_ready"))
        N_SMALL, N_LATE = 3, 3

        def rows(ap, r0=0, n=KT):
            return ap[r0:r0 + n * P, :].rearrange("(k p) n -> p k n", p=P)

        def pair2(bank):
            return bank.rearrange("p (a b) -> p a b", a=2)

        block = ctx.enter_context(nc.Block())

        @block.sync
        def _(sp):
            def fill(c, e, halves):
                s = c % NS
                if not (isinstance(e, int) and c + NS * e < NS):
                    after(sp, w_split, c - NS + 1, e * NS)
                for dst, src in halves(raw[s]):
                    sp.dma_start(dst, src).then_inc(raw_loaded[s], 16)

            def plain(src, n=KT):
                return lambda r: [(r[:, 0:4, :], src[:, 0:4, :]), (r[:, 4:n, :], src[:, 4:n, :])]

            def pair(first, second):
                return lambda r: [(r[:, :, 0:P], first), (r[:, :, P:UC], second)]

            def interleaved(first, second):
                return lambda r: [(r[:, :, SWD * (2 * j + g):SWD * (2 * j + g) + SWD], src[:, :, SWD * j:SWD * j + SWD])
                                  for j in range(2) for g, src in enumerate((first, second))]

            sp.dma_start(x_in, io["x"][0].rearrange("(t p) d -> p t d", p=P)).then_inc(x_loaded, 16)
            w_in = rows(io["w_in"][0])
            cols = [at + UC * i for at, m in ((0, 2), (512, 2), (1024, 4), (3072, 4), (4096, 4), (2048, 4))
                    for i in range(m)]
            c = 0
            for col in cols:
                fill(c, 0, plain(w_in[:, :, col:col + UC]))
                c += 1
            for name in ("lru_w_r", "lru_w_i"):
                fill(c, 0, plain(io[name][0].rearrange("b (k p) n -> p (b k) n", p=P)))
                c += 1
            for i in range(8):
                fill(c, 0, plain(w_in[:, :, 5120 + UC * i:5120 + UC * i + UC]))
                c += 1
            for name in ("w_ret_o", "w_lru_o", "w_out"):
                for i in range(4):
                    fill(c, 0, plain(rows(io[name][0])[:, :, UC * i:UC * i + UC]))
                    c += 1
            w_up = rows(io["ffn_w_up"][0])
            with sp.Fori(0, NF1 // 3) as i:
                for j in range(3):
                    fill(U1_UP + j, i, pair(w_up[:, :, bass.ds(i * (3 * P) + j * P, P)],
                                            w_up[:, :, bass.ds(i * (3 * P) + (j * P + DFF1), P)]))
            with sp.Fori(0, 2) as i:
                for j in range(6):
                    src = rows(io["ffn_w_down"][0], KT * P * (j % 3))
                    fill(U1_DOWN + j, i * 2, plain(src[:, :, bass.ds(i * 512 + UC * (j // 3), UC)]))

            def ffn(c, l, f):
                g_rows, u_rows = rows(io["ffn_w_gate_2"][l, f]), rows(io["ffn_w_up_2"][l, f])
                fill(c, 0, pair(g_rows[:, :, 0:P], u_rows[:, :, 0:P]))
                with sp.Fori(0, (NF2 - 1) // 3) as i:
                    for j in range(3):
                        at = bass.ds(i * (3 * P) + (j + 1) * P, P)
                        fill(c + 1 + j, i, pair(g_rows[:, :, at], u_rows[:, :, at]))
                with sp.Fori(0, 2) as i:
                    for j in range(6):
                        n = min(KT, NF2 - KT * (j % 3))
                        src = rows(io["ffn_w_down_2"][l, f], KT * P * (j % 3), n)
                        fill(c + NF2 + j, i * 2, plain(src[:, :, bass.ds(i * 512 + UC * (j // 3), UC)], n))

            for l in range(LAYERS):
                c0 = U1_END + UL * l
                ffn(c0, l, 0)
                c = c0 + UL_MIX
                wi = rows(io["w_in_2"][l])
                fill(c, 0, lambda r: [(r[:, 0:4, 0:P], wi[:, 0:4, 768:768 + P]), (r[:, 4:8, 0:P], wi[:, 4:8, 768:768 + P])])
                for n, col in enumerate((0, 784, 1040, 1808)):
                    fill(c + 1 + n, 0, plain(wi[:, :, col:col + UC]))
                for n in range(2):
                    col = 1296 + P * n
                    fill(c + 5 + n, 0, interleaved(wi[:, :, col:col + P], wi[:, :, col + 256:col + 256 + P]))
                for n, col in enumerate((256, 512)):
                    fill(c + 7 + n, 0, plain(wi[:, :, col:col + UC]))
                for n in range(4):
                    fill(c + 9 + n, 0, plain(rows(io["w_out_2"][l])[:, :, UC * n:UC * n + UC]))
                ffn(c0 + UL_UP_B, l, 1)
            for g in range(4):
                cols = slice(UC * g, UC * g + UC)
                sp.wait_ge(out_ready, g + 1)
                sp.dma_start(out[0].rearrange("(t p) d -> p t d", p=P)[:, :, cols], x_out[:, :, cols]).then_inc(out_stored, 16)
            sp.wait_ge(out_stored, 4 * 16)

        @block.gpsimd
        def _(pool):
            done = {"norm": 0, "head": 0}
            nc.gpsimd.memset(mhalf[:, :], -0.5).then_inc(pool_init, 1)
            nc.gpsimd.memset(ones_row[:, :], 1.0).then_inc(pool_init, 1)
            nc.gpsimd.memset(glr_t[:, :], 1.0).then_inc(pool_init, 1)
            pool.wait_ge(pool_init, 3)

            def power_norm():
                for k in range(1, 6):
                    pool.wait_ge(sq_ready, KT * done["norm"] + k + 1)
                    if k > 1:
                        pool.wait_ge(sq_sum, 5 * done["norm"] + k - 1)
                    nc.gpsimd.tensor_tensor(sq[:, 0, :], sq[:, 0, :], sq[:, k, :], ALU.add).then_inc(sq_sum, 1)
                done["norm"] += 1
                inverse_root()

            def inverse_root():
                pool.wait_ge(var_ready, done["norm"] + 1)
                nc.gpsimd.tensor_tensor(rstd2[:, :], var2[:, :], mhalf[:, 0:1].broadcast_to([P, 2]),
                                        ALU.pow).then_inc(rstd_ready, 1)

            def power_heads(n):
                done["head"] += 1
                pool.wait_ge(var8_ready, done["head"])
                nc.gpsimd.tensor_tensor(rstd8[:, 0:n], var8[:, 0:n], mhalf[:, 0:1].broadcast_to([P, n]),
                                        ALU.pow).then_inc(rstd8_ready, 1)

            inverse_root()
            power_heads(8)
            power_norm()
            power_norm()
            for l in range(LAYERS):
                power_norm()
                power_norm()
                power_norm()
                g_mix = G1_END + GL * l + GL_MIX
                pool.wait_ge(group_evac, g_mix)
                nc.gpsimd.memset(s_gla[:, :, :, :], 0.0).then_inc(zeroed, 1)
                nc.gpsimd.memset(up[:, :, 0:TAPS - 1], 0.0).then_inc(zeroed, 1)
                for t in range(TT):
                    pool.wait_ge(group_evac, g_mix + 2)
                    pool.wait_ge(e_ready, TT * l + t + 1)
                    nc.gpsimd.tensor_tensor(
                        ek[:, 1, t], ek[:, 0, t],
                        kg[:, t * P:t * P + P].rearrange("p (o i) -> p o i", o=1).broadcast_to([P, LEV, P]),
                        ALU.mult).then_inc(ke_ready, 1)
                pool.wait_ge(up_ready, l + 1)
                products, sums = (TAPS - TAPS_DVE) * l, (TAPS - TAPS_DVE - 1) * l
                for n in range(TAPS - TAPS_DVE):
                    tap = TAPS_DVE + n
                    at = VL["conv_w"] + 2 * tap + 1
                    dst = y_tap[:, n % 2, :] if n else y_pool
                    if n > 2:
                        pool.wait_ge(tap_sum, sums + n - 2)
                    nc.gpsimd.tensor_tensor(dst, up[:, 1, tap:tap + T], vecs[:, 2 + l, at:at + 1].broadcast_to([P, T]),
                                            ALU.mult).then_inc(tap_product, 1)
                    if n:
                        pool.wait_ge(tap_product, products + n + 1)
                        if n > 1:
                            pool.wait_ge(tap_sum, sums + n - 1)
                        nc.gpsimd.tensor_tensor(y_pool, y_pool, dst, ALU.add).then_inc(tap_sum, 1)
                power_heads(8)
                pool.wait_ge(centred_var, l + 1)
                nc.gpsimd.tensor_tensor(rstd2[:, :], var2[:, :], mhalf[:, 0:1].broadcast_to([P, 2]),
                                        ALU.pow).then_inc(conv_rstd, 1)
                power_norm()
                power_norm()
                power_norm()

        @block.scalar
        def _(act):
            count = {"chain": 0, "normed": 0}

            def link(ins):
                count["chain"] += 1
                ins.then_inc(act_chain, 1)
                act.wait_ge(act_chain, count["chain"])

            def hi(c, e=0):
                if isinstance(e, int) and c + NS * e >= TOTAL_UNITS:
                    return
                s = c % NS
                queries = sum(q <= c and q % NS == s for q in QUERY_UNITS)
                after(act, raw_loaded[s], 32 * (c // NS + 1 + queries), e * 32)
                if not (isinstance(e, int) and c + NS * e < NS):
                    after(act, unit_used, c - NS + 1, e * NS)
                nc.scalar.activation(w_hi[s][:, :, :], raw[s][:, :, :], ACT.Copy).then_inc(w_hi_ready, 1)

            def squares(src, tiles=range(KT)):
                for k in tiles:
                    nc.scalar.activation(sq[:, k, :], src[:, k, :], ACT.Square).then_inc(sq_ready, 1)

            def bank_squares(unit, bank, n):
                act.wait_ge(unit_used, unit + 1)
                for f in range(FT):
                    nc.scalar.activation(sq[:, FT * n + f, :], bank[:, f * T:f * T + T], ACT.Square).then_inc(sq_ready, 1)

            def x_hi(n, group, col):
                for k in range(KT):
                    act.wait_ge(x_ready, KT * n + k + 1)
                    nc.scalar.activation(a_hi[:, k, :], x[:, k, :], ACT.Identity,
                                         scale=vecs[:, group, col + k:col + k + 1]).then_inc(a_hi_ready, 1)
                    squares(x, (k,))

            def norm_hi():
                for k in range(KT):
                    count["normed"] += 1
                    act.wait_ge(normed, count["normed"])
                    nc.scalar.activation(a_hi[:, k, :], hn[:, k, :], ACT.Copy).then_inc(a_hi_ready, 1)

            def operand_hi(dst, src, ready, used=0):
                act.wait_ge(*ready)
                after(act, unit_used, used)
                nc.scalar.activation(dst, src, ACT.Copy).then_inc(op_hi_ready, 1)

            def op(n):
                return op_ready, n

            act.dma_start(keep[:, 0:NFIRST], io["table"][:, 0:NFIRST]).then_inc(ident_loaded, 16)
            act.dma_start(sq[:, 0:2, :].rearrange("p a b -> p (a b)"), io["vec_rows"]).then_inc(vecs_loaded, 16)
            act.dma_start(pos_i, io["positions"].broadcast_to([P, T])).then_inc(small_loaded, 16)
            act.dma_start(sink_row[:, :], io["sink_row"]).then_inc(small_loaded, 16)
            act.dma_start(w2aug[:, :, :].rearrange("p l n -> p (l n)"), io["gate2"]).then_inc(small_loaded, 16)

            act.wait_ge(x_loaded, 16)
            for t in range(TT):
                nc.scalar.activation(x_scrap[:, t, :], x_in[:, t, :], ACT.Square,
                                     accum_out=ms2[:, t:t + 1]).then_inc(x_stat, 1)
            act.dma_start(ret_d[:, :, :].rearrange("p h n -> p (h n)"),
                          io["table"][:, COLS["ret"][0]:COLS["ret"][1]]).then_inc(late_loaded, 16)
            act.dma_start(masks_f32, io["masks"]).then_inc(late_loaded, 16)
            act.dma_start(keep[:, NFIRST:NKEEP], io["table"][:, NFIRST:NKEEP]).then_inc(late_loaded, 16)
            hi(0)
            norm_hi()
            hi(1)
            for u in range(4):
                hi(u + 2)
                act.wait_ge(unit_used, u + 1)
                for half in range(2):
                    to, of = 64 * half, 64 * (1 - half)
                    nc.scalar.activation(qk_sw[to:to + 64, 2 * u:2 * u + 2, :], pair2(stream[u % 3][of:of + 64, :]),
                                         ACT.Copy).then_inc(swapped, 1)
            act.wait_ge(ang_ready, 1)
            nc.scalar.activation(sin2[:, :], ang[:, 0, :], ACT.Sin, scale=const("sgn")).then_inc(trig_ready, 1)
            act.wait_ge(ang_ready, 2)
            nc.scalar.activation(cos2[:, :], ang[:, 1, :], ACT.Sin).then_inc(trig_ready, 1)
            for u in range(4, 12):
                hi(u + 2)
                if u == 8:
                    act.wait_ge(lam_arg, 1)
                    nc.scalar.activation(sp_t[:, 1, :], sp_t[:, 0, :], ACT.Exp, scale=-1.0).then_inc(lam_exp, 1)
            act.wait_ge(group_evac, 12)
            act.wait_ge(rot_done, 1)
            for k in range(KT):
                nc.scalar.activation(xc[:, k, :], xl[:, k, 3:3 + T], ACT.Identity,
                                     bias=vecs[:, 0, V1["lconv_b"] + k:V1["lconv_b"] + k + 1],
                                     scale=vecs[:, 0, V1["lconv_w"] + 24 + k:V1["lconv_w"] + 25 + k]).then_inc(lru_conv0, 1)
            for u in range(12, 16):
                hi(u + 2)
            operand_hi(b_hi[:, :, :], xc[:, :, :], op(1))
            act.wait_ge(psm_free, PSM_MEAN + 1)
            nc.scalar.activation(sq[:, :, :], o_ret[:, :, :], ACT.Square).then_inc(o_sq, 1)
            for n in range(4):
                u = 16 + n
                hi(u + 2)
                act.wait_ge(unit_used, u + 1)
                nc.scalar.activation(g_ret[:, 2 * n:2 * n + 2, :], pair2(stream[u % 3][:, :]), ACT.Tanh,
                                     scale=0.5).then_inc(act_gate, 1)
            act.wait_ge(group_evac, 16)
            nc.scalar.activation(gel[:, :, :], y_lru[:, :, :], ACT.Square).then_inc(ge_sq, 1)
            for n in range(8):
                if n % 4 == 2:
                    hi(U1_RG + n // 4 + 2)
                g = G1_RG + n
                if n % 4 < 3:
                    act.wait_ge(rg_done, 3 * (n // 4) + n % 4 + 1)
                else:
                    act.wait_ge(unit_used, U1_RG + n // 4 + 1)
                dst = la if n < 4 else i_gate
                for f in range(2):
                    k = 2 * (n % 4) + f
                    col = 8 * (n // 4) + k
                    nc.scalar.activation(dst[:, k, :], stream[g % 3][:, f * T:f * T + T], ACT.Tanh,
                                         bias=half_b[:, col:col + 1], scale=0.5).then_inc(act_gate, 1)
            act.wait_ge(group_evac, G1_RG + 4)
            nc.scalar.activation(a_lru[:, :, :], la, ACT.Exp).then_inc(lru_act, 1)
            nc.scalar.activation(la, la, ACT.Tanh).then_inc(lru_act, 1)
            for n in range(8):
                hi(U1_GATES + n + 2)
                g = G1_GATES + n
                act.wait_ge(unit_used, U1_GATES + n + 1)
                if n == 4:
                    act.wait_ge(ge_done, 1)
                dst = ga if n < 4 else gb
                for f in range(2):
                    k = 2 * (n % 4) + f
                    col = 16 + 8 * (n // 4) + k
                    nc.scalar.activation(dst[:, k, :], stream[g % 3][:, f * T:f * T + T], ACT.Tanh,
                                         bias=half_b[:, col:col + 1], scale=0.5).then_inc(act_gate, 1)
                if n == 0:
                    act.wait_ge(ge_cube, 1)
                    nc.scalar.activation(gel[:, :, :], gel[:, :, :], ACT.Tanh, scale=SQ2PI * GELU_C).then_inc(ge_th, 1)
                    operand_hi(b_hi[:, :, :], o_ret[:, :, :], op(2), U1_GATES)
                    act.wait_ge(lru_act, 1)
                    nc.scalar.activation(a_sq[:, :, :], a_lru[:, :, :], ACT.Square).then_inc(lru_act, 1)
                if n == 4:
                    act.wait_ge(v_ready, 1)
                    nc.scalar.activation(la, la, ACT.Sqrt).then_inc(sqrt_done, 1)
            for n in range(8):
                hi(U1_RETO + n + 2)
                if n == 0:
                    operand_hi(a_hi[:, :, :], y_lru[:, :, :], op(3), U1_RETO)
                if n >= 4:
                    m = n - 4
                    operand_hi(b_hi[:, 2 * m:2 * m + 2, :], ga[:, 2 * m:2 * m + 2, :], op(4 + m), U1_LRUO)
            for n in range(4):
                hi(U1_OUT + n + 2)
                act.wait_ge(group_evac, G1_OUT + n + 1)
                squares(x, (2 * n, 2 * n + 1))
            norm_hi()

            def hidden_hi(j, e3, ready, before):
                after(act, ready, before + j + 1, e3)
                dst = h_hi[:, j, :] if isinstance(e3, int) else h_hi[:, bass.ds(e3 + j, 1), :].rearrange("p o n -> p (o n)")
                nc.scalar.activation(dst, hb[:, j % 3, :], ACT.Copy).then_inc(h_hi_ready, 1)

            def ff1_step(j, e, e3):
                def col(name, extra):
                    at = V1B[name] + extra + j
                    return vecs[:, 1, at:at + 1] if isinstance(e3, int) else vecs[:, 1, bass.ds(e3 + at, 1)]

                after(act, unit_used, U1_UP + j + 1, e3)
                nc.scalar.activation(cg[:, j % 3, :], stream[j % 3][:, 0:T], ACT.Identity, bias=col("fconv_b", 0),
                                     scale=col("fconv_w", 2 * NF1)).then_inc(tap_ready, 1)
                before = j or not isinstance(e3, int)
                if before:
                    gelu_tanh(j - 1, e3)
                hi(U1_UP + j + 3, e)
                after(act, conv_done, j + 1, e3)
                nc.scalar.activation(cub[:, j % 3, :], cg[:, j % 3, :], ACT.Square).then_inc(csq_ready, 1)
                if before:
                    hidden_hi(j - 1, e3, group_evac, G1_UP)

            def gelu_tanh(j, e3):
                after(act, cube_ready, j + 1, e3)
                nc.scalar.activation(th[:, j % 3, :], cub[:, j % 3, :], ACT.Tanh, scale=SQ2PI * GELU_C).then_inc(th_ready, 1)

            hi(U1_UP + 2)
            for j in range(3):
                ff1_step(j, 0, 0)
            with act.Fori(1, NF1 // 3) as i:
                for j in range(3):
                    ff1_step(j, i, i * 3)
            gelu_tanh(NF1 - 1, 0)
            hidden_hi(NF1 - 1, 0, group_evac, G1_UP)
            for n in range(4):
                for m in range(3 if n < 3 else 2):
                    hi(U1_DOWN + 3 * n + m + 3)
                act.wait_ge(group_evac, G1_DOWN + n + 1)
                squares(x, (2 * n, 2 * n + 1))

            def ffn(c0, g0, b0):
                def unit(j, e, e3):
                    after(act, group_evac, g0 + j + 1, e3)
                    nc.scalar.activation(th[:, j % 3, :], gu[:, j % 3, 0, :], ACT.Tanh, scale=0.5).then_inc(th_ready, 1)
                    if j:
                        hi(c0 + j + 3, e)
                    hidden_hi(j, e3, hb_ready, b0)

                hi(c0 + 2)
                hi(c0 + 3)
                for j in range(4):
                    unit(j, 0, 0)
                with act.Fori(0, (NF2 - 4) // 3) as i:
                    for j in range(4, 7):
                        unit(j, i, i * 3)
                for n in range(4):
                    for m in range(3 if n < 3 else 2):
                        hi(c0 + NF2 + 3 * n + m + 3)
                    bank_squares(c0 + NF2 + 3 * n + 2, psm[:, n % 2, :], n)

            for l in range(LAYERS):
                c0, g0 = U1_END + UL * l, G1_END + GL * l
                ps70, op0 = PS7_1 + PS7_L * l, 7 + 2 * l
                x_hi(3 * l, 2 + l, 0)
                ffn(c0, g0, 2 * l * NF2)
                x_hi(3 * l + 1, 2 + l, 16)
                cm, gm = c0 + UL_MIX, g0 + GL_MIX

                def bank(n):
                    return stream[(BANK_MIX + n) % 3]

                hi(cm + 2)
                hi(cm + 3)
                act.wait_ge(ps7_full, ps70 + PS7_Z + 1)
                link(nc.scalar.activation(lg[:, 0, :], ps7[:, 0:T], ACT.Abs))
                nc.scalar.activation(lg[:, 0, :], lg[:, 0, :], ACT.Exp, scale=-1.0).then_inc(ez_ready, 1)
                hi(cm + 4)
                hi(cm + 5)
                act.wait_ge(group_evac, gm + 4)
                nc.scalar.activation(th2[:, :, :], th2[:, :, :], ACT.Tanh, scale=0.5).then_inc(glu_th, 1)
                hi(cm + 6)
                hi(cm + 7)
                act.wait_ge(lev_ready, l + 1)
                for t in range(TT):
                    for m in range(2):
                        ins = nc.scalar.activation(ek[:, 0, t, 4 * m:4 * m + 4, :],
                                                   psm[:, 2 * t + m, :].rearrange("p (n i) -> p n i", n=4), ACT.Exp)
                    ins.then_inc(e_ready, 1)
                hi(cm + 8)
                hi(cm + 9)
                def softmax_rows():
                    for n in range(2 * SWH):
                        yield n, ss[:, n, 0:T] if n < SWH else ss[:, n - SWH, T:384]

                act.wait_ge(ss_ready, l + 1)
                nc.scalar.activation(mx[:, 2, :], mx[:, 2, :], ACT.Exp)
                for n, scores in softmax_rows():
                    ins = nc.scalar.activation(scores, scores, ACT.Exp, bias=mx[:, 3, n:n + 1], accum_out=mx[:, 0, n:n + 1])
                ins.then_inc(ss_exp, 1)
                hi(cm + 10)
                act.wait_ge(sums_ready, l + 1)
                for n, scores in softmax_rows():
                    ins = nc.scalar.activation(scores, scores, ACT.Identity, scale=mx[:, 3, n:n + 1])
                ins.then_inc(p_ready, 1)
                act.wait_ge(group_evac, gm + 9)
                nc.scalar.activation(sq2[:, :, :], gr[:, :, :], ACT.Tanh, scale=0.5).then_inc(gr_th, 1)
                for r in range(2):
                    act.wait_ge(pt_full, 2 * l + r + 1)
                    for m in range(3):
                        at = 12 * r + 4 * m
                        ins = nc.scalar.activation(pt[:, at:at + 4, :], stream[m].rearrange("p (n i) -> p n i", n=4), ACT.Copy)
                    ins.then_inc(pt_free, 1)
                act.wait_ge(centred, l + 1)
                nc.scalar.activation(th2[:, :, :], yc[0][:, :, :], ACT.Square).then_inc(yc_sq, 1)
                act.wait_ge(ps7_free, ps70 + PS7_PV + 1)
                nc.scalar.activation(sq2[:, :, :], og[:, :, :], ACT.Square).then_inc(og_sq, 1)
                operand_hi(b_hi[:, 4:8, :].rearrange("p (b f) n -> p b (f n)", b=2), psm[:, 0:2, :], (pv_full, l + 1))
                operand_hi(b_hi[:, 0:2, :], hn[:, 0:2, :], op(op0 + 1))
                act.wait_ge(silu_in, l + 1)
                nc.scalar.activation(th2[:, :, :], yc[0][:, :, :], ACT.Tanh).then_inc(silu_th, 1)
                operand_hi(b_hi[:, 2:4, :], hn[:, 2:4, :], op(op0 + 2))
                for n in range(4):
                    hi(cm + 11 + n)
                    bank_squares(cm + 9 + n, stream[(BANK_WOUT + n) % 3], n)
                x_hi(3 * l + 2, 2 + l, 32)
                ffn(c0 + UL_UP_B, g0 + GL_UP_B, (2 * l + 1) * NF2)
            for g in range(4):
                act.wait_ge(out_turned, g + 1)
                nc.scalar.activation(x_out[:, :, UC * g:UC * g + UC], pair2(psm[:, g, :]), ACT.Copy).then_inc(out_ready, 1)

        @block.vector
        def _(dve):
            V = nc.vector
            chain = {"n": 0, "e": 0}
            count = {"a_lo": 0, "op_lo": 0}

            def mark(ins):
                chain["n"] += 1
                ins.then_inc(dve_chain, 1)
                return chain["n"]

            def link(ins):
                after(dve, dve_chain, mark(ins), chain["e"])

            def lo(c, e=0):
                if isinstance(e, int) and c + NS * e >= TOTAL_UNITS:
                    return
                s = c % NS
                after(dve, w_hi_ready, c + 1, e * NS)
                V.tensor_tensor(w_lo[s][:, :, :], raw[s][:, :, :], w_hi[s][:, :, :].bitcast(F32),
                                ALU.subtract).then_inc(w_split, 1)

            def operand_lo(dst, src, hi_part):
                count["op_lo"] += 1
                dve.wait_ge(op_hi_ready, count["op_lo"])
                V.tensor_tensor(dst, src, hi_part.bitcast(F32), ALU.subtract).then_inc(op_split, 1)

            def variance(st):
                dve.wait_ge(stat_full, st + 1)
                V.tensor_scalar(var2[:, :], ps7[:, 0:2], RMS_EPS, None, ALU.add).then_inc(var_ready, 1)

            def inv_rms(p7):
                dve.wait_ge(ps7_full, p7 + 1)
                V.tensor_copy(rb[:, :], ps7[:, T:2 * T]).then_inc(ps7_free, 1)
                dve.wait_ge(ps7_free, p7 + 1)

            def pre_norm(st, p7, group, col):
                variance(st)
                inv_rms(p7)
                normalise(group, col)

            def normalise(group, col):
                def lo_tile(k):
                    count["a_lo"] += 1
                    dve.wait_ge(a_hi_ready, count["a_lo"])
                    V.tensor_tensor(a_lo[:, k, :], hn[:, k, :], a_hi[:, k, :].bitcast(F32),
                                    ALU.subtract).then_inc(a_split, 1)

                for k in range(KT):
                    V.scalar_tensor_tensor(out=hn[:, k, :], in0=x[:, k, :], scalar=vecs[:, group, col + k:col + k + 1],
                                           in1=rb[:, :], op0=ALU.mult, op1=ALU.mult).then_inc(normed, 1)
                    if k >= 2:
                        lo_tile(k - 2)
                lo_tile(KT - 2)
                lo_tile(KT - 1)

            def x_lo(k, group, col):
                count["a_lo"] += 1
                dve.wait_ge(a_hi_ready, count["a_lo"])
                V.scalar_tensor_tensor(out=a_lo[:, k, :], in0=x[:, k, :], scalar=vecs[:, group, col + k:col + k + 1],
                                       in1=a_hi[:, k, :].bitcast(F32), op0=ALU.mult, op1=ALU.subtract).then_inc(a_split, 1)

            def branch(bank, n, group, col, scale, norms):
                dve.wait_ge(sq_ready, KT * norms + FT * n + FT)
                for f in range(FT):
                    k = FT * n + f
                    ins = V.tensor_scalar(hn[:, k, :], bank[:, f * T:f * T + T], vecs[:, group, col + k:col + k + 1], scale,
                                          ALU.mult, ALU.mult)
                ins.then_inc(group_evac, 1)

            def post_norm(st, p7, next_gain=None):
                variance(st)
                dve.wait_ge(ps7_full, p7 + 1)
                at = []
                for k in range(KT + 2):
                    if k < KT:
                        ins = V.tensor_tensor(hn[:, k, :], hn[:, k, :], ps7[:, T:2 * T], ALU.mult)
                        if k < KT - 1:
                            at.append(mark(ins))
                        else:
                            ins.then_inc(ps7_free, 1)
                    if 1 <= k <= KT:
                        if k < KT:
                            dve.wait_ge(dve_chain, at[k - 1])
                        else:
                            dve.wait_ge(ps7_free, p7 + 1)
                        V.tensor_tensor(x[:, k - 1, :], x[:, k - 1, :], hn[:, k - 1, :], ALU.add).then_inc(x_ready, 1)
                    if k >= 2 and next_gain:
                        x_lo(k - 2, *next_gain)

            def half_log1p(dst, s, s2, e):
                link(V.tensor_scalar(s, e, 2.0, None, ALU.add))
                link(V.reciprocal(s, s))
                link(V.tensor_tensor(s, s, e, ALU.mult))
                link(V.tensor_tensor(s2, s, s, ALU.mult))
                link(V.tensor_scalar(dst, s2, 1.0 / 17, None, ALU.mult))
                for n in (15, 13, 11, 9, 7, 5, 3):
                    link(V.scalar_tensor_tensor(out=dst, in0=dst, scalar=1.0 / n, in1=s2, op0=ALU.add, op1=ALU.mult))
                link(V.scalar_tensor_tensor(out=dst, in0=dst, scalar=1.0, in1=s, op0=ALU.add, op1=ALU.mult))

            def angles(n):
                two_pi = 2 * np.pi
                c1 = 6.28125
                c2 = round((two_pi - c1) * 2 ** 20) / 2 ** 20
                c3 = two_pi - c1 - c2
                shift, offset = ((0.0, 0.0), (0.25, np.pi / 2))[n]
                if n == 0:
                    link(V.tensor_copy(ang_t[:, 0, :], pos_i))
                    link(V.tensor_scalar(ang_t[:, 1, :], ang_t[:, 0, :], const("invf"), None, ALU.mult))
                r = ang[:, n, :]
                link(V.tensor_scalar(ang_t[:, 2, :], ang_t[:, 1, :], 1 / two_pi, shift, ALU.mult, ALU.add))
                link(V.tensor_scalar(ang_t[:, 2, :], ang_t[:, 2, :], MAGIC, -MAGIC, ALU.add, ALU.add))
                link(V.scalar_tensor_tensor(out=r, in0=ang_t[:, 2, :], scalar=-c1, in1=ang_t[:, 1, :],
                                            op0=ALU.mult, op1=ALU.add))
                for cn in (c2, c3):
                    link(V.scalar_tensor_tensor(out=r, in0=ang_t[:, 2, :], scalar=-cn, in1=r, op0=ALU.mult, op1=ALU.add))
                link(V.tensor_scalar(r, r, offset, 3.1415925, ALU.add, ALU.min))
                V.tensor_scalar(r, r, -3.1415925, None, ALU.max).then_inc(ang_ready, 1)

            dve.wait_ge(x_stat, TT)
            V.tensor_scalar(var2[:, :], ms2[:, :], 1 / D, RMS_EPS, ALU.mult, ALU.add).then_inc(var_ready, 1)
            for n in range(4):
                dve.wait_ge(x_turned, n + 1)
                V.tensor_copy(x[:, 2 * n:2 * n + 2, :], pair2(psm[:, n, :]))
            inv_rms(PS7_N0)
            lo(0)
            dve.wait_ge(vecs_turned, 1)
            link(V.tensor_copy(vecs[:, :, :], stream[2][:, :].rearrange("p (g c) -> p g c", g=4)))
            normalise(0, V1["norm1"])
            lo(1)

            for u in range(4):
                lo(u + 2)
                dve.wait_ge(swapped, 2 * u + 2)
                V.tensor_copy(qk_raw[:, 2 * u:2 * u + 2, :], pair2(stream[u % 3][:, :])).then_inc(group_evac, 1)
                if u == 0:
                    dve.wait_ge(small_loaded, 16 * N_SMALL)
                if u < 2:
                    angles(u)
            dve.wait_ge(trig_ready, 2)
            dve.wait_ge(group_evac, 4)

            def over_tiles(ap):
                return ap.rearrange("p (o n) -> p o n", o=1).broadcast_to([P, KT, T])

            for n in range(4):
                u = 4 + n
                if n == 0:
                    mark(V.tensor_tensor(qk_raw, qk_raw, over_tiles(cos2[:, :]), ALU.mult))
                elif n == 1:
                    rot1 = mark(V.tensor_tensor(qk_sw[:, :, :], qk_sw[:, :, :], over_tiles(sin2[:, :]), ALU.mult))
                elif n == 2:
                    dve.wait_ge(dve_chain, rot1)
                    V.tensor_tensor(qk_rot[:, :, :], qk_raw, qk_sw[:, :, :], ALU.add).then_inc(rot_done, 1)
                lo(u + 2)
                dve.wait_ge(unit_used, u + 1)
                V.tensor_copy(v_ret[:, :, UC * n:UC * n + UC], pair2(stream[u % 3][:, :])).then_inc(group_evac, 1)
                if n == 3:
                    dve.wait_ge(late_loaded, 16 * N_LATE)
                    V.tensor_copy(masks[:, :, :].rearrange("p n i -> p (n i)"), masks_f32)
                    dve.wait_ge(ps7_full, PS7_SINK + 1)
                    V.tensor_copy(sinks[:, :, :], ps7[:, 0:LAYERS * 16].rearrange("p (l n) -> p l n", l=LAYERS)).then_inc(ps7_free, 1)
                    for dst, name, m in ((0, "b_r", 16), (16, "gate_b", 16), (32, "gn", 8)):
                        V.tensor_scalar(half_b[:, dst:dst + m], vecs[:, 0, V1[name]:V1[name] + m], 0.5, None, ALU.mult)
                    lam = vecs[:, 0, V1["lam"]:V1["lam"] + KT]
                    link(V.tensor_scalar(sp_t[:, 3, :], lam, -1.0, None, ALU.mult))
                    V.tensor_tensor(sp_t[:, 0, :], lam, sp_t[:, 3, :], ALU.max).then_inc(lam_arg, 1)
                    V.tensor_scalar(sp_t[:, 2, :], lam, 0.0, 4.0, ALU.min, ALU.mult)
            dve.wait_ge(rot_done, 1)
            link(V.memset(xl[:, :, 0:3], 0.0))
            for n in range(4):
                u = 8 + n
                lo(u + 2)
                dve.wait_ge(unit_used, u + 1)
                V.tensor_copy(xl[:, 2 * n:2 * n + 2, 3:3 + T], pair2(stream[u % 3][:, :])).then_inc(group_evac, 1)
                if n == 0:
                    dve.wait_ge(lam_exp, 1)
                    half_log1p(sp_t[:, 5, :], sp_t[:, 3, :], sp_t[:, 4, :], sp_t[:, 1, :])
                    link(V.scalar_tensor_tensor(out=sp4[:, :], in0=sp_t[:, 5, :], scalar=-8.0, in1=sp_t[:, 2, :],
                                                op0=ALU.mult, op1=ALU.add))
                if n == 2:
                    dve.wait_ge(psm_full, PSM_SC + 1)
                    for h in range(HEADS):
                        ins = V.tensor_tensor(st_ret[:, 384 * h:384 * h + 384], psm[:, h, 0:384], ret_d[:, h, :], ALU.mult)
                    ins.then_inc(psm_free, 1)

            at = [0] * KT
            for n in range(4):
                u = 12 + n
                lo(u + 2)
                dve.wait_ge(unit_used, u + 1)
                V.tensor_copy(y_lru[:, 2 * n:2 * n + 2, :], pair2(stream[u % 3][:, :])).then_inc(group_evac, 1)
                if n == 0:
                    dve.wait_ge(psm_full, PSM_O + 1)
                    for h in range(HEADS):
                        ins = V.tensor_copy(o_ret[:, 2 * h:2 * h + 2, :], pair2(psm[:, h, :]))
                    ins.then_inc(psm_free, 1)
                if n == 2:
                    dve.wait_ge(stat_full, ST_RMEAN + 1)
                    V.tensor_copy(var8[:, :], ps7[:, 0:8]).then_inc(mean_ready, 1)
                if n < 3:
                    tap = 2 - n
                    for k in range(KT):
                        if n == 0:
                            dve.wait_ge(lru_conv0, k + 1)
                        else:
                            dve.wait_ge(dve_chain, at[k])
                        col = V1["lconv_w"] + 8 * tap + k
                        ins = V.scalar_tensor_tensor(out=xc[:, k, :], in0=xl[:, k, tap:tap + T],
                                                     scalar=vecs[:, 0, col:col + 1], in1=xc[:, k, :],
                                                     op0=ALU.mult, op1=ALU.add)
                        if n < 2 or k < KT - 1:
                            at[k] = mark(ins)
                        else:
                            ins.then_inc(op_ready, 1)
            operand_lo(b_lo[:, :, :], xc[:, :, :], b_hi[:, :, :])

            def heads(tile, b):
                return tile[:, 4 * b:4 * b + 4, :].rearrange("p (h d) n -> p h d n", h=2)

            def over_halves(b):
                return psm[:, b, :].rearrange("p (h o n) -> p h o n", h=2, o=1).broadcast_to([P, 2, 2, T])

            dve.wait_ge(psm_full, PSM_MEAN + 1)
            for b in range(2):
                ins = V.tensor_tensor(heads(o_ret, b), heads(o_ret, b), over_halves(b), ALU.subtract)
            ins.then_inc(psm_free, 1)
            for n in range(4):
                u = 16 + n
                lo(u + 2)
                dve.wait_ge(act_gate, n + 1)
                V.scalar_tensor_tensor(out=g_ret[:, 2 * n:2 * n + 2, :], in0=g_ret[:, 2 * n:2 * n + 2, :], scalar=1.0,
                                       in1=pair2(stream[u % 3][:, :]), op0=ALU.add, op1=ALU.mult).then_inc(group_evac, 1)
                if n == 0:
                    dve.wait_ge(stat_full, ST_RVAR + 1)
                    V.tensor_scalar(var8[:, :], ps7[:, 0:8], RMS_EPS, None, ALU.add).then_inc(var8_ready, 1)
                if n == 1:
                    dve.wait_ge(psm_full, PSM_VAR + 1)
                    for b in range(2):
                        ins = V.tensor_tensor(heads(o_ret, b), heads(o_ret, b), over_halves(b), ALU.mult)
                    ins.then_inc(psm_free, 1)
            for n in range(8):
                if n % 4 == 3:
                    lo(U1_RG + n // 4 + 2)
                dve.wait_ge(act_gate, 4 + 2 * n + 2)
                for f in range(2):
                    k = 2 * (n % 4) + f
                    if n < 4:
                        ins = V.tensor_scalar(la[:, k, :], la[:, k, :], 1.0, sp4[:, k:k + 1], ALU.add, ALU.mult)
                    else:
                        ins = V.scalar_tensor_tensor(out=i_gate[:, k, :], in0=i_gate[:, k, :], scalar=1.0,
                                                     in1=xc[:, k, :], op0=ALU.add, op1=ALU.mult)
                ins.then_inc(group_evac, 1)
            dve.wait_ge(ge_sq, 1)
            V.scalar_tensor_tensor(out=gel[:, :, :], in0=gel[:, :, :], scalar=1 / GELU_C, in1=y_lru[:, :, :],
                                   op0=ALU.add, op1=ALU.mult).then_inc(ge_cube, 1)
            dve.wait_ge(group_evac, 20)
            dve.wait_ge(psm_free, PSM_VAR + 1)
            for k in range(KT):
                ins = V.scalar_tensor_tensor(out=o_ret[:, k, :], in0=o_ret[:, k, :], scalar=half_b[:, 32 + k:33 + k],
                                             in1=g_ret[:, k, :], op0=ALU.mult, op1=ALU.mult)
            ins.then_inc(op_ready, 1)
            for n in range(8):
                lo(U1_GATES + n + 2)
                dve.wait_ge(act_gate, 20 + 2 * n + 2)
                dst = (ga if n < 4 else gb)[:, 2 * (n % 4):2 * (n % 4) + 2, :]
                V.tensor_scalar(dst, dst, 0.5, 0.5, ALU.mult, ALU.add).then_inc(group_evac, 1)
                if n == 1:
                    operand_lo(b_lo[:, :, :], o_ret[:, :, :], b_hi[:, :, :])
                if n == 2:
                    dve.wait_ge(lru_act, 3)
                    link(V.scalar_tensor_tensor(out=la, in0=a_sq[:, :, :], scalar=1.0, in1=la, op0=ALU.add, op1=ALU.mult))
                    V.tensor_scalar(la, la, -1.0, 1e-30, ALU.mult, ALU.max).then_inc(v_ready, 1)
                if n == 3:
                    dve.wait_ge(ge_th, 1)
                    V.scalar_tensor_tensor(out=y_lru[:, :, :], in0=gel[:, :, :], scalar=1.0, in1=y_lru[:, :, :],
                                           op0=ALU.add, op1=ALU.mult).then_inc(ge_done, 1)
                if n == 5:
                    dve.wait_ge(sqrt_done, 1)
                    link(V.scalar_tensor_tensor(out=i_gate[:, :, :], in0=i_gate[:, :, :], scalar=0.5, in1=la,
                                                op0=ALU.mult, op1=ALU.mult))
                if n == 6:
                    for k in range(KT):
                        at[k] = mark(V.tensor_tensor_scan(h_lru[:, k, :], a_lru[:, k, :], i_gate[:, k, :], 0.0,
                                                          ALU.mult, ALU.add))
                if n == 7:
                    dve.wait_ge(dve_chain, at[KT - 1])
                    V.scalar_tensor_tensor(out=y_lru[:, :, :], in0=h_lru[:, :, :], scalar=0.5, in1=y_lru[:, :, :],
                                           op0=ALU.mult, op1=ALU.mult).then_inc(op_ready, 1)
            for n in range(4):
                lo(U1_RETO + n + 2)
                if n == 1:
                    operand_lo(a_lo[:, :, :], y_lru[:, :, :], a_hi[:, :, :])
                g = G1_RETO + n
                dve.wait_ge(unit_used, U1_RETO + n + 1)
                dst = ga[:, 2 * n:2 * n + 2, :]
                V.tensor_tensor(dst, dst, pair2(stream[g % 3][:, :]), ALU.mult).then_inc(group_evac, 1)
            for n in range(4):
                lo(U1_LRUO + n + 2)
                g = G1_LRUO + n
                dve.wait_ge(unit_used, U1_LRUO + n + 1)
                dst, acc = gb[:, 2 * n:2 * n + 2, :], ga[:, 2 * n:2 * n + 2, :]
                V.tensor_tensor(dst, dst, pair2(stream[g % 3][:, :]), ALU.mult).then_inc(group_evac, 1)
                dve.wait_ge(group_evac, g + 1)
                V.tensor_tensor(acc, acc, dst, ALU.add).then_inc(op_ready, 1)
                if n:
                    operand_lo(b_lo[:, 2 * n - 2:2 * n, :], ga[:, 2 * n - 2:2 * n, :], b_hi[:, 2 * n - 2:2 * n, :])
            operand_lo(b_lo[:, 6:8, :], ga[:, 6:8, :], b_hi[:, 6:8, :])
            for n in range(4):
                lo(U1_OUT + n + 2)
                g = G1_OUT + n
                dve.wait_ge(unit_used, U1_OUT + n + 1)
                dst = x[:, 2 * n:2 * n + 2, :]
                V.tensor_tensor(dst, dst, pair2(stream[g % 3][:, :]), ALU.add).then_inc(group_evac, 1)

            dve.wait_ge(group_evac, G1_OUT + 4)
            pre_norm(ST_N1, PS7_N1, 0, V1["norm2"])

            def hidden_lo(j, e3, h0):
                after(dve, h_hi_ready, h0 + j + 1, e3)

                def tile(t):
                    return t[:, j, :] if isinstance(e3, int) else t[:, bass.ds(e3 + j, 1), :].rearrange("p o n -> p (o n)")

                V.tensor_tensor(tile(h_lo), hb[:, j % 3, :], tile(h_hi).bitcast(F32), ALU.subtract).then_inc(h_split, 1)

            def gated(j, e3, th0, val, factor, ready):
                after(dve, th_ready, th0 + j + 1, e3)
                link(V.scalar_tensor_tensor(out=ab[:, j % 3, :], in0=th[:, j % 3, :], scalar=1.0, in1=factor,
                                            op0=ALU.add, op1=ALU.mult))
                V.scalar_tensor_tensor(out=hb[:, j % 3, :], in0=ab[:, j % 3, :], scalar=0.5, in1=val,
                                       op0=ALU.mult, op1=ALU.mult).then_inc(ready, 1)

            def ff1_step(j, e, e3):
                def col(tap):
                    at = V1B["fconv_w"] + NF1 * tap + j
                    return vecs[:, 1, at:at + 1] if isinstance(e3, int) else vecs[:, 1, bass.ds(e3 + at, 1)]

                before = j or not isinstance(e3, int)
                after(dve, tap_ready, j + 1, e3)
                bank, c = stream[j % 3], cg[:, j % 3, :]
                link(V.scalar_tensor_tensor(out=c[:, 1:T], in0=bank[:, 0:T - 1], scalar=col(1), in1=c[:, 1:T],
                                            op0=ALU.mult, op1=ALU.add))
                V.scalar_tensor_tensor(out=c[:, 2:T], in0=bank[:, 0:T - 2], scalar=col(0), in1=c[:, 2:T],
                                       op0=ALU.mult, op1=ALU.add).then_inc(conv_done, 1)
                if before:
                    ff1_product(j - 1, e3)
                if j > 1 or not isinstance(e3, int):
                    hidden_lo(j - 2, e3, 0)
                lo(U1_UP + j + 3, e)
                after(dve, csq_ready, j + 1, e3)
                V.scalar_tensor_tensor(out=cub[:, j % 3, :], in0=cub[:, j % 3, :], scalar=1 / GELU_C, in1=c,
                                       op0=ALU.add, op1=ALU.mult).then_inc(cube_ready, 1)

            def ff1_product(j, e3):
                gated(j, e3, 0, stream[j % 3][:, T:2 * T], cg[:, j % 3, :], group_evac)

            lo(U1_UP + 2)
            for j in range(3):
                ff1_step(j, 0, 0)
            n0 = chain["n"]
            with dve.Fori(1, NF1 // 3) as i:
                chain["e"] = (i - 1) * 6
                for j in range(3):
                    ff1_step(j, i, i * 3)
                assert chain["n"] - n0 == 6
            chain["n"], chain["e"] = n0 + 6 * (NF1 // 3 - 1), 0
            ff1_product(NF1 - 1, 0)
            hidden_lo(NF1 - 2, 0, 0)
            hidden_lo(NF1 - 1, 0, 0)
            for n in range(4):
                for m in range(3 if n < 3 else 2):
                    lo(U1_DOWN + 3 * n + m + 3)
                dve.wait_ge(unit_used, U1_DOWN + 3 * n + 3)
                dst = x[:, 2 * n:2 * n + 2, :]
                V.tensor_tensor(dst, dst, pair2(psm[:, n % 2, :]), ALU.add).then_inc(group_evac, 1)
            dve.wait_ge(group_evac, G1_END)
            variance(ST_NF)
            inv_rms(PS7_NF)
            for k in range(KT):
                V.scalar_tensor_tensor(out=x[:, k, :], in0=x[:, k, :], scalar=vecs[:, 0, V1["norm_f"] + k:V1["norm_f"] + k + 1],
                                       in1=rb[:, :], op0=ALU.mult, op1=ALU.mult).then_inc(x_ready, 1)
                if k >= 2:
                    x_lo(k - 2, 2, 0)
            x_lo(KT - 2, 2, 0)
            x_lo(KT - 1, 2, 0)

            def ffn(c0, g0, bank0, h0, st, p7, group, col, norms):
                def unit(j, e, e3):
                    after(dve, unit_used, c0 + j + 1, e3)
                    V.tensor_tensor(gu[:, j % 3, :, :], pair2(stream[(bank0 + j) % 3][:, :]),
                                    rb[:, :].rearrange("p (o n) -> p o n", o=1).broadcast_to([P, 2, T]),
                                    ALU.mult).then_inc(group_evac, 1)
                    if j >= 2:
                        lo(c0 + j + 2, e)
                    gated(j, e3, h0, gu[:, j % 3, 1, :], gu[:, j % 3, 0, :], hb_ready)
                    if j:
                        hidden_lo(j - 1, e3, h0)

                lo(c0 + 2)
                variance(st)
                lo(c0 + 3)
                inv_rms(p7)
                for j in range(4):
                    unit(j, 0, 0)
                n0 = chain["n"]
                with dve.Fori(0, (NF2 - 4) // 3) as i:
                    chain["e"] = i * 3
                    for j in range(4, 7):
                        unit(j, i, i * 3)
                    assert chain["n"] - n0 == 3
                chain["n"], chain["e"] = n0 + NF2 - 4, 0
                hidden_lo(NF2 - 1, 0, h0)
                for n in range(4):
                    for m in range(3):
                        lo(c0 + NF2 + 3 * n + m + 2)
                    branch(psm[:, n % 2, :], n, group, col, 0.5, norms)
                dve.wait_ge(group_evac, g0 + NF2 + 4)

            for l in range(LAYERS):
                c0, g0 = U1_END + UL * l, G1_END + GL * l
                psm0, ps70, st0, h0 = PSM_1 + PSM_L * l, PS7_1 + PS7_L * l, ST_1 + ST_L * l, NF1 + 2 * NF2 * l
                group = 2 + l

                def vec(name, k):
                    return vecs[:, group, VL[name] + k:VL[name] + k + 1]

                ffn(c0, g0, 0, h0, st0 + ST_G0, ps70 + PS7_G0, group, 8, 3 + 6 * l)
                post_norm(st0 + ST_G1, ps70 + PS7_G1, (group, 16))

                cm, gm = c0 + UL_MIX, g0 + GL_MIX

                def bank(n):
                    return stream[(BANK_MIX + n) % 3]

                conv_steps = [(tap, f) for tap in range(TAPS) for f in range(2) if f == 0 or tap < TAPS_DVE]
                conv_at = {}

                def conv(steps):
                    for tap, f in conv_steps[len(conv_at):len(conv_at) + steps]:
                        n = 2 * tap + f
                        acc, src, w = yc[tap % 2][:, f, :], up[:, f, tap:tap + T], vec("conv_w", n)
                        if tap == 0:
                            ins = V.tensor_scalar(acc, src, w, vec("conv_b", f), ALU.mult, ALU.add)
                        elif tap == 1:
                            ins = V.tensor_scalar(acc, src, w, None, ALU.mult)
                        else:
                            dve.wait_ge(dve_chain, conv_at[tap - 2, f])
                            ins = V.scalar_tensor_tensor(out=acc, in0=src, scalar=w, in1=acc, op0=ALU.mult, op1=ALU.add)
                        conv_at[tap, f] = mark(ins)

                def gla_scores(n):
                    t, heads = n // 4, slice(2 * (n % 2), 2 * (n % 2) + 2)
                    dve.wait_ge(zeroed, 2 * l + 1)
                    if n >= 2:
                        dve.wait_ge(psm_free, psm0 + PSM_GLA + n - 1)
                    dve.wait_ge(psm_full, psm0 + PSM_GLA + n + 1)
                    for m in range(4):
                        level = 4 * (n // 2 % 2) + m
                        ins = V.copy_predicated(s_gla[:, t, heads, :], masks[:, level:level + 1, :].broadcast_to([P, 2, P]),
                                                psm[:, heads, m * P:m * P + P])
                        if m < 3:
                            written = mark(ins)
                            if m == 1:
                                conv(1)
                            dve.wait_ge(dve_chain, written)
                    ins.then_inc(psm_free, 1)
                    conv(1)

                def window_scores(b):
                    dve.wait_ge(psm_full, psm0 + PSM_SWA + b + 1)
                    for n in range(4):
                        head = (n % 2) * 4 + 2 * b + n // 2
                        ins = V.scalar_tensor_tensor(out=ss[:, 4 * b + n, :], in0=const("alibi"), scalar=2.0 ** -(head + 1),
                                                     in1=psm[:, n, 0:384], op0=ALU.mult, op1=ALU.add)
                    ins.then_inc(psm_free, 1)

                def over2(ap):
                    return ap.rearrange("p (o n) -> p o n", o=1).broadcast_to([P, 2, T])

                def read_pair(n, dst, scale):
                    dve.wait_ge(unit_used, cm + n + 1)
                    V.scalar_tensor_tensor(out=dst, in0=pair2(bank(n)[:, :]), scalar=scale, in1=over2(rb[:, :]),
                                           op0=ALU.mult, op1=ALU.mult).then_inc(group_evac, 1)

                lo(cm + 2)
                variance(st0 + ST_G2)
                lo(cm + 3)
                inv_rms(ps70 + PS7_G2)
                dve.wait_ge(pool_init, 3)
                dve.wait_ge(unit_used, cm + 1)
                V.tensor_tensor(glr_t[0:16, :], bank(0)[0:16, 0:T], rb[0:16, :], ALU.mult).then_inc(group_evac, 1)
                dve.wait_ge(unit_used, cm + 2)
                V.scalar_tensor_tensor(out=qg[:, :], in0=bank(1)[:, 0:T], scalar=GDK ** -0.5, in1=rb[:, :],
                                       op0=ALU.mult, op1=ALU.mult)
                V.tensor_tensor(kg[:, :], bank(1)[:, T:2 * T], rb[:, :], ALU.mult).then_inc(group_evac, 1)
                read_pair(2, ca[:, :, :], 0.5)
                lo(cm + 4)
                dve.wait_ge(ez_ready, l + 1)
                V.tensor_scalar(lg[:, 1, :], ps7[:, 0:T], 0.0, None, ALU.min).then_inc(ps7_free, 1)
                half_log1p(lg[:, 4, :], lg[:, 2, :], lg[:, 3, :], lg[:, 0, :])
                dve.wait_ge(ps7_free, ps70 + PS7_Z + 1)
                V.scalar_tensor_tensor(out=lg[:, 1, :], in0=lg[:, 4, :], scalar=-2.0, in1=lg[:, 1, :],
                                       op0=ALU.mult, op1=ALU.add).then_inc(glog_ready, 1)
                read_pair(3, th2[:, :, :], 1.0)
                lo(cm + 5)
                dve.wait_ge(zeroed, 2 * l + 2)
                dve.wait_ge(group_evac, gm + 3)
                dve.wait_ge(glu_th, l + 1)
                V.scalar_tensor_tensor(out=up[:, :, TAPS - 1:TAPS - 1 + T], in0=th2[:, :, :], scalar=1.0,
                                       in1=ca[:, :, :], op0=ALU.add, op1=ALU.mult).then_inc(up_ready, 1)
                dve.wait_ge(up_ready, l + 1)
                conv(3)
                dve.wait_ge(unit_used, cm + 5)
                V.tensor_tensor(ks[:, :], bank(4)[:, 0:T], rb[:, :], ALU.mult)
                for t in range(TT):
                    ins = V.tensor_scalar(vs[:, t, :], bank(4)[:, T + t * P:T + t * P + P], rstd2[:, t:t + 1], None, ALU.mult)
                ins.then_inc(group_evac, 1)
                lo(cm + 6)
                conv(3)
                read_pair(5, qs[:, 0:2, :], SWD ** -0.5)
                lo(cm + 7)
                dve.wait_ge(group_evac, gm + 2)
                for t in range(TT):
                    dve.wait_ge(e_ready, TT * l + t + 1)
                    ins = V.tensor_tensor(qe[:, t, :, :], ek[:, 0, t, :, :],
                                          qg[:, t * P:t * P + P].rearrange("p (o i) -> p o i", o=1).broadcast_to([P, LEV, P]),
                                          ALU.mult)
                ins.then_inc(qe_ready, 1)
                window_scores(0)
                lo(cm + 8)
                conv(2)
                read_pair(6, qs[:, 2:4, :], SWD ** -0.5)
                conv(6)
                window_scores(1)
                dve.wait_ge(psm_free, psm0 + PSM_SWA + 2)
                V.tensor_reduce(mx[:, 0, 0:8], ss[:, :, 0:T], AX, ALU.max)
                link(V.tensor_reduce(mx[:, 0, 8:16], ss[:, :, T:384], AX, ALU.max))
                link(V.tensor_tensor(mx[:, 1, :], mx[:, 0, :], sinks[:, l, :], ALU.max))
                V.tensor_tensor(mx[:, 2, :], sinks[:, l, :], mx[:, 1, :], ALU.subtract)
                V.tensor_scalar(mx[:, 3, :], mx[:, 1, :], -1.0, None, ALU.mult).then_inc(ss_ready, 1)
                for n in range(8):
                    gla_scores(n)
                    if n == 2:
                        dve.wait_ge(ss_exp, l + 1)
                        link(V.tensor_tensor(mx[:, 0, :], mx[:, 0, :], mx[:, 2, :], ALU.add))
                        V.reciprocal(mx[:, 3, :], mx[:, 0, :]).then_inc(sums_ready, 1)
                    if n == 1:
                        dve.wait_ge(unit_used, cm + 8)
                        for t in range(TT):
                            ins = V.tensor_scalar(vg[:, t, :], bank(7)[:, t * T:t * T + T], rstd2[:, t:t + 1], None, ALU.mult)
                        ins.then_inc(group_evac, 1)
                    if n == 4:
                        read_pair(8, gr[:, :, :], 1.0)
                dve.wait_ge(group_evac, gm + 9)
                dve.wait_ge(gr_th, l + 1)
                V.scalar_tensor_tensor(out=gr[:, :, :], in0=sq2[:, :, :], scalar=1.0, in1=gr[:, :, :],
                                       op0=ALU.add, op1=ALU.mult).then_inc(gate_ready, 1)
                conv(len(conv_steps))
                dve.wait_ge(dve_chain, conv_at[TAPS - 1, 0])
                dve.wait_ge(tap_sum, (TAPS - TAPS_DVE - 1) * (l + 1))
                V.tensor_tensor(yc[0][:, 1, :], yc[0][:, 1, :], y_pool, ALU.add)
                link(V.tensor_tensor(yc[0][:, 0, :], yc[0][:, 0, :], yc[1][:, 0, :], ALU.add))
                V.tensor_tensor(yc[0][:, 1, :], yc[0][:, 1, :], yc[1][:, 1, :], ALU.add).then_inc(yc_ready, 1)
                dve.wait_ge(psm_full, psm0 + PSM_CROSS + 1)
                V.tensor_copy(s_cross[:, :, :], psm[:, :, 0:P]).then_inc(psm_free, 1)

                cbank = stream[(BANK_WOUT + 2) % 3]
                dve.wait_ge(conv_full, 2 * l + 1)
                dve.wait_ge(yc_ready, l + 1)
                V.tensor_tensor(yc[0][:, :, :], yc[0][:, :, :], over2(cbank[:, T:2 * T]), ALU.subtract).then_inc(centred, 1)
                lo(cm + 9)
                dve.wait_ge(ps7_full, ps70 + PS7_PV + 1)
                V.tensor_copy(og[:, :, :], pair2(ps7[:, :])).then_inc(ps7_free, 1)
                lo(cm + 10)
                dve.wait_ge(stat_full, st0 + ST_GLA + 1)
                V.tensor_scalar(var8[:, :], ps7[:, 0:8], RMS_EPS, None, ALU.add).then_inc(var8_ready, 1)
                dve.wait_ge(stat_full, st0 + ST_CVAR + 1)
                V.tensor_scalar(var2[:, :], cbank[:, 0:2], LN_EPS, None, ALU.add).then_inc(centred_var, 1)
                operand_lo(b_lo[:, 4:8, :].rearrange("p (b f) n -> p b (f n)", b=2), psm[:, 0:2, :],
                           b_hi[:, 4:8, :].rearrange("p (b f) n -> p b (f n)", b=2))
                dve.wait_ge(ps7_full, ps70 + PS7_GBC + 1)
                for f in range(2):
                    ins = V.scalar_tensor_tensor(out=og[:, f, :], in0=og[:, f, :], scalar=vec("gla_g", f),
                                                 in1=ps7[:, f * T:f * T + T], op0=ALU.mult, op1=ALU.mult)
                ins.then_inc(ps7_free, 1)
                dve.wait_ge(ps7_free, ps70 + PS7_GBC + 1)
                dve.wait_ge(gate_ready, l + 1)
                V.scalar_tensor_tensor(out=hn[:, 0:2, :], in0=og[:, :, :], scalar=0.5, in1=gr[:, :, :],
                                       op0=ALU.mult, op1=ALU.mult).then_inc(op_ready, 1)
                dve.wait_ge(conv_full, 2 * l + 2)
                for f in range(2):
                    ins = V.scalar_tensor_tensor(out=yc[0][:, f, :], in0=yc[0][:, f, :], scalar=vec("ln_g", f),
                                                 in1=cbank[:, T:2 * T], op0=ALU.mult, op1=ALU.mult)
                link(ins)
                for f in range(2):
                    ins = V.tensor_scalar(yc[0][:, f, :], yc[0][:, f, :], vec("ln_b", f), 0.5, ALU.add, ALU.mult)
                ins.then_inc(silu_in, 1)
                operand_lo(b_lo[:, 0:2, :], hn[:, 0:2, :], b_hi[:, 0:2, :])
                dve.wait_ge(silu_th, l + 1)
                V.scalar_tensor_tensor(out=hn[:, 2:4, :], in0=th2[:, :, :], scalar=1.0, in1=yc[0][:, :, :],
                                       op0=ALU.add, op1=ALU.mult).then_inc(op_ready, 1)
                operand_lo(b_lo[:, 2:4, :], hn[:, 2:4, :], b_hi[:, 2:4, :])
                for n in range(4):
                    lo(cm + 11 + n)
                    branch(stream[(BANK_WOUT + n) % 3], n, group, 24, 1.0, 5 + 6 * l)
                dve.wait_ge(group_evac, g0 + GL_WOUT + 4)
                post_norm(st0 + ST_G3, ps70 + PS7_G3, (group, 32))
                ffn(c0 + UL_UP_B, g0 + GL_UP_B, BANK_UP_B, h0 + NF2, st0 + ST_G4, ps70 + PS7_G4, group, 40, 7 + 6 * l)
                post_norm(st0 + ST_G5, ps70 + PS7_G5, (group + 1, 0) if l < LAYERS - 1 else None)
        @block.tensor
        def _(pe):
            seen = {"norm": 0}

            def mm(dst, lhs, rhs, start, stop):
                return nc.tensor.matmul(dst, lhs, rhs, start=start, stop=stop, skip_group_check=True)

            def split_unit(c, e=0):
                after(pe, w_split, c + 1, e * NS)

            def feature_major(s, dst, tiles, hi_t, lo_t, first, last, kts=range(KT), ready=None):
                for n, (lhs, at) in enumerate(tiles):
                    for k in kts:
                        if ready and n == 0:
                            ready(k)
                        to = dst[:, at:at + T]
                        begin, end = first and n == 0 and k == kts[0], last and n == len(tiles) - 1 and k == kts[-1]
                        mm(to, lhs(w_hi[s], k), hi_t[:, k, :], begin, False)
                        mm(to, lhs(w_hi[s], k), lo_t[:, k, :], False, False)
                        ins = mm(to, lhs(w_lo[s], k), hi_t[:, k, :], False, end)
                return ins

            def block_cols(f):
                return lambda w, k: w[:, k, f * P:f * P + P]

            BOTH = [(block_cols(0), 0), (block_cols(1), T)]

            def token_major(s, dst, col, width, at, begin, tiles=range(TT)):
                for t in tiles:
                    to = dst[:, at + t * width:at + t * width + width]
                    tok = slice(t * P, t * P + P)
                    for k in range(KT):
                        w = slice(col, col + width)
                        mm(to, a_hi[:, k, tok], w_hi[s][:, k, w], begin and t == 0 and k == 0, False)
                        mm(to, a_lo[:, k, tok], w_hi[s][:, k, w], False, False)
                        ins = mm(to, a_hi[:, k, tok], w_lo[s][:, k, w], False, t == TT - 1 and k == KT - 1)
                return ins

            def bank_free(g, e3=0, back=2):
                after(pe, group_evac, g - back, e3)

            def a_ready(n):
                return lambda k: pe.wait_ge(a_split, KT * n + k + 1)

            def mean_squares(p7):
                seen["norm"] += 1
                after(pe, ps7_free, p7)
                pe.wait_ge(sq_sum, 5 * seen["norm"])
                for k in (0, KT - 2, KT - 1):
                    pe.wait_ge(sq_ready, KT * (seen["norm"] - 1) + k + 1)
                    for t in range(TT):
                        ins = mm(ps7[:, t:t + 1], sq[:, k, t * P:t * P + P], means[:, 0:1], k == 0 and t == 0,
                                 k == KT - 1 and t == TT - 1)
                ins.then_inc(stat_full, 1)

            def inverse_rms():
                pe.wait_ge(rstd_ready, seen["norm"] + 1)
                for t in range(TT):
                    ins = mm(ps7[:, T + t * P:T + t * P + P], rstd2[:, t:t + 1].broadcast_to([P, P]), ident, t == 0, t == 1)
                ins.then_inc(ps7_full, 1)

            def keep_warm(n):
                for _ in range(n):
                    mm(psm[:, 3, 0:T], b_hi[:, 0, 0:P], b_hi[:, 0, :], True, True)

            def norm(p7):
                keep_warm(2)
                mean_squares(p7)
                keep_warm(10)
                inverse_rms()
                keep_warm(20)

            pe.wait_ge(ident_loaded, 16)
            pe.wait_ge(x_loaded, 16)
            for k in range(KT):
                for t in range(TT):
                    at = (k % 2) * T + t * P
                    ins = nc.tensor.transpose(psm[:, k // 2, at:at + P], x_in[:, t, k * P:k * P + P], ident)
                if k % 2:
                    ins.then_inc(x_turned, 1)
            inverse_rms()
            pe.wait_ge(vecs_loaded, 16)
            staged = sq[:, 0:2, :].rearrange("p a (b c) -> p (a b) c", b=2)
            for n in range(4):
                ins = nc.tensor.transpose(stream[2][:, n * P:n * P + P], staged[:, n, :], ident)
            ins.then_inc(vecs_turned, 1)

            def project(c, g, bank, hi_t, lo_t, ready=None):
                split_unit(c)
                bank_free(g)
                feature_major(c % NS, bank, BOTH[0:1], hi_t, lo_t, True, False, ready=ready)
                ins = feature_major(c % NS, bank, BOTH[1:2], hi_t, lo_t, False, True)
                ins.then_inc(unit_used, 1)

            for u in range(8):
                if u < 4:
                    project(u, u, stream[u % 3], a_hi, a_lo, a_ready(0) if u == 0 else None)
                else:
                    split_unit(u)
                    bank_free(u)
                    token_major(u % NS, stream[u % 3], 0, UC, 0, True).then_inc(unit_used, 1)
                if u == 4:
                    pe.wait_ge(ps7_free, PS7_SINK)
                    pe.wait_ge(pool_init, 2)
                    pe.wait_ge(small_loaded, 16 * N_SMALL)
                    mm(ps7[:, 0:LAYERS * 16], ones_row[:, :], sink_row[:, :], True, True).then_inc(ps7_full, 1)
            for u in range(8, 20):
                project(u, u, stream[u % 3], a_hi, a_lo)
                if u == 9:
                    pe.wait_ge(rot_done, 1)
                    for h in range(HEADS):
                        mm(psm[:, h, 0:T], qk_rot[:, 4 + h, 0:P], qk_rot[:, h, :], True, False)
                        ins = mm(psm[:, h, T:384], qk_rot[:, 4 + h, P:T], qk_rot[:, h, P:T], False, True)
                    ins.then_inc(psm_full, 1)
                if u == 11:
                    pe.wait_ge(psm_free, PSM_O)
                    for h in range(HEADS):
                        for d in range(2):
                            v = slice(h * DV + d * P, h * DV + d * P + P)
                            mm(psm[:, h, d * T:d * T + T], v_ret[:, 0, v], st_ret[:, 384 * h:384 * h + T], d == 0, False)
                            ins = mm(psm[:, h, d * T + P:d * T + T], v_ret[:, 1, v], st_ret[:, 384 * h + T:384 * h + 384],
                                     False, d == 1)
                    ins.then_inc(psm_full, 1)
                if u in (13, 16):
                    pe.wait_ge(psm_free, PSM_O + 1)
                    if u == 16:
                        pe.wait_ge(o_sq, 1)
                    src = o_ret if u == 13 else sq
                    after(pe, ps7_free, PS7_N1)
                    for t in range(TT):
                        for h in range(HEADS):
                            for d in range(2):
                                ins = mm(ps7[:, 4 * t + h:4 * t + h + 1], src[:, 2 * h + d, t * P:t * P + P], means[:, 1:2],
                                         t + h + d == 0, t == 1 and h == 3 and d == 1)
                    ins.then_inc(stat_full, 1)
                if u in (15, 17):
                    if u == 15:
                        pe.wait_ge(mean_ready, 1)
                    else:
                        pe.wait_ge(rstd8_ready, 1)
                    pe.wait_ge(psm_free, PSM_MEAN if u == 15 else PSM_VAR)
                    src = var8 if u == 15 else rstd8
                    for h in range(HEADS):
                        for t in range(TT):
                            at = (h % 2) * T + t * P
                            ins = mm(psm[:, h // 2, at:at + P], src[:, 4 * t + h:4 * t + h + 1].broadcast_to([P, P]), ident,
                                     h % 2 == 0 and t == 0, h % 2 == 1 and t == 1)
                    ins.then_inc(psm_full, 1)
            pe.wait_ge(op_split, 1)
            for m in range(2):
                c = U1_RG + m
                split_unit(c)
                for n in range(4):
                    g = G1_RG + 4 * m + n
                    bank_free(g)
                    ins = feature_major(c % NS, stream[g % 3], BOTH, b_hi, b_lo, True, True, kts=(2 * n, 2 * n + 1))
                    if n < 3:
                        ins.then_inc(rg_done, 1)
                ins.then_inc(unit_used, 1)
            for n in range(8):
                project(U1_GATES + n, G1_GATES + n, stream[(G1_GATES + n) % 3], a_hi, a_lo)
            pe.wait_ge(op_split, 2)
            for n in range(4):
                project(U1_RETO + n, G1_RETO + n, stream[(G1_RETO + n) % 3], b_hi, b_lo)
            pe.wait_ge(op_split, 3)
            for n in range(4):
                project(U1_LRUO + n, G1_LRUO + n, stream[(G1_LRUO + n) % 3], a_hi, a_lo)
            split_unit(U1_OUT)
            bank_free(G1_OUT)
            for k in range(KT):
                pe.wait_ge(op_split, 4 + k // 2)
                ins = feature_major(U1_OUT % NS, stream[G1_OUT % 3], BOTH, b_hi, b_lo, k == 0, k == KT - 1, kts=(k,))
            ins.then_inc(unit_used, 1)
            for n in range(1, 4):
                project(U1_OUT + n, G1_OUT + n, stream[(G1_OUT + n) % 3], b_hi, b_lo)
            norm(PS7_N1)

            def hidden(c, e, g, e3, bank, ready=None):
                split_unit(c, e)
                bank_free(g, e3)
                feature_major(c % NS, bank, BOTH[0:1], a_hi, a_lo, True, False, ready=ready)
                ins = feature_major(c % NS, bank, BOTH[1:2], a_hi, a_lo, False, True)
                ins.then_inc(unit_used, 1)

            def down(c, g, nf, h0):
                with pe.Fori(0, 2) as i:
                    for j in range(6):
                        n, m = j // 3, j % 3
                        split_unit(c + j, i * 2)
                        if m == 0:
                            bank_free(g + n, i * 2, back=1)
                        k0 = KT * m
                        kts = range(min(KT, nf - k0))
                        pe.wait_ge(h_split, h0 + k0 + len(kts))
                        hi_t, lo_t = h_hi[:, k0:k0 + len(kts), :], h_lo[:, k0:k0 + len(kts), :]
                        ins = feature_major((c + j) % NS, psm[:, n, :], BOTH, hi_t, lo_t, m == 0, m == 2, kts=kts)
                        ins.then_inc(unit_used, 1)

            for j in range(3):
                hidden(U1_UP + j, 0, G1_UP + j, 0, stream[j % 3], a_ready(1) if j == 0 else None)
            with pe.Fori(1, NF1 // 3) as i:
                for j in range(3):
                    hidden(U1_UP + j, i, G1_UP + j, i * 3, stream[j % 3])
            keep_warm(26)
            down(U1_DOWN, G1_DOWN, NF1, 0)
            norm(PS7_NF)

            def two_units(c, g, banks, hi_t, lo_t, ready, tiles=(BOTH, BOTH), order=range(KT)):
                for n in range(2):
                    split_unit(c + n)
                    bank_free(g + n)
                for k in order:
                    ready(k)
                    for n in range(2):
                        ins = feature_major((c + n) % NS, banks[n], tiles[n], hi_t, lo_t, k == order[0], k == order[-1], kts=(k,))
                        if k == order[-1]:
                            ins.then_inc(unit_used, 1)

            def third_unit(c, g, bank, p7):
                mean_squares(p7)
                split_unit(c)
                bank_free(g)
                feature_major(c % NS, bank, BOTH[0:1], a_hi, a_lo, True, False)
                inverse_rms()
                feature_major(c % NS, bank, BOTH[1:2], a_hi, a_lo, False, True).then_inc(unit_used, 1)

            def ffn(c, g, bank0, norm_no, h0, p7):
                two_units(c, g, [stream[(bank0 + n) % 3] for n in range(2)], a_hi, a_lo, a_ready(norm_no))
                third_unit(c + 2, g + 2, stream[(bank0 + 2) % 3], p7)
                hidden(c + 3, 0, g + 3, 0, stream[bank0])
                with pe.Fori(0, (NF2 - 4) // 3) as i:
                    for j in range(4, 7):
                        hidden(c + j, i, g + j, i * 3, stream[(bank0 + j) % 3])
                down(c + NF2, g + NF2, NF2, h0)

            for l in range(LAYERS):
                c0, g0 = U1_END + UL * l, G1_END + GL * l
                psm0, ps70 = PSM_1 + PSM_L * l, PS7_1 + PS7_L * l
                ffn(c0, g0, 0, 2 + 3 * l, NF1 + NF2 * (2 * l), ps70 + PS7_G0)
                norm(ps70 + PS7_G1)
                cm, gm = c0 + UL_MIX, g0 + GL_MIX

                def bank(n):
                    return stream[(BANK_MIX + n) % 3]

                def psm_ready(n):
                    pe.wait_ge(psm_free, psm0 + n)

                def cols(tile, n):
                    return tile[:, n * P:n * P + P]

                two_units(cm, gm, [bank(0), bank(1)], a_hi, a_lo, a_ready(3 + 3 * l), tiles=(BOTH[0:1], BOTH))
                third_unit(cm + 2, gm + 2, bank(2), ps70 + PS7_G2)
                pe.wait_ge(group_evac, gm + 1)
                pe.wait_ge(ps7_free, ps70 + PS7_Z)
                for t in range(TT):
                    ins = mm(cols(ps7, t), cols(glr_t[0:17, :], t), w2aug[:, l, :], t == 0, t == 1)
                ins.then_inc(ps7_full, 1)
                project(cm + 3, gm + 3, bank(3), a_hi, a_lo)
                split_unit(cm + 4)
                bank_free(gm + 4)
                feature_major((cm + 4) % NS, bank(4), BOTH[0:1], a_hi, a_lo, True, False)
                token_major((cm + 4) % NS, bank(4), P, P, T, False).then_inc(unit_used, 1)

                pe.wait_ge(glog_ready, l + 1)
                psm_ready(0)
                pe.wait_ge(late_loaded, 16 * N_LATE)
                lev = const("lev")
                for t in range(TT):
                    g_t = cols(lg[:, 1, :], t)
                    mm(psm[:, 2 * t, :], g_t, lev[:, 0:4 * P], True, True)
                    mm(psm[:, 2 * t + 1, 0:3 * P], g_t, lev[:, 4 * P:7 * P], True, False)
                    ins = mm(psm[:, 2 * t + 1, 3 * P:4 * P], g_t, cols(lev, 7 + t), False, True)
                ins.then_inc(lev_ready, 1)
                def head(tile, h):
                    return tile[GDK * h:GDK * h + GDK]

                def gla_scores(n):
                    t = n // 4
                    psm_ready(PSM_GLA + max(n - 1, 0))
                    pe.wait_ge(ke_ready, TT * l + t + 1)
                    for m in range(4):
                        level = 4 * (n // 2 % 2) + m
                        for h in (2 * (n % 2), 2 * (n % 2) + 1):
                            if level < LEV - 1:
                                k_t, q_t = head(ek[:, 1, t, level, :], h), head(qe[:, t, level, :], h)
                            else:
                                k_t, q_t = head(cols(kg, t), h), head(cols(qg, t), h)
                            ins = mm(psm[:, h, m * P:m * P + P], k_t, q_t, m == 0, m == 3)
                    ins.then_inc(psm_full, 1)

                def window_scores(b):
                    psm_ready(PSM_SWA + b)
                    pe.wait_ge(e_ready, TT * (l + 1))
                    pe.wait_ge(group_evac, gm + 6 + b)
                    for n in range(4):
                        half, j = n % 2, 2 * b + n // 2
                        part = slice(SWD * half, SWD * half + SWD)
                        mm(psm[:, n, 0:T], qs[part, j, P:T], ks[part, :], True, False)
                        ins = mm(psm[:, n, T:384], qs[part, j, 0:P], ks[part, 0:P], False, True)
                    ins.then_inc(psm_full, 1)

                project(cm + 5, gm + 5, bank(5), a_hi, a_lo)
                s = (cm + 6) % NS
                split_unit(cm + 6)
                bank_free(gm + 6)
                feature_major(s, bank(6), BOTH[0:1], a_hi, a_lo, True, False)
                window_scores(0)
                feature_major(s, bank(6), BOTH[1:2], a_hi, a_lo, False, True).then_inc(unit_used, 1)

                def probabilities(r):
                    for n in range(12 * r, 12 * r + 12):
                        src = cols(ss[:, n // 2, 0:T], n % 2) if n < 2 * SWH else ss[:, n - 2 * SWH, T:384]
                        ins = nc.tensor.transpose(cols(stream[n // 4 % 3], n % 4), src, ident)
                    ins.then_inc(pt_full, 1)

                s = (cm + 7) % NS
                split_unit(cm + 7)
                bank_free(gm + 7)
                token_major(s, bank(7), 0, 256, 0, True, (0,))
                window_scores(1)
                token_major(s, bank(7), 0, 256, 0, True, (1,)).then_inc(unit_used, 1)
                pe.wait_ge(qe_ready, l + 1)
                gla_scores(0)
                gla_scores(1)
                s = (cm + 8) % NS
                split_unit(cm + 8)
                bank_free(gm + 8)
                feature_major(s, bank(8), BOTH[0:1], a_hi, a_lo, True, False)
                gla_scores(2)
                gla_scores(3)
                feature_major(s, bank(8), BOTH[1:2], a_hi, a_lo, False, True).then_inc(unit_used, 1)
                gla_scores(4)
                gla_scores(5)
                gla_scores(6)
                gla_scores(7)
                pe.wait_ge(group_evac, gm + 9)
                pe.wait_ge(p_ready, l + 1)
                probabilities(0)
                pe.wait_ge(pt_free, 2 * l + 1)
                probabilities(1)
                psm_ready(PSM_CROSS)
                for h in range(GH):
                    ins = mm(psm[:, h, 0:P], head(ek[:, 1, 0, LEV - 1, :], h), head(qe[:, 1, LEV - 1, :], h), True, True)
                ins.then_inc(psm_full, 1)

                cbank = stream[(BANK_WOUT + 2) % 3]

                pe.wait_ge(pt_free, 2 * l + 2)
                pe.wait_ge(yc_ready, l + 1)
                for f in range(2):
                    ins = mm(cbank[:, T:2 * T], means[:, 1:2].broadcast_to([P, P]), yc[0][:, f, :], f == 0, f == 1)
                ins.then_inc(conv_full, 1)
                psm_ready(PSM_CROSS + 1)
                pe.wait_ge(ps7_free, ps70 + PS7_PV)
                for h in range(GH):
                    part, f = slice(GDV * (h % 2), GDV * (h % 2) + GDV), h // 2
                    v = slice(GDV * h, GDV * h + GDV)
                    mm(ps7[part, f * T:f * T + P], vg[:, 0, v], s_gla[:, 0, h, :], f == 0, False)
                    mm(ps7[part, f * T + P:f * T + T], vg[:, 1, v], s_gla[:, 1, h, :], False, False)
                    ins = mm(ps7[part, f * T + P:f * T + T], vg[:, 0, v], s_cross[:, h, :], False, f == 1)
                ins.then_inc(ps7_full, 1)
                def window_out(heads):
                    for h in heads:
                        f, part = h // 2, slice(SWD * (h % 2), SWD * (h % 2) + SWD)
                        half, j = h // 4, h % 4
                        slot = 4 * (j // 2) + 2 * (j % 2) + half
                        at = (f % 2) * T
                        v = slice(SWD * half, SWD * half + SWD)
                        mm(psm[part, f // 2, at:at + P], vs[:, 0, v], pt[:, 16 + slot, :], f % 2 == 0, False)
                        for t in range(TT):
                            ins = mm(psm[part, f // 2, at + P:at + T], vs[:, t, v], pt[:, 2 * slot + t, :], False,
                                     f % 2 == 1 and t == 1)
                    return ins

                window_out(range(SWH)).then_inc(pv_full, 1)
                pe.wait_ge(og_sq, l + 1)
                pe.wait_ge(ps7_free, ps70 + PS7_GBC)
                for t in range(TT):
                    for f in range(2):
                        at = 4 * t + 2 * f
                        ins = mm(ps7[:, at:at + 2], cols(sq2[:, f, :], t), headsel, at == 0, at == 6)
                ins.then_inc(stat_full, 1)

                pe.wait_ge(yc_sq, l + 1)
                for t in range(TT):
                    for f in range(2):
                        ins = mm(cbank[:, t:t + 1], cols(th2[:, f, :], t), means[:, 1:2], t + f == 0, t + f == 2)
                ins.then_inc(stat_full, 1)
                keep_warm(11)
                pe.wait_ge(rstd8_ready, l + 2)
                for f in range(2):
                    for t in range(TT):
                        for h in range(2):
                            at, part = 4 * t + 2 * f + h, slice(GDV * h, GDV * h + GDV)
                            ins = mm(cols(ps7[part, :], TT * f + t), rstd8[:, at:at + 1].broadcast_to([P, GDV]), ident,
                                     f + t == 0, f + t == 2)
                ins.then_inc(ps7_full, 1)
                pe.wait_ge(conv_rstd, l + 1)
                for t in range(TT):
                    ins = mm(cols(cbank, TT + t), rstd2[:, t:t + 1].broadcast_to([P, P]), ident, t == 0, t == 1)
                ins.then_inc(conv_full, 1)
                def branch_ready(k):
                    pe.wait_ge(op_split, 7 + 3 * l + (1 if k >= 4 else 2 + k // 2))

                two_units(cm + 9, g0 + GL_WOUT, [stream[(BANK_WOUT + n) % 3] for n in range(2)], b_hi, b_lo, branch_ready,
                          order=(4, 5, 6, 7, 0, 1, 2, 3))
                for n in range(2, 4):
                    project(cm + 9 + n, g0 + GL_WOUT + n, stream[(BANK_WOUT + n) % 3], b_hi, b_lo)
                norm(ps70 + PS7_G3)
                ffn(c0 + UL_UP_B, g0 + GL_UP_B, BANK_UP_B, 4 + 3 * l, NF1 + NF2 * (2 * l + 1), ps70 + PS7_G4)
                norm(ps70 + PS7_G5)
            for g in range(4):
                for f in range(FT):
                    k = FT * g + f
                    pe.wait_ge(x_ready, KT * 3 * LAYERS + k + 1)
                    if k == 0:
                        pe.wait_ge(group_evac, G1_END + LAYERS * GL)
                    for t in range(TT):
                        at = t * UC + f * P
                        ins = nc.tensor.transpose(psm[:, g, at:at + P], x[:, k, t * P:t * P + P], ident)
                ins.then_inc(out_turned, 1)


def kernel(**inputs):
    import concourse.bacc as bacc
    from concourse.bass_utils import run_bass_kernel_spmd as run

    def rows(name, *index):
        return np.asarray(inputs[name])[index].reshape(-1, P)

    vec_rows = np.zeros((P, 4, VCOL), np.float32)
    for name, src in (("norm1", "norm1_w"), ("gate_b", "merge_gate_b"), ("gn", "ret_gn_w"), ("lconv_w", "lru_conv_w"),
                      ("lconv_b", "lru_conv_b"), ("b_r", "lru_b_r"), ("b_i", "lru_b_i"), ("lam", "lru_lambda"),
                      ("norm2", "norm2_w"), ("norm_f", "norm_f_w")):
        r = rows(src)
        vec_rows[V1[name]:V1[name] + len(r), 0] = r
    for name, src in (("fconv_w", "ffn_conv_w"), ("fconv_b", "ffn_conv_b")):
        r = rows(src)
        vec_rows[V1B[name]:V1B[name] + len(r), 1] = r
    for l in range(LAYERS):
        for name, src in (("norm", "norm_g_2"), ("conv_w", "conv_w_2"), ("conv_b", "conv_b_2"), ("ln_g", "conv_ln_g_2"),
                          ("ln_b", "conv_ln_b_2"), ("gla_g", "gla_norm_g_2")):
            r = rows(src, l)
            vec_rows[VL[name]:VL[name] + len(r), 2 + l] = r
    gate2 = np.concatenate([np.asarray(inputs["gla_w_gate2_2"]), np.asarray(inputs["gla_b_gate_2"])[:, None]], axis=1)
    sink = np.asarray(inputs["swa_sinks_2"]).reshape(LAYERS, 2, 2, 2).transpose(0, 2, 3, 1).reshape(LAYERS, 1, 8)
    sent = {
        "table": TABLE, "masks": MASKS, "vec_rows": vec_rows.reshape(P, -1),
        "gate2": np.ascontiguousarray(gate2.transpose(1, 0, 2)).reshape(17, -1),
        "sink_row": np.ascontiguousarray(np.concatenate([sink, sink], axis=1)).reshape(1, -1),
    }
    for name in ("x", "positions", "w_in", "w_ret_o", "lru_w_r", "lru_w_i", "w_lru_o", "w_out", "ffn_w_up", "ffn_w_down",
                 "ffn_w_gate_2", "ffn_w_up_2", "ffn_w_down_2", "w_in_2", "w_out_2"):
        sent[name] = np.ascontiguousarray(inputs[name])
    nc = bacc.Bacc("TRN2", target_bir_lowering=False, num_devices=1)
    io = {name: nc.dram_tensor(f"in_{name}", a.shape, mybir.dt.from_np(a.dtype), kind="ExternalInput").ap()
          for name, a in sent.items()}
    out = nc.dram_tensor("out", (1, T, D), F32, kind="ExternalOutput").ap()
    build(nc, io, out)
    result = run(nc, [{f"in_{name}": a for name, a in sent.items()}], core_ids=[0])
    return result.results[0]["out"]
```
